# Optimizing a Trainium2 kernel written in Bass

```python
import jax, jax.numpy as jnp
from jax import lax
import numpy as np

D_MODEL = 1024
BATCH = 1
SEQ = 512
DEPTH = 1

LRU_WIDTH = 1024
LRU_BLOCKS = 16
LRU_BLOCK_W = LRU_WIDTH // LRU_BLOCKS
CONV_WIDTH = 4
LRU_C = 8.0
HEAD_DIM = 64
N_Q_HEADS = 16
N_KV_HEADS = 4
Q_PER_KV = N_Q_HEADS // N_KV_HEADS
ATTN_WIDTH = N_Q_HEADS * HEAD_DIM
KV_WIDTH = N_KV_HEADS * HEAD_DIM
WINDOW = 128
BLOCK = 128
ROPE_THETA = 10000.0
D_FF = 2816
MACARON_SCALE = 0.5
NORM_EPS = 1e-6
MASK_VALUE = -1e30
IN_WIDTH = 2 * LRU_WIDTH + ATTN_WIDTH + 2 * KV_WIDTH + 2 * D_MODEL
IN_SPLITS = (
    LRU_WIDTH,
    2 * LRU_WIDTH,
    2 * LRU_WIDTH + ATTN_WIDTH,
    2 * LRU_WIDTH + ATTN_WIDTH + KV_WIDTH,
    2 * LRU_WIDTH + ATTN_WIDTH + 2 * KV_WIDTH,
    2 * LRU_WIDTH + ATTN_WIDTH + 2 * KV_WIDTH + D_MODEL,
)


def rms_norm(x, g):
    xf = x.astype(jnp.float32)
    y = xf * lax.rsqrt(jnp.mean(xf * xf, axis=-1, keepdims=True) + NORM_EPS)
    return (y * g.astype(jnp.float32)).astype(x.dtype)

def swiglu(x, w_gu, w_down):
    g, u = jnp.split(x @ w_gu, 2, axis=-1)
    return (jax.nn.silu(g) * u) @ w_down

def rope_tables(seq_len):
    half = HEAD_DIM // 2
    inv_freq = ROPE_THETA ** (-jnp.arange(half, dtype=jnp.float32) / half)
    ang = jnp.arange(seq_len, dtype=jnp.float32)[:, None] * inv_freq[None, :]
    return jnp.cos(ang), jnp.sin(ang)

def apply_rope(x, cos, sin):
    half = HEAD_DIM // 2
    xf = x.astype(jnp.float32)
    x1, x2 = xf[..., :half], xf[..., half:]
    c = cos[None, :, None, :]
    s = sin[None, :, None, :]
    return jnp.concatenate([x1 * c - x2 * s, x2 * c + x1 * s], axis=-1).astype(x.dtype)

def causal_depthwise_conv(x, w, b):
    s = x.shape[1]
    xp = jnp.pad(x, ((0, 0), (CONV_WIDTH - 1, 0), (0, 0)))
    y = xp[:, 0:s] * w[0]
    for k in range(1, CONV_WIDTH):
        y = y + xp[:, k:k + s] * w[k]
    return y + b

def block_diag_linear(x, w, b):
    bsz, s, _ = x.shape
    xb = x.reshape(bsz, s, LRU_BLOCKS, LRU_BLOCK_W)
    y = jnp.einsum('bsnc,ncd->bsnd', xb, w).reshape(bsz, s, LRU_WIDTH)
    return y + b

def rg_lru(x, w_a, b_a, w_x, b_x, lam):
    xf = x.astype(jnp.float32)
    r = jax.nn.sigmoid(block_diag_linear(x, w_a, b_a).astype(jnp.float32))
    i = jax.nn.sigmoid(block_diag_linear(x, w_x, b_x).astype(jnp.float32))
    log_a = -LRU_C * r * jax.nn.softplus(-lam.astype(jnp.float32))
    a = jnp.exp(log_a)
    mult = jnp.sqrt(jnp.maximum(-jnp.expm1(2.0 * log_a), 0.0))
    bterm = mult * (i * xf)

    def combine(left, right):
        a1, b1 = left
        a2, b2 = right
        return a1 * a2, a2 * b1 + b2

    _, h = lax.associative_scan(combine, (a, bterm), axis=1)
    return h.astype(x.dtype)

def band_blocks(t):
    bsz, s, h, d = t.shape
    tb = t.reshape(bsz, s // BLOCK, BLOCK, h, d)
    prev = jnp.pad(tb, ((0, 0), (1, 0), (0, 0), (0, 0), (0, 0)))[:, :-1]
    return jnp.concatenate([prev, tb], axis=2)

def sliding_window_attention_with_sinks(q, k, v, sinks):
    bsz, s = q.shape[0], q.shape[1]
    nb = s // BLOCK
    qb = q.reshape(bsz, nb, BLOCK, N_KV_HEADS, Q_PER_KV, HEAD_DIM)
    kb = band_blocks(k)
    vb = band_blocks(v)
    scores = jnp.einsum('bnqhgd,bnshd->bhgnqs', qb, kb).astype(jnp.float32) * (HEAD_DIM ** -0.5)
    qi = jnp.arange(BLOCK)[:, None]
    si = jnp.arange(2 * BLOCK)[None, :]
    diff = BLOCK + qi - si
    key_pos = (jnp.arange(nb)[:, None, None] - 1) * BLOCK + si[None]
    mask = ((diff >= 0) & (diff < WINDOW))[None] & (key_pos >= 0)
    scores = jnp.where(mask, scores, MASK_VALUE)
    sink = sinks.astype(jnp.float32).reshape(1, N_KV_HEADS, Q_PER_KV, 1, 1, 1)
    sink = jnp.broadcast_to(sink, scores.shape[:-1] + (1,))
    probs = jax.nn.softmax(jnp.concatenate([scores, sink], axis=-1), axis=-1)[..., :-1]
    out = jnp.einsum('bhgnqs,bnshd->bnqhgd', probs.astype(v.dtype), vb)
    return out.reshape(bsz, s, ATTN_WIDTH)

def hybrid_mixer(u, cos, sin, w_in, conv_w, conv_b, lru_w_a, lru_b_a, lru_w_x, lru_b_x,
                 lru_lambda, attn_sinks, w_proj_lru, w_proj_attn, w_out):
    bsz, s, _ = u.shape
    z = u @ w_in
    gate_br, x_br, q, k, v, g_lru, g_attn = jnp.split(z, IN_SPLITS, axis=-1)
    xc = causal_depthwise_conv(x_br, conv_w, conv_b)
    y_lru = rg_lru(xc, lru_w_a, lru_b_a, lru_w_x, lru_b_x, lru_lambda) * jax.nn.gelu(gate_br)
    q = apply_rope(q.reshape(bsz, s, N_Q_HEADS, HEAD_DIM), cos, sin)
    k = apply_rope(k.reshape(bsz, s, N_KV_HEADS, HEAD_DIM), cos, sin)
    v = v.reshape(bsz, s, N_KV_HEADS, HEAD_DIM)
    y_attn = sliding_window_attention_with_sinks(q, k, v, attn_sinks)
    merged = jax.nn.sigmoid(g_lru) * (y_lru @ w_proj_lru) + jax.nn.sigmoid(g_attn) * (y_attn @ w_proj_attn)
    return merged @ w_out

def first_inputs(seed: int = 0) -> dict:
    key = jax.random.key(seed)
    ks = jax.random.split(key, 24)

    def nrm(k, shape, scale):
        return jax.random.normal(k, shape, jnp.float32) * scale

    def gain(k, shape):
        return 1.0 + 0.05 * jax.random.normal(k, shape, jnp.float32)

    u = jax.random.uniform(ks[13], (DEPTH, LRU_WIDTH), jnp.float32, minval=0.9, maxval=0.999)
    a0 = u ** (1.0 / LRU_C)
    lam = jnp.log(a0) - jnp.log1p(-a0)
    return {
        "x": nrm(ks[0], (BATCH, SEQ, D_MODEL), 1.0),
        "ffn1_pre_g": gain(ks[1], (DEPTH, D_MODEL)),
        "ffn1_w_gu": nrm(ks[2], (DEPTH, D_MODEL, 2 * D_FF), D_MODEL ** -0.5),
        "ffn1_w_down": nrm(ks[3], (DEPTH, D_FF, D_MODEL), D_FF ** -0.5),
        "ffn1_post_g": gain(ks[4], (DEPTH, D_MODEL)),
        "mix_pre_g": gain(ks[5], (DEPTH, D_MODEL)),
        "w_in": nrm(ks[6], (DEPTH, D_MODEL, IN_WIDTH), D_MODEL ** -0.5),
        "conv_w": nrm(ks[7], (DEPTH, CONV_WIDTH, LRU_WIDTH), CONV_WIDTH ** -0.5),
        "conv_b": nrm(ks[8], (DEPTH, LRU_WIDTH), 0.01),
        "lru_w_a": nrm(ks[9], (DEPTH, LRU_BLOCKS, LRU_BLOCK_W, LRU_BLOCK_W), LRU_BLOCK_W ** -0.5),
        "lru_b_a": nrm(ks[10], (DEPTH, LRU_WIDTH), 0.01),
        "lru_w_x": nrm(ks[11], (DEPTH, LRU_BLOCKS, LRU_BLOCK_W, LRU_BLOCK_W), LRU_BLOCK_W ** -0.5),
        "lru_b_x": nrm(ks[12], (DEPTH, LRU_WIDTH), 0.01),
        "lru_lambda": lam,
        "attn_sinks": nrm(ks[14], (DEPTH, N_Q_HEADS), 0.5),
        "w_proj_lru": nrm(ks[15], (DEPTH, LRU_WIDTH, D_MODEL), LRU_WIDTH ** -0.5),
        "w_proj_attn": nrm(ks[16], (DEPTH, ATTN_WIDTH, D_MODEL), ATTN_WIDTH ** -0.5),
        "w_out": nrm(ks[17], (DEPTH, D_MODEL, D_MODEL), D_MODEL ** -0.5),
        "mix_post_g": gain(ks[18], (DEPTH, D_MODEL)),
        "ffn2_pre_g": gain(ks[19], (DEPTH, D_MODEL)),
        "ffn2_w_gu": nrm(ks[20], (DEPTH, D_MODEL, 2 * D_FF), D_MODEL ** -0.5),
        "ffn2_w_down": nrm(ks[21], (DEPTH, D_FF, D_MODEL), D_FF ** -0.5),
        "ffn2_post_g": gain(ks[22], (DEPTH, D_MODEL)),
    }

def first_block(x, ffn1_pre_g, ffn1_w_gu, ffn1_w_down, ffn1_post_g,
              mix_pre_g, w_in, conv_w, conv_b, lru_w_a, lru_b_a, lru_w_x, lru_b_x,
              lru_lambda, attn_sinks, w_proj_lru, w_proj_attn, w_out, mix_post_g,
              ffn2_pre_g, ffn2_w_gu, ffn2_w_down, ffn2_post_g):
    cos, sin = rope_tables(x.shape[1])
    h = x
    for l in range(DEPTH):
        f = swiglu(rms_norm(h, ffn1_pre_g[l]), ffn1_w_gu[l], ffn1_w_down[l])
        h = h + MACARON_SCALE * rms_norm(f, ffn1_post_g[l])
        m = hybrid_mixer(rms_norm(h, mix_pre_g[l]), cos, sin, w_in[l], conv_w[l], conv_b[l],
                         lru_w_a[l], lru_b_a[l], lru_w_x[l], lru_b_x[l], lru_lambda[l],
                         attn_sinks[l], w_proj_lru[l], w_proj_attn[l], w_out[l])
        h = h + rms_norm(m, mix_post_g[l])
        f = swiglu(rms_norm(h, ffn2_pre_g[l]), ffn2_w_gu[l], ffn2_w_down[l])
        h = h + MACARON_SCALE * rms_norm(f, ffn2_post_g[l])
    return h


DEPTH_2 = 2

GRID_W = 64
CTX_LEN = 256
N_EVEN = (DEPTH_2 + 1) // 2
N_ODD = DEPTH_2 // 2
EPS = 1e-6

FOURIER_GROUPS = 4
FOURIER_GROUP_DIM = 128
FOURIER_WIDTH = FOURIER_GROUPS * FOURIER_GROUP_DIM
CONV_GROUPS = 4
CONV_WIDTH_2 = 512
CONV_K = 3
EVEN_IN = FOURIER_WIDTH + 3 * CONV_WIDTH_2
EVEN_OUT = FOURIER_WIDTH + CONV_WIDTH_2

N_HEADS = 16
GQA_GROUP = N_HEADS // N_KV_HEADS
Q_DIM = N_HEADS * HEAD_DIM
KV_DIM = N_KV_HEADS * HEAD_DIM
QKV_OUT = Q_DIM + 2 * KV_DIM
ATT_BLOCK = 128
ROPE_BASE = 10000.0
ROPE_PAIRS_PER_AXIS = HEAD_DIM // 4
NEG_INF = -1e30

N_GROUPS = 4
EXPERTS_PER_GROUP = 8
N_EXPERTS = N_GROUPS * EXPERTS_PER_GROUP
TOP_K = 2
D_FF_EXPERT = 512
MOE_BLOCK = 128


def rms_norm_2(x, g):
    xf = x.astype(jnp.float32)
    y = xf * lax.rsqrt(jnp.mean(xf * xf, axis=-1, keepdims=True) + EPS)
    return (y * g.astype(jnp.float32)).astype(x.dtype)

def modulate(h, shift, scale):
    return h * (1 + scale) + shift

def fourier_mix(a):
    b_, l_, _ = a.shape
    a4 = a.reshape(b_, l_, FOURIER_GROUPS, FOURIER_GROUP_DIM).astype(jnp.float32)
    f = jnp.fft.fftn(a4, axes=(1, 3), norm="ortho").real
    return f.reshape(b_, l_, FOURIER_WIDTH).astype(a.dtype)

def short_conv_mix(b_gate, c_gate, h, w):
    u = c_gate * h
    up = jnp.pad(u, ((0, 0), (1, 1), (0, 0)))
    y = w[0] * up[:, :-2] + w[1] * up[:, 1:-1] + w[2] * up[:, 2:]
    return b_gate * y

def even_mixer(h, w_in, conv_w, w_out):
    p = h @ w_in
    a, b_gate, c_gate, hv = jnp.split(
        p, [FOURIER_WIDTH, FOURIER_WIDTH + CONV_WIDTH_2, FOURIER_WIDTH + 2 * CONV_WIDTH_2], axis=-1)
    y = jnp.concatenate([fourier_mix(a), short_conv_mix(b_gate, c_gate, hv, conv_w)], axis=-1)
    return y @ w_out

def axial_rope_tables(n_tok):
    t = jnp.arange(n_tok, dtype=jnp.int32)
    pos = jnp.stack([t // GRID_W, t % GRID_W], axis=-1).astype(jnp.float32)
    freqs = ROPE_BASE ** (-jnp.arange(ROPE_PAIRS_PER_AXIS, dtype=jnp.float32) / ROPE_PAIRS_PER_AXIS)
    ang = pos[:, :, None] * freqs
    return jnp.cos(ang), jnp.sin(ang)

def apply_axial_rope(x, cos, sin):
    b_, l_, h_, _ = x.shape
    xf = x.astype(jnp.float32).reshape(b_, l_, h_, 2, 2, ROPE_PAIRS_PER_AXIS)
    x1, x2 = xf[..., 0, :], xf[..., 1, :]
    cs, sn = cos[None, :, None], sin[None, :, None]
    out = jnp.stack([x1 * cs - x2 * sn, x1 * sn + x2 * cs], axis=-2)
    return out.reshape(x.shape).astype(x.dtype)

def project_q(h, w_qkv, q_g):
    b_, l_, _ = h.shape
    q = (h @ w_qkv[:, :Q_DIM]).reshape(b_, l_, N_HEADS, HEAD_DIM)
    return rms_norm_2(q, q_g)

def project_kv(h, w_qkv, k_g):
    b_, l_, _ = h.shape
    kv = h @ w_qkv[:, Q_DIM:]
    k = rms_norm_2(kv[..., :KV_DIM].reshape(b_, l_, N_KV_HEADS, HEAD_DIM), k_g)
    v = kv[..., KV_DIM:].reshape(b_, l_, N_KV_HEADS, HEAD_DIM)
    return k, v

def window_attention(hl, hc, w_qkv, q_g, k_g, sink, w_o, need_ctx_out):
    B, L, _ = hl.shape
    Lc = hc.shape[1]
    scale = HEAD_DIM ** -0.5
    cos, sin = axial_rope_tables(L)
    ql = apply_axial_rope(project_q(hl, w_qkv, q_g), cos, sin) * scale
    kl, vl = project_kv(hl, w_qkv, k_g)
    kl = apply_axial_rope(kl, cos, sin)
    kc, vc = project_kv(hc, w_qkv, k_g)
    sink_g = sink.reshape(N_KV_HEADS, GQA_GROUP).astype(jnp.float32)

    n_blocks = L // ATT_BLOCK
    qg = ql.reshape(B, L, N_KV_HEADS, GQA_GROUP, HEAD_DIM)
    pad = ((0, 0), (ATT_BLOCK, ATT_BLOCK), (0, 0), (0, 0))
    kp, vp = jnp.pad(kl, pad), jnp.pad(vl, pad)
    qi = jnp.arange(ATT_BLOCK)
    kj = jnp.arange(3 * ATT_BLOCK)
    band = jnp.abs(kj[None, :] - ATT_BLOCK - qi[:, None]) <= WINDOW

    def block(bidx):
        start = bidx * ATT_BLOCK
        qb = lax.dynamic_slice_in_dim(qg, start, ATT_BLOCK, axis=1)
        kb = lax.dynamic_slice_in_dim(kp, start, 3 * ATT_BLOCK, axis=1)
        vb = lax.dynamic_slice_in_dim(vp, start, 3 * ATT_BLOCK, axis=1)
        kpos = start - ATT_BLOCK + kj
        mask = band & ((kpos >= 0) & (kpos < L))[None, :]
        s_loc = jnp.einsum("bqkgd,bskd->bkgqs", qb, kb, preferred_element_type=jnp.float32)
        s_loc = jnp.where(mask, s_loc, NEG_INF)
        s_ctx = jnp.einsum("bqkgd,bskd->bkgqs", qb, kc, preferred_element_type=jnp.float32)
        s_sink = jnp.broadcast_to(sink_g[None, :, :, None, None], s_loc.shape[:-1] + (1,))
        p = jax.nn.softmax(jnp.concatenate([s_loc, s_ctx, s_sink], axis=-1), axis=-1)
        p_loc = p[..., :3 * ATT_BLOCK].astype(vb.dtype)
        p_ctx = p[..., 3 * ATT_BLOCK:3 * ATT_BLOCK + Lc].astype(vc.dtype)
        return (jnp.einsum("bkgqs,bskd->bqkgd", p_loc, vb)
                + jnp.einsum("bkgqs,bskd->bqkgd", p_ctx, vc))

    ob = lax.map(block, jnp.arange(n_blocks))
    yl = jnp.moveaxis(ob, 0, 1).reshape(B, L, Q_DIM) @ w_o

    if not need_ctx_out:
        return yl, None
    qc = project_q(hc, w_qkv, q_g).reshape(B, Lc, N_KV_HEADS, GQA_GROUP, HEAD_DIM) * scale
    s = jnp.einsum("bqkgd,bskd->bkgqs", qc, kc, preferred_element_type=jnp.float32)
    s_sink = jnp.broadcast_to(sink_g[None, :, :, None, None], s.shape[:-1] + (1,))
    p = jax.nn.softmax(jnp.concatenate([s, s_sink], axis=-1), axis=-1)[..., :Lc].astype(vc.dtype)
    yc = jnp.einsum("bkgqs,bskd->bqkgd", p, vc).reshape(B, Lc, Q_DIM) @ w_o
    return yl, yc

def hier_moe(xf, w_rg, b_rg, w_re, b_re, w1, w3, w2):
    T, D = xf.shape
    xr = xf.astype(jnp.float32)
    g_logits = xr @ w_rg.astype(jnp.float32) + b_rg.astype(jnp.float32)
    g_prob = jax.nn.softmax(g_logits, axis=-1)
    g_val, g_idx = lax.top_k(g_prob, 1)
    e_logits = (xr @ w_re.astype(jnp.float32) + b_re.astype(jnp.float32)).reshape(
        T, N_GROUPS, EXPERTS_PER_GROUP)
    e_in = jnp.take_along_axis(e_logits, g_idx[:, :, None], axis=1)[:, 0]
    top_v, top_i = lax.top_k(e_in, TOP_K)
    gate = jax.nn.softmax(top_v, axis=-1) * g_val
    expert = g_idx * EXPERTS_PER_GROUP + top_i

    A = T * TOP_K
    e_flat = expert.reshape(A)
    t_flat = jnp.repeat(jnp.arange(T, dtype=jnp.int32), TOP_K)
    g_flat = gate.reshape(A)
    counts = jnp.bincount(e_flat, length=N_EXPERTS)
    padded = (counts + MOE_BLOCK - 1) // MOE_BLOCK * MOE_BLOCK
    pad_end = jnp.cumsum(padded)
    pad_start = pad_end - padded
    raw_start = jnp.cumsum(counts) - counts
    order = jnp.argsort(e_flat)
    e_s = e_flat[order]
    dest = pad_start[e_s] + jnp.arange(A) - raw_start[e_s]
    n_blocks = -(-A // MOE_BLOCK) + N_EXPERTS
    R = n_blocks * MOE_BLOCK
    row_tok = jnp.full((R,), T, jnp.int32).at[dest].set(t_flat[order])
    row_gate = jnp.zeros((R,), jnp.float32).at[dest].set(g_flat[order])
    block_exp = jnp.clip(jnp.searchsorted(pad_end, jnp.arange(n_blocks) * MOE_BLOCK, side="right"),
                         0, N_EXPERTS - 1)

    x_pad = jnp.concatenate([xf, jnp.zeros((1, D), xf.dtype)], axis=0)
    xb = x_pad[row_tok].reshape(n_blocks, MOE_BLOCK, D)

    def expert_block(args):
        xblk, e = args
        return (jax.nn.silu(xblk @ w1[e]) * (xblk @ w3[e])) @ w2[e]

    yb = lax.map(expert_block, (xb, block_exp)).reshape(R, D)
    out = jnp.zeros((T + 1, D), yb.dtype).at[row_tok].add(yb * row_gate[:, None].astype(yb.dtype))
    return out[:T]

def second_inputs(seed: int = 0) -> dict:
    key = jax.random.key(seed)
    ks = jax.random.split(key, 24)
    D = D_MODEL

    def nrm(k, shape, s):
        return jax.random.normal(k, shape, jnp.float32) * s

    return {
        "x": nrm(ks[0], (BATCH, SEQ, D), 1.0),
        "c": nrm(ks[1], (BATCH, D), 1.0),
        "ctx": nrm(ks[2], (BATCH, CTX_LEN, D), 1.0),
        "c_ctx": nrm(ks[3], (D,), 1.0),
        "w_mod": nrm(ks[4], (DEPTH_2, D, 6 * D), 0.5 * D ** -0.5),
        "b_mod": nrm(ks[5], (DEPTH_2, 6 * D), 0.01),
        "norm_mix_g": 1.0 + nrm(ks[6], (DEPTH_2, D), 0.02),
        "norm_ffn_g": 1.0 + nrm(ks[7], (DEPTH_2, D), 0.02),
        "w_in_even": nrm(ks[8], (N_EVEN, D, EVEN_IN), D ** -0.5),
        "conv_w": nrm(ks[9], (N_EVEN, CONV_K, CONV_WIDTH_2), CONV_K ** -0.5),
        "w_out_even": nrm(ks[10], (N_EVEN, EVEN_OUT, D), EVEN_OUT ** -0.5),
        "w_qkv": nrm(ks[11], (N_ODD, D, QKV_OUT), D ** -0.5),
        "q_norm_g": 1.0 + nrm(ks[12], (N_ODD, HEAD_DIM), 0.02),
        "k_norm_g": 1.0 + nrm(ks[13], (N_ODD, HEAD_DIM), 0.02),
        "sink_logit": nrm(ks[14], (N_ODD, N_HEADS), 1.0),
        "w_o": nrm(ks[15], (N_ODD, Q_DIM, D), Q_DIM ** -0.5),
        "w_router_g": nrm(ks[16], (DEPTH_2, D, N_GROUPS), D ** -0.5),
        "b_router_g": nrm(ks[17], (DEPTH_2, N_GROUPS), 0.01),
        "w_router_e": nrm(ks[18], (DEPTH_2, D, N_EXPERTS), D ** -0.5),
        "b_router_e": nrm(ks[19], (DEPTH_2, N_EXPERTS), 0.01),
        "w1": nrm(ks[20], (DEPTH_2, N_EXPERTS, D, D_FF_EXPERT), D ** -0.5),
        "w3": nrm(ks[21], (DEPTH_2, N_EXPERTS, D, D_FF_EXPERT), D ** -0.5),
        "w2": nrm(ks[22], (DEPTH_2, N_EXPERTS, D_FF_EXPERT, D), D_FF_EXPERT ** -0.5),
    }

def second_block(x, c, ctx, c_ctx, w_mod, b_mod, norm_mix_g, norm_ffn_g, w_in_even, conv_w, w_out_even,
              w_qkv, q_norm_g, k_norm_g, sink_logit, w_o, w_router_g, b_router_g, w_router_e, b_router_e,
              w1, w3, w2):
    B, L, D = x.shape
    Lc = ctx.shape[1]
    xl, xc = x, ctx
    for layer in range(DEPTH_2):
        last = layer == DEPTH_2 - 1
        is_even = layer % 2 == 0
        j = layer // 2
        mod_l = (jax.nn.silu(c) @ w_mod[layer] + b_mod[layer])[:, None, :]
        mod_c = jax.nn.silu(c_ctx) @ w_mod[layer] + b_mod[layer]
        sh1_l, sc1_l, g1_l, sh2_l, sc2_l, g2_l = jnp.split(mod_l, 6, axis=-1)
        sh1_c, sc1_c, g1_c, sh2_c, sc2_c, g2_c = jnp.split(mod_c, 6, axis=-1)

        hl = modulate(rms_norm_2(xl, norm_mix_g[layer]), sh1_l, sc1_l)
        if is_even:
            yl = even_mixer(hl, w_in_even[j], conv_w[j], w_out_even[j])
            yc = None
            if not last:
                hc = modulate(rms_norm_2(xc, norm_mix_g[layer]), sh1_c, sc1_c)
                yc = even_mixer(hc, w_in_even[j], conv_w[j], w_out_even[j])
        else:
            hc = modulate(rms_norm_2(xc, norm_mix_g[layer]), sh1_c, sc1_c)
            yl, yc = window_attention(hl, hc, w_qkv[j], q_norm_g[j], k_norm_g[j], sink_logit[j], w_o[j],
                                      not last)
        xl = xl + g1_l * yl

        hl2 = modulate(rms_norm_2(xl, norm_ffn_g[layer]), sh2_l, sc2_l).reshape(B * L, D)
        moe_args = (w_router_g[layer], b_router_g[layer], w_router_e[layer], b_router_e[layer],
                    w1[layer], w3[layer], w2[layer])
        if last:
            xl = xl + g2_l * hier_moe(hl2, *moe_args).reshape(B, L, D)
        else:
            xc = xc + g1_c * yc
            hc2 = modulate(rms_norm_2(xc, norm_ffn_g[layer]), sh2_c, sc2_c).reshape(B * Lc, D)
            f = hier_moe(jnp.concatenate([hl2, hc2], axis=0), *moe_args)
            xl = xl + g2_l * f[:B * L].reshape(B, L, D)
            xc = xc + g2_c * f[B * L:].reshape(B, Lc, D)
    return xl


def setup_inputs(seed=0):
    out = dict(first_inputs(seed))
    for name, value in second_inputs(seed + 1).items():
        if name != "x":
            out[name + "_2"] = value
    return out


def reference(
    x, ffn1_pre_g, ffn1_w_gu, ffn1_w_down, ffn1_post_g, mix_pre_g, w_in, conv_w, conv_b,
    lru_w_a, lru_b_a, lru_w_x, lru_b_x, lru_lambda, attn_sinks, w_proj_lru, w_proj_attn, w_out,
    mix_post_g, ffn2_pre_g, ffn2_w_gu, ffn2_w_down, ffn2_post_g, c_2, ctx_2, c_ctx_2, w_mod_2,
    b_mod_2, norm_mix_g_2, norm_ffn_g_2, w_in_even_2, conv_w_2, w_out_even_2, w_qkv_2,
    q_norm_g_2, k_norm_g_2, sink_logit_2, w_o_2, w_router_g_2, b_router_g_2, w_router_e_2,
    b_router_e_2, w1_2, w3_2, w2_2,
):
    x = first_block(
        x, ffn1_pre_g, ffn1_w_gu, ffn1_w_down, ffn1_post_g, mix_pre_g, w_in, conv_w, conv_b,
        lru_w_a, lru_b_a, lru_w_x, lru_b_x, lru_lambda, attn_sinks, w_proj_lru, w_proj_attn,
        w_out, mix_post_g, ffn2_pre_g, ffn2_w_gu, ffn2_w_down, ffn2_post_g,
    )
    return second_block(
        x, c_2, ctx_2, c_ctx_2, w_mod_2, b_mod_2, norm_mix_g_2, norm_ffn_g_2, w_in_even_2,
        conv_w_2, w_out_even_2, w_qkv_2, q_norm_g_2, k_norm_g_2, sink_logit_2, w_o_2,
        w_router_g_2, b_router_g_2, w_router_e_2, b_router_e_2, w1_2, w3_2, w2_2,
    )


_drawn_inputs = setup_inputs


def setup_inputs(seed=0):
    import zlib

    import numpy as np

    out = dict(_drawn_inputs(seed))
    spreads = {}
    factors = {'lru_b_a': 8.0,
     'lru_b_x': 8.0,
     'attn_sinks': 4.373,
     'ffn2_post_g': 2.977,
     'ctx_2': 4.66,
     'b_mod_2': 4.467,
     'norm_mix_g_2': 6.726,
     'norm_ffn_g_2': 35.295,
     'q_norm_g_2': 64.0,
     'k_norm_g_2': 64.0,
     'sink_logit_2': 8.0,
     'b_router_g_2': 64.0,
     'b_router_e_2': 64.0}
    for name, (base, spread) in spreads.items():
        noise = np.random.default_rng([zlib.crc32(name.encode()), seed]).standard_normal(out[name].shape)
        drawn = base * np.exp(spread * noise) if base else spread * noise
        out[name] = __import__('jax').numpy.asarray(drawn.astype(out[name].dtype))
    for name, factor in factors.items():
        out[name] = (out[name] * factor).astype(out[name].dtype)
    return out
```

```python
from contextlib import ExitStack

import numpy as np

import concourse.bass as bass
from concourse import mybir

F32 = mybir.dt.float32
I32 = mybir.dt.int32
U32 = mybir.dt.uint32
ACT = mybir.ActivationFunctionType
ALU = mybir.AluOpType
AX = mybir.AxisListType

P = 128
D = 1024
KT = D // P
S = 512
C = 256
SC = S + C
FF = 2816
FT = FF // P
HD = 64
NH = 16
PAIRS = NH // 2
EPS = 1e-6
NE = 32
NG = 4
EF = 512
MB = 128
NBMAX = -(-2 * SC // MB) + NE
TABW = NBMAX + 1
CONV1 = 4
LRU_C = 8.0
SLOT = FT * P
CHUNK = 2 * KT * P
ROUTE = NG + NE
TT = SC // P
LT = S // P
ZERO = 512
XPAD = S + CONV1 - 1
SCALE = HD ** -0.5
NEG = -1e30

HEADS = [8 * (j // 4) + j % 4 + 4 * s for j in range(PAIRS) for s in range(2)]

DENSE = [("mod", 48, 24), ("gu1", 22, 11), ("down1", 8, 2), ("xbr", 4, 2), ("q1", 4, 2), ("kv1", 2, 1),
         ("gate", 4, 2), ("merge", 16, 8), ("out1", 4, 2), ("gu2", 22, 11), ("down2", 8, 2),
         ("even_in", 8, 8), ("even_out", 4, 4), ("q2", 4, 2), ("kv2", 2, 2), ("wo", 4, 2)]


def dense_plan():
    rounds, loads, plan, at = 1, 0, {}, {"w": 0, "d": 0}
    for name, chunks, n in DENSE:
        kind = "d" if name.startswith("down") else "w"
        plan[name] = (rounds, loads, at[kind])
        rounds, loads = rounds + n, loads + chunks // 2
        at[kind] += chunks
    return plan


VECS = [("ffn1_pre_g", 8), ("ffn1_post_g", 8), ("mix_pre_g", 8), ("mix_post_g", 8), ("ffn2_pre_g", 8),
        ("ffn2_post_g", 8), ("conv_w", 32), ("conv_b", 8), ("lru_b_a", 8), ("lru_b_x", 8), ("lru_lambda", 8),
        ("norm_mix", 16), ("norm_ffn", 16), ("conv_w2", 12), ("q_g", 1), ("k_g", 1), ("cond", 16), ("b_mod", 192),
        ("sinks1", 16), ("sinks2", 16), ("route_b", 2 * TT * ROUTE)]
CONSTS = [("ident", 128), ("ones", 128), ("swap1", 128), ("swap2", 128), ("headsum", 128), ("before", 128),
          ("mask1", 256), ("mask2", 384), ("cos1", S), ("sin1", S), ("cos2", S), ("sin2", S),
          ("eps", 1), ("gdesc", NG), ("edesc", NE), ("tri_lt", NE), ("tri_le", NE), ("blocks", TABW), ("thr", 16)]
DFT = [("cs_d", 2 * P), ("c_ctx", 2 * C), ("s_ctx", 2 * C), ("c_lat", 4 * S), ("s_lat", 4 * S)]


def offsets(fields):
    at, out = 0, {}
    for name, n in fields:
        out[name] = (at, n)
        at += n
    return out, at


VEC_AT, VEC_N = offsets(VECS)
CONST_AT, CONST_N = offsets(CONSTS)
DFT_AT, DFT_N = offsets(DFT)


def program(nc, d):
    ctx = ExitStack()
    with ctx:
        def sb(name, shape, dt=F32):
            return ctx.enter_context(nc.sbuf_tensor(name, shape, dt))

        def sem(name):
            return ctx.enter_context(nc.semaphore(name))

        plan = dense_plan()

        lat = sb("lat", [P, KT, S])
        cxt = sb("cxt", [P, KT, C])
        vecs = sb("vecs", [P, VEC_N])
        consts = sb("consts", [P, CONST_N])
        mod = sb("mod", [P, 2, 6, KT, 2])
        amod = sb("amod", [P, 2, 2, 2, KT])
        slot = [sb(f"slot{s}", [P, SLOT]) for s in range(2)]
        half_g = sb("half_g", [P, 2, KT])
        lam8 = sb("lam8", [P, 8, KT])
        silu_c = sb("silu_c", [P, KT, 2])
        small = sb("small", [P, 64])

        ar_u = sb("ar_u", [P, KT * SC])
        ar_f = sb("ar_f", [P, KT * S])
        rs = sb("rs", [P, SC])
        tmp = sb("tmp", [P, 4, S])
        BIG = 22560
        big = sb("big", [P, BIG])

        def vec(name):
            a, n = VEC_AT[name]
            return vecs[:, a:a + n]

        def const(name):
            a, n = CONST_AT[name]
            return consts[:, a:a + n]

        def part(at, shape):
            n = int(np.prod(shape))
            assert at + n <= BIG, (at, shape)
            v = big[:, at:at + n]
            names = "abcd"[:len(shape)]
            return v.rearrange(f"p ({' '.join(names)}) -> p {' '.join(names)}",
                               **{c: x for c, x in zip(names, shape)}) if len(shape) > 1 else v

        ident, ones = const("ident"), const("ones")
        u1 = ar_u[:, 0:KT * S].rearrange("p (k t) -> p k t", k=KT)
        u2 = ar_u[:, :].rearrange("p (k t) -> p k t", k=KT)
        f = ar_f[:, :].rearrange("p (k t) -> p k t", k=KT)
        act_t = part(0, [FT, S])
        xbr = part(0, [KT, XPAD])
        xc = part(KT * XPAD, [KT, S])
        o = KT * (XPAD + S)
        gr = part(o, [KT, S])
        gi = part(o + KT * S, [KT, S])
        qt1 = part(o + 2 * KT * S, [KT, S])
        kt1 = part(o + 3 * KT * S, [2, S])
        v1 = part(o + 3 * KT * S + 2 * S, [LT, C])
        lru_w = ar_u[:, KT * S:KT * S + 2 * KT * P].rearrange("p (g k c) -> p g k c", g=2, k=KT)
        merged = gr
        qt2 = part(0, [KT, S])
        kt2 = part(KT * S, [2, SC])
        v2 = part(KT * S + 2 * SC, [TT, C])
        att2 = KT * S + 2 * SC + TT * C

        def att_views(at):
            return (part(at, [S]), part(at + S, [2, 2, 640]), part(at + S + 2560, [2, 10 * P]))

        pt = part(0, [16, SC])
        yt = part(16 * SC, [8, SC])
        ac = part(24 * SC, [TT, 2 * P])
        dft = part(24 * SC + TT * 2 * P, [DFT_AT["c_lat"][0]])
        csd = dft[:, 0:2 * P]
        c_ctx = dft[:, 2 * P:2 * P + 2 * C].rearrange("p (l t) -> p l t", l=2)
        s_ctx = dft[:, 2 * P + 2 * C:2 * P + 4 * C].rearrange("p (l t) -> p l t", l=2)
        c_lat = ar_f[:, 0:4 * S].rearrange("p (l t) -> p l t", l=4)
        s_lat = tmp[:, :, :]
        wslot = [part(2048 * c, [2048]) for c in range(6)]
        m0 = 6 * 2048
        xg = part(m0, [D])
        xT = part(m0 + D, [KT, MB])
        hsil = part(m0 + 2 * D, [EF])
        hmul = part(m0 + 2 * D + EF, [EF])
        hT = part(m0 + 3 * D, [EF // P, MB])
        ysb = part(m0 + 3 * D + EF, [D])
        yget = [part(m0 + 4 * D + EF + n * D, [D]) for n in range(2)]
        fsum = part(m0 + 6 * D + EF, [D])
        rt = m0 + 7 * D + EF
        lg = part(rt, [TT, ROUTE])
        ge = part(rt + 216, [TT, NG])
        gsel = part(rt + 240, [TT, NG])
        ecand = part(rt + 264, [TT, NE])
        elog = part(rt + 456, [TT, NE])
        oh = [part(rt + 648 + 192 * n, [TT, NE]) for n in range(2)]
        both = part(rt + 1032, [TT, NE])
        rank = part(rt + 1224, [TT, NE])
        over = part(rt + 1416, [TT, NE])
        wr = part(rt + 1608, [KT, ROUTE])
        scal = part(rt + 1896, [12, TT])
        nbb = part(rt + 1968, [P])
        cmpb = part(rt + 2096, [TABW + 1])
        col = part(rt + 2096 + TABW + 1, [8])
        pos_f = part(rt + 2200, [2, 2, TT])
        pos_u = sb("pos_u", [P, 2, 2, TT], U32)
        tok_u = sb("tok_u", [P, TT], U32)
        tab_u = sb("tab_u", [P, TABW], U32)
        zeros = sb("zeros", [P, ZERO])
        idx_u = sb("idx_u", [P, 1], U32)
        exp_i = sb("exp_i", [1, TABW + 1], I32)

        bank = [ctx.enter_context(nc.psum_tensor(f"bank{i}", [P, 512], F32)) for i in range(8)]

        loaded = sem("loaded")
        lru_loaded, dft_loaded, wr_loaded = sem("lru_loaded"), sem("dft_loaded"), sem("wr_loaded")
        wload = [sem(f"wload{s}") for s in range(2)]
        full = [sem(f"full{j}") for j in range(4)]
        free = [sem(f"free{j}") for j in range(4)]
        phase_done = sem("phase_done")
        sq_ready, ssum_ready, std_ready, u_ready = (sem(n) for n in ("sq_ready", "ssum_ready", "std_ready", "u_ready"))
        cond_ready, act_ready = sem("cond_ready"), sem("act_ready")
        xbr_ready, xc_ready, raw_ready = sem("xbr_ready"), sem("xc_ready"), sem("raw_ready")
        lin_full, lin_free = sem("lin_full"), sem("lin_free")
        gates_ready, decay_ready, msq_ready, mult_ready = (sem(n) for n in ("gates_ready", "decay_ready", "msq_ready", "mult_ready"))
        gate_ready = sem("gate_ready")
        rope_full, rope_free, rope_ready = sem("rope_full"), sem("rope_free"), sem("rope_ready")
        qsq_ready, qsum_full, qstd_ready, qn_ready = (sem(n) for n in ("qsq_ready", "qsum_full", "qstd_ready", "qn_ready"))
        q_staged, s_full, s_evac, max_ready = (sem(n) for n in ("q_staged", "s_full", "s_evac", "max_ready"))
        exp_ready, p_ready, t_full, t_evac = (sem(n) for n in ("exp_ready", "p_ready", "t_full", "t_evac"))
        o_full, o_evac = sem("o_full"), sem("o_evac")
        ac_full, ac_ready, dft_full, dft_evac, conv_ready = (sem(n) for n in ("ac_full", "ac_ready", "dft_full", "dft_evac", "conv_ready"))
        mrg_ready = sem("mrg_ready")
        moe = [{n: sem(f"{n}_{l}") for n in
                ("xt_tr", "xt_cp", "xt_out", "logits", "gexp_in", "gexp", "eexp_in", "eexp", "onehot", "counts", "nblk",
                 "starts", "cmp", "exp_row", "expert", "pos", "zeros", "scatter", "table", "gathered", "xt_full", "xt_ready", "gate_full",
                 "up_full", "sg_ready", "h_ready", "htp_full", "ht_ready", "y_full", "y_ready", "y_written", "y_last", "got",
                 "sum_ready", "sum_tr", "sum_read", "w2_done")} for l in range(2)]
        mload = [[sem(f"mload{c}_{l}") for c in range(6)] for l in range(2)]
        mdone = [[sem(f"mdone{c}_{l}") for c in range(2)] for l in range(2)]
        yb_zeroed, lat_final, stored = sem("yb_zeroed"), sem("lat_final"), sem("stored")

        block = ctx.enter_context(nc.Block())
        TILES_OF = [TT, LT]

        class Phase:
            def __init__(self, eng):
                self.eng, self.n = eng, 0

            def end(self):
                self.n += 1
                self.eng.drain().then_inc(phase_done, 1)
                self.eng.wait_ge(phase_done, 4 * self.n)

        def att_tiles(second, n):
            lo, hi = max(n - 1, 0), (min(n + 1, LT - 1) if second else n)
            return lo, hi + 1, (lo - n + 1) * P

        def att_groups(second, n):
            lo, hi, _ = att_tiles(second, n)
            per = hi - lo + (2 if second else 0)
            return per, -(-2 * per // 4)

        @block.sync
        def _(sp):
            for dst, src in ((consts[:, :], d["consts"]), (vecs[:, :], d["vecs"]), (lat[:, :, :], d["x"]),
                             (cxt[:, :, :], d["ctx"])):
                sp.dma_start(dst, src).then_inc(loaded, 16)

            def stream(name, its):
                r0, l0, c0 = plan[name]
                with sp.Fori(0, its) as i:
                    for s in range(2):
                        sp.wait_ge(full[2 * s + 1], r0 + i)
                        sp.dma_start(slot[s][:, 0:CHUNK],
                                     d["w"][bass.ds(c0 + 2 * i + s, 1)].rearrange("a p n -> (a p) n")).then_inc(wload[s], 16)

            def stream_down(name):
                r0, l0, c0 = plan[name]
                with sp.Fori(0, 2) as i:
                    for t in range(4):
                        s = t % 2
                        if t < 2:
                            sp.wait_ge(full[2 * s + 1], r0 + i)
                        else:
                            sp.wait_ge(full[2 * s], r0 + i + 1)
                        sp.dma_start(slot[s][:, :],
                                     d["wd"][bass.ds(c0 + 4 * i + t, 1)].rearrange("a p n -> (a p) n")).then_inc(wload[s], 16)

            def stream_paired(name, its):
                r0, l0, c0 = plan[name]
                with sp.Fori(0, its) as i:
                    for s in range(2):
                        if s == 0:
                            sp.wait_ge(full[1], r0)
                        sp.wait_ge(full[3], r0 + 2 * i - 1 + s)
                        sp.dma_start(slot[s][:, 0:CHUNK],
                                     d["w"][bass.ds(c0 + 2 * i + s, 1)].rearrange("a p n -> (a p) n")).then_inc(wload[s], 16)

            def stream_experts(l):
                q = moe[l]
                w1 = d["w1"].rearrange("l e (h k p) f -> (l e) h p k f", h=2, p=P)
                w3 = d["w3"].rearrange("l e (h k p) f -> (l e) h p k f", h=2, p=P)
                w2 = d["w2"].rearrange("l e (h k p) f -> (l e) h p k f", h=2, p=P)

                def load(c, w, e, half):
                    dst = wslot[c].rearrange("p (k f) -> p k f", k=4 if c < 4 else 2)
                    sp.dma_start(dst, w[bass.ds(e + l * NE, 1), half].rearrange("e p k f -> (e p) k f")).then_inc(mload[l][c], 16)

                def up(b, first=False):
                    e = sp.value_load(exp_i[0:1, bass.ds(b, 1)], min_val=0, max_val=NE - 1)
                    for c in range(4):
                        if not first:
                            sp.wait_ge([mdone[l][0], q["gate_full"], mdone[l][1], q["up_full"]][c], b)
                        load(c, w1 if c < 2 else w3, e, c % 2)

                def down(b, first=False):
                    e = sp.value_load(exp_i[0:1, bass.ds(b, 1)], min_val=0, max_val=NE - 1)
                    if not first:
                        sp.wait_ge(q["w2_done"], b)
                    for c in range(4, 6):
                        load(c, w2, e, c % 2)

                sp.wait_ge(q["expert"], 1)
                last = sp.value_load(exp_i[0:1, TABW:TABW + 1], min_val=2, max_val=NBMAX - 1)
                up(0, first=True)
                up(1)
                down(0, first=True)
                with sp.Fori(2, last + 1) as b:
                    up(b)
                    down(b - 1)
                down(last)

            stream("mod", 24)
            stream("gu1", 11)
            stream_down("down1")
            stream("xbr", 2)
            stream("q1", 2)
            stream("kv1", 1)
            stream("gate", 2)
            stream("merge", 8)
            stream("out1", 2)
            stream("gu2", 11)
            stream_down("down2")
            stream_paired("even_in", 4)
            stream_paired("even_out", 2)
            stream_experts(0)
            stream("q2", 2)
            stream_paired("kv2", 1)
            stream("wo", 2)
            stream_experts(1)
            sp.wait_ge(lat_final, 1)
            sp.dma_start(d["out"], lat[:, :, :]).then_inc(stored, 16)
            sp.wait_ge(stored, 16)

        @block.tensor
        def _(pe):
            phase = Phase(pe)
            norms = [0]

            def dense(name, its, rhs):
                r0, l0, _ = plan[name]
                with pe.Fori(0, its) as i:
                    for j in range(4):
                        s = j // 2
                        if j % 2 == 0:
                            pe.wait_ge(wload[s], 16 * l0 + 16 + i * 16)
                        pe.wait_ge(free[j], r0 + i)
                        for k in range(KT):
                            w = slot[s][:, (j % 2) * KT * P + k * P:(j % 2) * KT * P + (k + 1) * P]
                            m = rhs(j, k)
                            mm = nc.tensor.matmul(bank[j][:, 0:m.shape[1]], w, m, start=(k == 0), stop=(k == KT - 1))
                        mm.then_inc(full[j], 1)

            def down(name):
                r0, l0, _ = plan[name]
                with pe.Fori(0, 2) as i:
                    for t in range(4):
                        s, j = t % 2, (0, 2, 1, 3)[t]
                        pe.wait_ge(wload[s], 16 * l0 + 16 + 16 * (t // 2) + i * 32)
                        pe.wait_ge(free[j], r0 + i)
                        for k in range(FT):
                            mm = nc.tensor.matmul(bank[j][:, :], slot[s][:, k * P:(k + 1) * P], act_t[:, k, :],
                                                  start=(k == 0), stop=(k == FT - 1))
                        mm.then_inc(full[j], 1)

            def paired(name, its, rhs, first=0):
                r0, l0, _ = plan[name]
                with pe.Fori(0, its) as i:
                    for s in range(2):
                        pe.wait_ge(wload[s], 16 * l0 + 16 + i * 16)
                        for j in range(4):
                            pe.wait_ge(free[j], r0 + s + i * 2)
                            a, n = ((0, S), (S, C))[j % 2]
                            for k in range(KT):
                                w = slot[s][:, (j // 2) * KT * P + k * P:(j // 2) * KT * P + (k + 1) * P]
                                mm = nc.tensor.matmul(bank[j][:, 0:n], w, rhs[:, k, a:a + n],
                                                      start=(k == 0), stop=(k == KT - 1))
                            mm.then_inc(full[j], 1)

            def norm_sum(u, context=False):
                n = norms[0]
                norms[0] += 1
                for k in range(KT):
                    pe.wait_ge(sq_ready, KT * n + k + 1)
                    mm = nc.tensor.matmul(bank[4][:, :], ones, u[:, k, 0:S], start=(k == 0), stop=(k == KT - 1))
                    if context:
                        mm = nc.tensor.matmul(bank[5][:, 0:C], ones, u[:, k, S:SC], start=(k == 0), stop=(k == KT - 1))
                mm.then_inc(ssum_ready, 1)

            def normed(n):
                pe.wait_ge(u_ready, KT * n)

            def ffn(n, n_norm):
                norm_sum(u1)
                normed(n_norm)
                dense(f"gu{n}", 11, lambda j, k: u1[:, k, :])
                pe.wait_ge(act_ready, n)
                down(f"down{n}")
                norm_sum(u1)
                phase.end()

            def attend(second, i0, qs, sm, pT, kt, v):
                g0 = 0 if not second else 32
                per_it = sum(att_groups(second, n)[1] for n in range(LT))
                for kv in range(2):
                    with pe.Fori(0, 4) as i:
                        it = i0 + 4 * kv

                        def scores(n):
                            lo, hi, _ = att_tiles(second, n)
                            pe.wait_ge(q_staged, 4 * it + n + 1 + i * 4)
                            pe.wait_ge(s_evac, 4 * it + n + 1 + i * 4)
                            for s in range(2):
                                h = slice(64 * s, 64 * s + 64)
                                mm = nc.tensor.matmul(bank[s][:, 0:(hi - lo) * P], qs[h, n * P:(n + 1) * P],
                                                      kt[h, kv, lo * P:hi * P], start=True, stop=True)
                                if second:
                                    mm = nc.tensor.matmul(bank[2 + s][:, 0:C], qs[h, n * P:(n + 1) * P],
                                                          kt[h, kv, S:SC], start=True, stop=True)
                            mm.then_inc(s_full, 1)

                        def values(n):
                            lo, hi, _ = att_tiles(second, n)
                            per, groups = att_groups(second, n)
                            before = sum(att_groups(second, m)[1] for m in range(n))
                            pe.wait_ge(p_ready, 4 * it + n + 1 + i * 4)
                            for g in range(groups):
                                at = g0 + kv * 4 * per_it + before + g
                                pe.wait_ge(t_evac, at + 1 + i * per_it)
                                for x in range(4 * g, min(4 * g + 4, 2 * per)):
                                    tr = nc.tensor.transpose(bank[4 + at % 2][:, (x % 4) * P:(x % 4 + 1) * P],
                                                             sm[:, n % 2, x // per, (x % per) * P:(x % per + 1) * P], ident)
                                tr.then_inc(t_full, 1)
                            pe.wait_ge(t_evac, g0 + kv * 4 * per_it + before + groups + 2 + i * per_it)
                            pe.wait_ge(o_evac, 4 * it + n + 1 + i * 4)
                            for s in range(2):
                                for x in range(per):
                                    tile = lo + x if x < hi - lo else LT + x - (hi - lo)
                                    mm = nc.tensor.matmul(bank[6 + n % 2][64 * s:64 * s + 64, 0:P],
                                                          v[:, tile, (2 * kv + s) * HD:(2 * kv + s + 1) * HD],
                                                          pT[:, n % 2, (s * per + x) * P:(s * per + x + 1) * P],
                                                          start=(x == 0), stop=(x == per - 1))
                            mm.then_inc(o_full, 1)

                        scores(0)
                        for n in range(LT):
                            if n + 1 < LT:
                                scores(n + 1)
                            values(n)

            def rope(at, src, swap, count0):
                for x, a in enumerate(src):
                    pe.wait_ge(rope_free, count0 + x + 1)
                    at(x)
                    nc.tensor.matmul(bank[6][:, 0:a.shape[1]], swap, a, start=True, stop=True).then_inc(rope_full, 1)

            def moe_layer(l):
                q, nt = moe[l], TILES_OF[l]
                for t in range(nt):
                    if t > 0:
                        pe.wait_ge(q["xt_cp"], 2 * t)
                    for k in range(KT):
                        tr = nc.tensor.transpose(bank[k // 4][:, (k % 4) * P:(k % 4 + 1) * P], u2[:, k, t * P:(t + 1) * P], ident)
                    tr.then_inc(q["xt_tr"], 1)
                pe.wait_ge(wr_loaded, 16 * (l + 1))
                for t in range(nt):
                    for k in range(KT):
                        mm = nc.tensor.matmul(bank[2][:, t * ROUTE:(t + 1) * ROUTE], u2[:, k, t * P:(t + 1) * P], wr[:, k, :],
                                              start=(k == 0), stop=(k == KT - 1))
                mm.then_inc(q["logits"], 1)
                pe.wait_ge(q["onehot"], 1)
                for t in range(nt):
                    for j in range(t + 1):
                        nc.tensor.matmul(bank[3][:, t * NE:(t + 1) * NE], ones if j < t else const("before"), both[:, j, :],
                                         start=(j == 0), stop=(j == t))
                for j in range(nt):
                    mm = nc.tensor.matmul(bank[4][0:NE, 0:2], both[:, j, :], ones[:, 0:2], start=(j == 0), stop=(j == nt - 1))
                mm.then_inc(q["counts"], 1)
                pe.wait_ge(q["nblk"], 1)
                nc.tensor.matmul(bank[5][:, 0:NE], nbb[0:NE, :], const("tri_lt")[0:NE, :], start=True, stop=True)
                nc.tensor.matmul(bank[6][0:NE, 0:2], const("tri_le")[0:NE, :], nbb[0:NE, 0:2], start=True, stop=True)
                nc.tensor.matmul(bank[7][0:2, TABW:TABW + 2], nbb[0:NE, 0:2], ones[0:NE, 0:2], start=True, stop=True).then_inc(q["starts"], 1)
                pe.wait_ge(q["cmp"], 1)
                nc.tensor.matmul(bank[6][0:2, 64:64 + TABW], ones[0:NE, 0:2], cmpb[0:NE, 0:TABW], start=True, stop=True).then_inc(q["exp_row"], 1)

                def spread_x(b):
                    pe.wait_ge(q["gathered"], 16 * (b + 1))
                    for k in range(KT):
                        tr = nc.tensor.transpose(bank[2 + k // 4][:, (k % 4) * P:(k % 4 + 1) * P], xg[:, k * P:(k + 1) * P], ident)
                    tr.then_inc(q["xt_full"], 1)

                def up(b, first=False):
                    pe.wait_ge(q["xt_ready"], 2 * (b + 1))
                    if not first:
                        pe.wait_ge(q["h_ready"], b)
                    for c in range(4):
                        pe.wait_ge(mload[l][c], 16 * (b + 1))
                        for k in range(4):
                            mm = nc.tensor.matmul(bank[c // 2][:, :], xT[:, 4 * (c % 2) + k, :], wslot[c][:, k * EF:(k + 1) * EF],
                                                  start=(c % 2 == 0 and k == 0), stop=(c % 2 == 1 and k == 3))
                        mm.then_inc([mdone[l][0], q["gate_full"], mdone[l][1], q["up_full"]][c], 1)

                def out(b, first=False):
                    pe.wait_ge(q["ht_ready"], b + 1)
                    if not first:
                        pe.wait_ge(q["y_ready"], 2 * b)
                    for c in range(2):
                        pe.wait_ge(mload[l][4 + c], 16 * (b + 1))
                        for k in range(2):
                            for n in range(2):
                                mm = nc.tensor.matmul(bank[4 + n][:, :], hT[:, 2 * c + k, :],
                                                      wslot[4 + c][:, k * D + n * 512:k * D + (n + 1) * 512],
                                                      start=(c == 0 and k == 0), stop=(c == 1 and k == 1))
                    mm.then_inc(q["w2_done"], 1)

                def spread_h(b):
                    pe.wait_ge(q["h_ready"], b + 1)
                    for k in range(EF // P):
                        tr = nc.tensor.transpose(bank[6][:, k * P:(k + 1) * P], hmul[:, k * P:(k + 1) * P], ident)
                    tr.then_inc(q["htp_full"], 1)

                phase.end()
                last = pe.value_load(exp_i[0:1, TABW:TABW + 1], min_val=2, max_val=NBMAX - 1)
                spread_x(0)
                up(0, first=True)
                spread_x(1)
                spread_h(0)
                up(1)
                spread_x(2)
                out(0, first=True)
                spread_h(1)
                with pe.Fori(2, last + 1) as b:
                    up(b)
                    spread_x(b + 1)
                    out(b - 1)
                    spread_h(b)
                out(last)
                phase.end()
                for t in range(nt):
                    pe.wait_ge(q["sum_ready"], t + 1)
                    if t > 0:
                        pe.wait_ge(q["sum_read"], t)
                    for k in range(KT):
                        tr = nc.tensor.transpose(bank[k // 4][:, (k % 4) * P:(k % 4 + 1) * P], fsum[:, k * P:(k + 1) * P], ident)
                    tr.then_inc(q["sum_tr"], 1)
                phase.end()

            pe.wait_ge(loaded, 64)
            for j in range(4):
                nc.tensor.matmul(bank[j][:, 0:P], ident, ident, start=True, stop=True).then_inc(full[j], 1)
            pe.wait_ge(cond_ready, 1)
            dense("mod", 24, lambda j, k: silu_c[:, k, :])
            phase.end()
            ffn(1, 1)

            norm_sum(u1)
            normed(3)
            dense("xbr", 2, lambda j, k: u1[:, k, :])
            dense("q1", 2, lambda j, k: u1[:, k, :])
            r0, l0, _ = plan["kv1"]
            pe.wait_ge(wload[0], 16 * (l0 + 1))
            for j in range(2):
                pe.wait_ge(free[j], r0)
                for k in range(KT):
                    mm = nc.tensor.matmul(bank[j][:, :], slot[0][:, j * KT * P + k * P:j * KT * P + (k + 1) * P], u1[:, k, :],
                                          start=(k == 0), stop=(k == KT - 1))
                mm.then_inc(full[j], 1)
            pe.wait_ge(wload[1], 16 * (l0 + 1))
            for j in range(2):
                pe.wait_ge(free[2 + j], r0)
                for t in range(2):
                    for k in range(KT):
                        mm = nc.tensor.matmul(bank[2 + j][:, t * C:(t + 1) * C], u1[:, k, (2 * j + t) * P:(2 * j + t + 1) * P],
                                              slot[1][:, k * C:(k + 1) * C], start=(k == 0), stop=(k == KT - 1))
                mm.then_inc(full[2 + j], 1)
            dense("gate", 2, lambda j, k: u1[:, k, :])
            pe.wait_ge(lru_loaded, 16)
            for t in range(KT):
                pe.wait_ge(xc_ready, t + 1)
                if t > 0:
                    pe.wait_ge(lin_free, t)
                nc.tensor.matmul(bank[4][:, :], lru_w[:, 0, t, :], xc[:, t, :], start=True, stop=True)
                nc.tensor.matmul(bank[5][:, :], lru_w[:, 1, t, :], xc[:, t, :], start=True, stop=True).then_inc(lin_full, 1)
            rope(lambda x: pe.wait_ge(raw_ready, 1 if x < KT else 2), [qt1[:, x, :] for x in range(KT)] + [kt1[:, x, :] for x in range(2)],
                 const("swap1"), 0)
            phase.end()
            attend(False, 0, *att_views(o), kt1, v1)
            phase.end()
            dense("merge", 8, lambda j, k: (u1, xc, u1, f)[j][:, k, :])
            pe.wait_ge(mrg_ready, 8)
            dense("out1", 2, lambda j, k: merged[:, k, :])
            norm_sum(u1)
            phase.end()
            ffn(2, 5)

            norm_sum(u2, context=True)
            normed(7)
            paired("even_in", 4, u2)
            phase.end()
            pe.wait_ge(dft_loaded, 80)
            for g in range(4):
                if g > 0:
                    pe.wait_ge(ac_ready, 3 * g)
                for t in range(TT):
                    mm = nc.tensor.matmul(bank[t // 2][:, (t % 2) * 2 * P:(t % 2 + 1) * 2 * P], pt[:, g, t * P:(t + 1) * P], csd,
                                          start=True, stop=True)
                    if t % 2:
                        mm.then_inc(ac_full, 1)
                if g > 0:
                    pe.wait_ge(dft_evac, g)
                pe.wait_ge(ac_ready, 3 * g + 3)
                for t in range(LT):
                    nc.tensor.matmul(bank[3][:, :], ac[:, t, 0:P], c_lat[:, t, :], start=(t == 0), stop=False)
                    nc.tensor.matmul(bank[3][:, :], ac[:, t, P:2 * P], s_lat[:, t, :], start=False, stop=(t == LT - 1))
                for t in range(2):
                    nc.tensor.matmul(bank[4][:, 0:C], ac[:, LT + t, 0:P], c_ctx[:, t, :], start=(t == 0), stop=False)
                    mm = nc.tensor.matmul(bank[4][:, 0:C], ac[:, LT + t, P:2 * P], s_ctx[:, t, :], start=False, stop=(t == 1))
                mm.then_inc(dft_full, 1)
            phase.end()
            paired("even_out", 2, yt)
            phase.end()
            norm_sum(u2, context=True)
            normed(8)
            moe_layer(0)

            norm_sum(u2, context=True)
            normed(9)
            dense("q2", 2, lambda j, k: u2[:, k, 0:S])
            r0, l0, _ = plan["kv2"]
            pe.wait_ge(wload[0], 16 * (l0 + 1))
            for j in range(4):
                pe.wait_ge(free[j], r0)
                a, n = ((0, S), (S, C))[j % 2]
                for k in range(KT):
                    mm = nc.tensor.matmul(bank[j][:, 0:n], slot[0][:, (j // 2) * KT * P + k * P:(j // 2) * KT * P + (k + 1) * P],
                                          u2[:, k, a:a + n], start=(k == 0), stop=(k == KT - 1))
                mm.then_inc(full[j], 1)
            pe.wait_ge(wload[1], 16 * (l0 + 1))
            for j in range(4):
                pe.wait_ge(free[j], r0 + 1)
                for t in ((0, 1), (2, 3), (4,), (5,))[j]:
                    for k in range(KT):
                        mm = nc.tensor.matmul(bank[j][:, (t % 2 if j < 2 else 0) * C:(t % 2 if j < 2 else 0) * C + C],
                                              u2[:, k, t * P:(t + 1) * P], slot[1][:, k * C:(k + 1) * C],
                                              start=(k == 0), stop=(k == KT - 1))
                mm.then_inc(full[j], 1)
            for x in range(KT + 4):
                pe.wait_ge(qsq_ready, x + 1)
                if x > 0:
                    pe.wait_ge(qstd_ready, x)
                n = C if x in (KT + 1, KT + 3) else S
                nc.tensor.matmul(bank[4][:, 0:n], const("headsum"), tmp[:, x % 2, 0:n], start=True, stop=True).then_inc(qsum_full, 1)
            rope(lambda x: pe.wait_ge(qn_ready, x + 1 if x <= KT else KT + 3), [qt2[:, x, :] for x in range(KT)] + [kt2[:, x, 0:S] for x in range(2)],
                 const("swap2"), 10)
            phase.end()
            attend(True, 8, *att_views(att2), kt2, v2)
            phase.end()
            dense("wo", 2, lambda j, k: f[:, k, :])
            phase.end()
            norm_sum(u2)
            normed(10)
            moe_layer(1)

        @block.scalar
        def _(act):
            phase = Phase(act)
            norms = [0]

            def squares(src, u, a=0, last=True):
                for k in range(KT):
                    i = nc.scalar.activation(u[:, k, a:a + src.shape[2]], src[:, k, :], ACT.Square)
                    if last:
                        i.then_inc(sq_ready, 1)

            def std(context=False):
                norms[0] += 1
                act.wait_ge(ssum_ready, norms[0])
                i = nc.scalar.activation(rs[:, 0:S], bank[4][:, :], ACT.Sqrt, bias=const("eps"), scale=1.0 / D)
                if context:
                    i = nc.scalar.activation(rs[:, S:SC], bank[5][:, 0:C], ACT.Sqrt, bias=const("eps"), scale=1.0 / D)
                i.then_inc(std_ready, 1)

            def before_norm(name, its, order=(0, 1, 2, 3)):
                r0 = plan[name][0]
                with act.Fori(0, its) as i:
                    for n, j in enumerate(order):
                        act.wait_ge(full[j], r0 + 1 + i)
                        nc.scalar.activation(f[:, bass.ds(4 * i + n, 1), :].rearrange("p a t -> p (a t)"), bank[j][:, :], ACT.Copy)
                        nc.scalar.activation(u1[:, bass.ds(4 * i + n, 1), :].rearrange("p a t -> p (a t)"), bank[j][:, :],
                                             ACT.Square).then_inc(free[j], 1)
                act.drain().then_inc(sq_ready, KT)

            def evacuate(name, its, dst, n=S):
                r0 = plan[name][0]
                with act.Fori(0, its) as i:
                    for j in range(4):
                        act.wait_ge(full[j], r0 + 1 + i)
                        nc.scalar.activation(dst(4 * i + j), bank[j][:, 0:n], ACT.Copy).then_inc(free[j], 1)

            def ffn(n):
                squares(lat[:, :, :], u1)
                std()
                r0 = plan[f"gu{n}"][0]
                with act.Fori(0, 11) as i:
                    for j in range(2):
                        act.wait_ge(full[j], r0 + 1 + i)
                        act.wait_ge(free[2 + j], r0 + i)
                        nc.scalar.activation(tmp[:, j, :], bank[j][:, :], ACT.Silu).then_inc(free[j], 1)
                before_norm(f"down{n}", 2, (0, 2, 1, 3))
                std()
                phase.end()

            def attend(second, i0, qs, sm, pT):
                g0 = 0 if not second else 32
                per_it = sum(att_groups(second, n)[1] for n in range(LT))
                for kv in range(2):
                    with act.Fori(0, 4) as i:
                        it = i0 + 4 * kv

                        def exps(n):
                            per, _ = att_groups(second, n)
                            st = small[:, 16 * (n % 2):16 * (n % 2) + 16]
                            act.wait_ge(max_ready, 4 * it + n + 1 + i * 4)
                            for s in range(2):
                                nc.scalar.activation(sm[:, n % 2, s, 0:per * P], sm[:, n % 2, s, 0:per * P], ACT.Exp,
                                                     bias=st[:, 4 + s:5 + s], accum_out=st[:, 6 + s:7 + s])
                            nc.scalar.activation(st[:, 8:10], st[:, 10:12], ACT.Exp)
                            act.drain().then_inc(exp_ready, 1)

                        def copies(n):
                            per, groups = att_groups(second, n)
                            before = sum(att_groups(second, m)[1] for m in range(n))
                            for g in range(groups):
                                at = g0 + kv * 4 * per_it + before + g
                                w = min(4, 2 * per - 4 * g) * P
                                act.wait_ge(t_full, at + 1 + i * per_it)
                                nc.scalar.activation(pT[:, n % 2, 4 * g * P:4 * g * P + w], bank[4 + at % 2][:, 0:w],
                                                     ACT.Copy).then_inc(t_evac, 1)

                        def outputs(n):
                            act.wait_ge(o_full, 4 * it + n + 3 + i * 4)
                            nc.scalar.activation(f[:, bass.ds(4 * kv + i, 1), n * P:(n + 1) * P].rearrange("p a t -> p (a t)"),
                                                 bank[6 + n % 2][:, 0:P], ACT.Copy).then_inc(o_evac, 1)

                        exps(0)
                        for n in range(LT):
                            if n + 1 < LT:
                                exps(n + 1)
                            copies(n)
                            outputs(n)

            def moe_layer(l):
                q, nt = moe[l], TILES_OF[l]
                act.dma_start(wr, d["wr"][l]).then_inc(wr_loaded, 16)
                for t in range(nt):
                    act.wait_ge(q["xt_tr"], t + 1)
                    if t > 0:
                        act.wait_ge(q["xt_out"], 16 * t)
                    nc.scalar.activation(xg[:, 0:512], bank[0][:, :], ACT.Copy).then_inc(q["xt_cp"], 1)
                act.wait_ge(q["gexp_in"], 1)
                nc.scalar.activation(ge[:, 0:nt, :], ge[:, 0:nt, :], ACT.Exp).then_inc(q["gexp"], 1)
                act.wait_ge(q["eexp_in"], 1)
                nc.scalar.activation(scal[:, 5, 0:nt], scal[:, 4, 0:nt], ACT.Exp).then_inc(q["eexp"], 1)

                def copy_x(b):
                    act.wait_ge(q["xt_full"], b + 1)
                    nc.scalar.activation(xT[:, 0:4, :], bank[2][:, :], ACT.Copy).then_inc(q["xt_ready"], 1)

                def silu(b, first=False):
                    act.wait_ge(q["gate_full"], b + 1)
                    if not first:
                        act.wait_ge(q["h_ready"], b)
                    nc.scalar.activation(hsil, bank[0][:, :], ACT.Silu).then_inc(q["sg_ready"], 1)

                def copy_y(b, first=False):
                    act.wait_ge(q["w2_done"], b + 1)
                    if not first:
                        act.wait_ge(q["y_written"], 16 * b)
                    nc.scalar.activation(ysb[:, 0:512], bank[4][:, :], ACT.Copy).then_inc(q["y_ready"], 1)

                phase.end()
                last = act.value_load(exp_i[0:1, TABW:TABW + 1], min_val=2, max_val=NBMAX - 1)
                copy_x(0)
                silu(0, first=True)
                copy_x(1)
                silu(1)
                copy_x(2)
                copy_y(0, first=True)
                with act.Fori(2, last + 1) as b:
                    silu(b)
                    copy_x(b + 1)
                    copy_y(b - 1)
                copy_y(last)
                phase.end()
                phase.end()

            act.wait_ge(loaded, 64)
            nc.scalar.activation(silu_c[:, :, :], vec("cond").rearrange("p (k s) -> p k s", k=KT), ACT.Silu).then_inc(cond_ready, 1)
            phase.end()
            ffn(1)

            act.dma_start(lru_w, d["lru_w"]).then_inc(lru_loaded, 16)
            squares(lat[:, :, :], u1)
            std()
            act.wait_ge(cond_ready, 2)
            nc.scalar.activation(lam8[:, 4, :], lam8[:, 3, :], ACT.Exp).then_inc(cond_ready, 1)
            r0 = plan["xbr"][0]
            with act.Fori(0, 2) as i:
                for j in range(4):
                    act.wait_ge(full[j], r0 + 1 + i)
                    nc.scalar.activation(xbr[:, bass.ds(4 * i + j, 1), CONV1 - 1:XPAD].rearrange("p a t -> p (a t)"),
                                         bank[j][:, :], ACT.Copy).then_inc(free[j], 1)
            act.drain().then_inc(xbr_ready, 1)
            evacuate("q1", 2, lambda x: qt1[:, bass.ds(x, 1), :].rearrange("p a t -> p (a t)"))
            act.drain().then_inc(raw_ready, 1)
            r0 = plan["kv1"][0]
            for j in range(4):
                act.wait_ge(full[j], r0 + 1)
                nc.scalar.activation(kt1[:, j, :] if j < 2 else v1[:, 2 * (j - 2):2 * (j - 2) + 2, :], bank[j][:, :],
                                     ACT.Copy).then_inc(free[j], 1)
            act.drain().then_inc(raw_ready, 1)
            r0 = plan["gate"][0]
            with act.Fori(0, 2) as i:
                for j in range(4):
                    act.wait_ge(full[j], r0 + 1 + i)
                    nc.scalar.activation(f[:, bass.ds(4 * i + j, 1), :].rearrange("p a t -> p (a t)"), bank[j][:, :],
                                         ACT.Gelu_apprx_tanh).then_inc(free[j], 1)
            act.drain().then_inc(gate_ready, 1)
            ba, bx = vec("lru_b_a"), vec("lru_b_x")
            for t in range(KT):
                act.wait_ge(lin_full, t + 1)
                nc.scalar.activation(gr[:, t, :], bank[4][:, :], ACT.Sigmoid, bias=ba[:, t:t + 1])
                nc.scalar.activation(gi[:, t, :], bank[5][:, :], ACT.Sigmoid, bias=bx[:, t:t + 1]).then_inc(lin_free, 1)
            act.drain()
            for t in range(KT):
                nc.scalar.activation(xbr[:, t, 0:S], gr[:, t, :], ACT.Exp, scale=lam8[:, 1, t:t + 1])
                nc.scalar.activation(gr[:, t, :], gr[:, t, :], ACT.Tanh, scale=lam8[:, 0, t:t + 1])
                act.drain().then_inc(decay_ready, 1)
            for t in range(KT):
                act.wait_ge(msq_ready, t + 1)
                nc.scalar.activation(gr[:, t, :], gr[:, t, :], ACT.Sqrt).then_inc(mult_ready, 1)
            phase.end()
            attend(False, 0, *att_views(o))
            phase.end()
            r0 = plan["merge"][0]
            with act.Fori(0, 8) as i:
                for n in range(2):
                    act.wait_ge(full[2 * n], r0 + 1 + i)
                    act.wait_ge(free[2 * n + 1], r0 + i)
                    nc.scalar.activation(tmp[:, n, :], bank[2 * n][:, :], ACT.Sigmoid).then_inc(free[2 * n], 1)
            before_norm("out1", 2)
            std()
            phase.end()
            ffn(2)

            for dst, name in ((csd, "cs_d"), (c_ctx, "c_ctx"), (s_ctx, "s_ctx"), (c_lat, "c_lat"), (s_lat, "s_lat")):
                a, n = DFT_AT[name]
                src = d["dft"][:, a:a + n]
                if len(dst.shape) == 3:
                    src = src.rearrange("p (l t) -> p l t", l=dst.shape[1])
                act.dma_start(dst, src).then_inc(dft_loaded, 16)
            squares(cxt[:, :, :], u2, S, last=False)
            squares(lat[:, :, :], u2)
            std(context=True)
            r0 = plan["even_in"][0]
            with act.Fori(0, 8) as i:
                for j in range(4):
                    act.wait_ge(full[j], r0 + 1 + i)
                    a, n = ((0, S), (S, C))[j % 2]
                    nc.scalar.activation(pt[:, bass.ds(2 * i + j // 2, 1), a:a + n].rearrange("p a t -> p (a t)"), bank[j][:, 0:n],
                                         ACT.Copy).then_inc(free[j], 1)
            phase.end()
            for g in range(4):
                if g > 0:
                    act.wait_ge(dft_full, g)
                for h in range(3):
                    act.wait_ge(ac_full, 3 * g + h + 1)
                    nc.scalar.activation(ac[:, 2 * h:2 * h + 2, :], bank[h][:, :], ACT.Copy).then_inc(ac_ready, 1)
                act.wait_ge(dft_full, g + 1)
                nc.scalar.activation(yt[:, g, 0:S], bank[3][:, :], ACT.Copy)
                nc.scalar.activation(yt[:, g, S:SC], bank[4][:, 0:C], ACT.Copy).then_inc(dft_evac, 1)
            phase.end()
            phase.end()
            squares(cxt[:, :, :], u2, S, last=False)
            squares(lat[:, :, :], u2)
            std(context=True)
            moe_layer(0)

            squares(cxt[:, :, :], u2, S, last=False)
            squares(lat[:, :, :], u2)
            std(context=True)
            evacuate("q2", 2, lambda x: qt2[:, bass.ds(x, 1), :].rearrange("p a t -> p (a t)"))
            r0 = plan["kv2"][0]
            for j in range(4):
                act.wait_ge(full[j], r0 + 1)
                a, n = ((0, S), (S, C))[j % 2]
                nc.scalar.activation(kt2[:, j // 2, a:a + n], bank[j][:, 0:n], ACT.Copy).then_inc(free[j], 1)
            for j in range(4):
                act.wait_ge(full[j], r0 + 2)
                a, n = ((0, 2), (2, 2), (4, 1), (5, 1))[j]
                nc.scalar.activation(v2[:, a:a + n, :], bank[j][:, 0:n * C], ACT.Copy).then_inc(free[j], 1)
            act.drain()
            heads = [qt2[:, x, :] for x in range(KT)] + [kt2[:, x, a:b] for x in range(2) for a, b in ((0, S), (S, SC))]
            for x, a in enumerate(heads):
                n = a.shape[1]
                if x > 1:
                    act.wait_ge(qsum_full, x - 1)
                nc.scalar.activation(tmp[:, x % 2, 0:n], a, ACT.Square).then_inc(qsq_ready, 1)
                act.wait_ge(qsum_full, x + 1)
                if x > 1:
                    act.wait_ge(qn_ready, x - 1)
                nc.scalar.activation(tmp[:, 2 + x % 2, 0:n], bank[4][:, 0:n], ACT.Sqrt, bias=const("eps"),
                                     scale=1.0 / HD).then_inc(qstd_ready, 1)
            phase.end()
            attend(True, 8, *att_views(att2))
            phase.end()
            phase.end()
            squares(lat[:, :, :], u2)
            std()
            moe_layer(1)

        @block.vector
        def _(dve):
            phase = Phase(dve)
            norms = [0]

            def rsqrt(n):
                norms[0] += 1
                dve.wait_ge(std_ready, norms[0])
                nc.vector.reciprocal(rs[:, 0:n], rs[:, 0:n])
                dve.drain()

            def pre_norm(g, u):
                rsqrt(S)
                for k in range(KT):
                    nc.vector.scalar_tensor_tensor(u[:, k, :], lat[:, k, :], g[:, k:k + 1], rs[:, 0:S], ALU.mult,
                                                   ALU.mult).then_inc(u_ready, 1)

            def post_norm(g):
                rsqrt(S)
                for k in range(KT):
                    nc.vector.scalar_tensor_tensor(f[:, k, :], f[:, k, :], g[:, k:k + 1], rs[:, 0:S], ALU.mult, ALU.mult)
                    dve.drain()
                    nc.vector.tensor_tensor(lat[:, k, :], lat[:, k, :], f[:, k, :], ALU.add).then_inc(u_ready, 1)

            def mod_norm(l, which, context):
                rsqrt(SC if context else S)
                for k in range(KT):
                    parts = [(0, lat, 0, S)] + ([(1, cxt, S, C)] if context else [])
                    for st, src, a, n in parts:
                        nc.vector.scalar_tensor_tensor(u2[:, k, a:a + n], src[:, k, :], amod[:, l, which, st, k:k + 1],
                                                       rs[:, a:a + n], ALU.mult, ALU.mult)
                    dve.drain()
                    for st, src, a, n in parts:
                        i = nc.vector.tensor_scalar(u2[:, k, a:a + n], u2[:, k, a:a + n], mod[:, l, 3 * which, k, st:st + 1], None,
                                                    ALU.add)
                    i.then_inc(u_ready, 1)

            def ffn(n, pre, post):
                pre_norm(vec(pre), u1)
                r0 = plan[f"gu{n}"][0]
                with dve.Fori(0, 11) as i:
                    for j in range(2):
                        dve.wait_ge(full[2 + j], r0 + 1 + i)
                        dve.wait_ge(free[j], r0 + 1 + i)
                        nc.vector.tensor_tensor(act_t[:, bass.ds(2 * i + j, 1), :].rearrange("p a t -> p (a t)"), tmp[:, j, :],
                                                bank[2 + j][:, :], ALU.mult).then_inc(free[2 + j], 1)
                dve.drain().then_inc(act_ready, 1)
                post_norm(post)
                phase.end()

            def attend(second, i0, qs, sm, pT, sinks, mask):
                for kv in range(2):
                    with dve.Fori(0, 4) as i:
                        it = i0 + 4 * kv

                        def stats(n):
                            lo, hi, m0 = att_tiles(second, n)
                            per, _ = att_groups(second, n)
                            w = (hi - lo) * P
                            st = small[:, 16 * (n % 2):16 * (n % 2) + 16]
                            dve.wait_ge(s_full, 4 * it + n + 5 + i * 4)
                            dve.wait_ge(o_full, 4 * it + n + 1 + i * 4)
                            for s in range(2):
                                x = nc.vector.scalar_tensor_tensor(sm[:, n % 2, s, 0:w], bank[s][:, 0:w], SCALE, mask[:, m0:m0 + w],
                                                                   ALU.mult, ALU.add)
                                if second:
                                    x = nc.vector.tensor_scalar(sm[:, n % 2, s, w:w + C], bank[2 + s][:, 0:C], SCALE, None, ALU.mult)
                            x.then_inc(s_evac, 1)
                            dve.drain()
                            nc.vector.tensor_reduce(st[:, 0:2], sm[:, n % 2, :, 0:per * P], AX.X, ALU.max)
                            dve.drain()
                            sk = sinks[:, bass.ds(8 * kv + 2 * i, 2)]
                            nc.vector.tensor_tensor(st[:, 2:4], st[:, 0:2], sk, ALU.max)
                            dve.drain()
                            nc.vector.tensor_scalar(st[:, 4:6], st[:, 2:4], -1.0, None, ALU.mult)
                            nc.vector.tensor_tensor(st[:, 10:12], sk, st[:, 2:4], ALU.subtract)
                            dve.drain().then_inc(max_ready, 1)

                        def normalise(n):
                            per, _ = att_groups(second, n)
                            st = small[:, 16 * (n % 2):16 * (n % 2) + 16]
                            dve.wait_ge(exp_ready, 4 * it + n + 1 + i * 4)
                            nc.vector.tensor_tensor(st[:, 12:14], st[:, 6:8], st[:, 8:10], ALU.add)
                            dve.drain()
                            nc.vector.reciprocal(st[:, 14:16], st[:, 12:14])
                            dve.drain()
                            for s in range(2):
                                x = nc.vector.tensor_scalar(sm[:, n % 2, s, 0:per * P], sm[:, n % 2, s, 0:per * P],
                                                            st[:, 14 + s:15 + s], None, ALU.mult)
                            x.then_inc(p_ready, 1)

                        stats(0)
                        for n in range(LT):
                            if n + 1 < LT:
                                stats(n + 1)
                            normalise(n)

            def rope(src, cos, sin, count0):
                for x, a in enumerate(src):
                    dve.wait_ge(rope_full, count0 + x + 1)
                    nc.vector.tensor_tensor(rs[:, 0:S], bank[6][:, :], sin, ALU.mult).then_inc(rope_free, 1)
                    nc.vector.tensor_tensor(a, a, cos, ALU.mult)
                    dve.drain()
                    nc.vector.tensor_tensor(a, a, rs[:, 0:S], ALU.add)
                    dve.drain()

            def moe_layer(l):
                q, nt = moe[l], TILES_OF[l]
                for t in range(nt):
                    dve.wait_ge(q["xt_tr"], t + 1)
                    if t > 0:
                        dve.wait_ge(q["xt_out"], 16 * t)
                    nc.vector.tensor_copy(xg[:, 512:D], bank[1][:, :]).then_inc(q["xt_cp"], 1)

                def bc(x, n):
                    return x.unsqueeze(2).to_broadcast([P, x.shape[1], n])

                def over_last(dst, src, op):
                    nc.vector.tensor_reduce(dst, src, AX.X, op)
                    dve.drain()

                def first_max(dst, cand, src, best, desc, n):
                    nc.vector.tensor_tensor(cand, src, bc(best, n), ALU.is_equal)
                    dve.drain()
                    nc.vector.tensor_tensor(cand, cand, desc.unsqueeze(1).to_broadcast([P, nt, n]), ALU.mult)
                    dve.drain()
                    over_last(scal[:, 11, 0:nt], cand, ALU.max)
                    nc.vector.tensor_tensor(dst, cand, bc(scal[:, 11, 0:nt], n), ALU.is_equal)
                    dve.drain()

                sc = lambda x: scal[:, x, 0:nt]
                lgv, gev, gsv, elv, ecv = lg[:, 0:nt, :], ge[:, 0:nt, :], gsel[:, 0:nt, :], elog[:, 0:nt, :], ecand[:, 0:nt, :]
                dve.wait_ge(q["logits"], 1)
                rb = vec("route_b")[:, l * TT * ROUTE:l * TT * ROUTE + nt * ROUTE]
                nc.vector.tensor_tensor(lgv.rearrange("p t r -> p (t r)"), bank[2][:, 0:nt * ROUTE], rb, ALU.add)
                dve.drain()
                over_last(sc(0), lgv[:, :, 0:NG], ALU.max)
                nc.vector.tensor_tensor(gev, lgv[:, :, 0:NG], bc(sc(0), NG), ALU.subtract)
                dve.drain().then_inc(q["gexp_in"], 1)
                dve.wait_ge(q["gexp"], 1)
                over_last(sc(1), gev, ALU.add)
                over_last(sc(2), gev, ALU.max)
                nc.vector.reciprocal(sc(1), sc(1))
                dve.drain()
                nc.vector.tensor_tensor(sc(1), sc(1), sc(2), ALU.mult)
                first_max(gsv, gev, gev, sc(2), const("gdesc"), NG)
                elg = elv.rearrange("p t (g e) -> p t g e", g=NG)
                for g in range(NG):
                    nc.vector.tensor_tensor(elg[:, :, g, :], lgv[:, :, NG + 8 * g:NG + 8 * g + 8], bc(gsv[:, :, g], 8), ALU.mult)
                nc.vector.tensor_scalar(gev, gsv, -NEG, NEG, ALU.mult, ALU.add)
                dve.drain()
                for g in range(NG):
                    nc.vector.tensor_tensor(elg[:, :, g, :], elg[:, :, g, :], bc(gev[:, :, g], 8), ALU.add)
                dve.drain()
                over_last(sc(2), elv, ALU.max)
                first_max(oh[0][:, 0:nt, :], ecv, elv, sc(2), const("edesc"), NE)
                nc.vector.scalar_tensor_tensor(elv, oh[0][:, 0:nt, :], 2 * NEG, elv, ALU.mult, ALU.add)
                dve.drain()
                over_last(sc(3), elv, ALU.max)
                first_max(oh[1][:, 0:nt, :], ecv, elv, sc(3), const("edesc"), NE)
                nc.vector.tensor_tensor(both[:, 0:nt, :], oh[0][:, 0:nt, :], oh[1][:, 0:nt, :], ALU.add)
                dve.drain().then_inc(q["onehot"], 1)
                nc.vector.tensor_tensor(sc(4), sc(3), sc(2), ALU.subtract)
                dve.drain().then_inc(q["eexp_in"], 1)
                dve.wait_ge(q["eexp"], 1)
                nc.vector.tensor_scalar(sc(6), sc(5), 1.0, None, ALU.add)
                dve.drain()
                nc.vector.reciprocal(sc(6), sc(6))
                dve.drain()
                nc.vector.tensor_tensor(sc(7), sc(6), sc(1), ALU.mult)
                dve.drain()
                nc.vector.tensor_tensor(sc(8), sc(7), sc(5), ALU.mult)
                dve.wait_ge(q["counts"], 1)
                nc.vector.tensor_scalar(col[0:NE, 0:1], bank[4][0:NE, 0:1], 1.0, None, ALU.mult)
                dve.drain()
                nthr = -(-2 * SC // 2 // MB)
                nc.vector.tensor_scalar(cmpb[0:NE, 0:nthr], const("thr")[0:NE, 0:nthr], col[0:NE, 0:1], None, ALU.is_lt)
                dve.drain()
                nc.vector.tensor_reduce(col[0:NE, 1:2], cmpb[0:NE, 0:nthr], AX.X, ALU.add)
                dve.drain()
                nc.vector.tensor_scalar(nbb[0:NE, :], ones[0:NE, :], col[0:NE, 1:2], None, ALU.mult)
                dve.drain().then_inc(q["nblk"], 1)
                dve.wait_ge(q["starts"], 1)
                nc.vector.tensor_copy(col[0:NE, 2:3], bank[6][0:NE, 0:1])
                dve.drain()
                nc.vector.tensor_scalar(cmpb[0:NE, 0:TABW], const("blocks")[0:NE, :], col[0:NE, 2:3], None, ALU.is_ge)
                dve.drain().then_inc(q["cmp"], 1)
                rkv, ovv = rank[:, 0:nt, :], over[:, 0:nt, :]
                nc.vector.tensor_copy(rkv.rearrange("p t e -> p (t e)"), bank[3][:, 0:nt * NE])
                dve.drain()
                nc.vector.tensor_scalar(ovv, rkv, float(MB), None, ALU.is_ge)
                dve.drain()
                for x in range(2, nthr):
                    nc.vector.scalar_tensor_tensor(ovv, rkv, float(MB * x), ovv, ALU.is_ge, ALU.add)
                    dve.drain()
                nc.vector.tensor_copy(nbb[:, 0:NE], bank[5][:, 0:NE])
                dve.drain()
                start = nbb[:, 0:NE].unsqueeze(1).to_broadcast([P, nt, NE])
                nc.vector.scalar_tensor_tensor(ecv, rkv, float(TABW), start, ALU.mult, ALU.add)
                nc.vector.scalar_tensor_tensor(elv, start, float(MB), rkv, ALU.mult, ALU.add)
                dve.drain()
                nc.vector.scalar_tensor_tensor(ecv, ovv, 1.0 - MB * TABW, ecv, ALU.mult, ALU.add)
                dve.drain()
                for which, src in ((0, elv), (1, ecv)):
                    for x in range(2):
                        nc.vector.tensor_tensor(lg[:, 0:nt, 0:NE], oh[x][:, 0:nt, :], src, ALU.mult)
                        dve.drain()
                        over_last(pos_f[:, which, x, 0:nt], lg[:, 0:nt, 0:NE], ALU.add)
                        nc.vector.tensor_copy(pos_u[:, which, x, 0:nt], pos_f[:, which, x, 0:nt])
                dve.drain().then_inc(q["pos"], 1)
                dve.wait_ge(q["exp_row"], 1)
                nc.vector.tensor_scalar(exp_i[0:1, 0:TABW], bank[6][0:1, 64:64 + TABW], float(NE - 1), None, ALU.min)
                nc.vector.tensor_scalar(exp_i[0:1, TABW:TABW + 1], bank[7][0:1, TABW:TABW + 1], -1.0, None, ALU.add)
                dve.drain().then_inc(q["expert"], 1)

                def copy_x(b):
                    dve.wait_ge(q["xt_full"], b + 1)
                    nc.vector.tensor_copy(xT[:, 4:8, :], bank[3][:, :]).then_inc(q["xt_ready"], 1)

                def mul(b, first=False):
                    dve.wait_ge(q["up_full"], b + 1)
                    dve.wait_ge(q["sg_ready"], b + 1)
                    if not first:
                        dve.wait_ge(q["htp_full"], b)
                    nc.vector.tensor_tensor(hmul, hsil, bank[1][:, :], ALU.mult).then_inc(q["h_ready"], 1)

                def copy_y(b, first=False):
                    dve.wait_ge(q["w2_done"], b + 1)
                    if not first:
                        dve.wait_ge(q["y_written"], 16 * b)
                    nc.vector.tensor_copy(ysb[:, 512:D], bank[5][:, :]).then_inc(q["y_ready"], 1)

                def copy_h(b):
                    dve.wait_ge(q["htp_full"], b + 1)
                    nc.vector.tensor_copy(hT, bank[6][:, :]).then_inc(q["ht_ready"], 1)

                phase.end()
                last = dve.value_load(exp_i[0:1, TABW:TABW + 1], min_val=2, max_val=NBMAX - 1)
                copy_x(0)
                mul(0, first=True)
                copy_x(1)
                copy_h(0)
                mul(1)
                copy_x(2)
                copy_y(0, first=True)
                copy_h(1)
                with dve.Fori(2, last + 1) as b:
                    mul(b)
                    copy_x(b + 1)
                    copy_y(b - 1)
                    copy_h(b)
                copy_y(last)
                phase.end()
                for t in range(nt):
                    dve.wait_ge(q["got"], 32 * (t + 1))
                    if t > 0:
                        dve.wait_ge(q["sum_tr"], t)
                    nc.vector.tensor_scalar(fsum, yget[0], scal[:, 7, t:t + 1], None, ALU.mult)
                    dve.drain()
                    nc.vector.scalar_tensor_tensor(fsum, yget[1], scal[:, 8, t:t + 1], fsum, ALU.mult, ALU.add).then_inc(q["sum_ready"], 1)
                    dve.wait_ge(q["sum_tr"], t + 1)
                    st, dst = (0, lat[:, :, t * P:(t + 1) * P]) if t < LT else (1, cxt[:, :, (t - LT) * P:(t - LT + 1) * P])
                    for k in range(KT):
                        x = nc.vector.scalar_tensor_tensor(dst[:, k, :], bank[k // 4][:, (k % 4) * P:(k % 4 + 1) * P],
                                                           mod[:, l, 5, k, st:st + 1], dst[:, k, :], ALU.mult, ALU.add)
                    x.then_inc(q["sum_read"], 1)
                phase.end()

            for s, n in ([(x, 1) for x in free] + [(s_full, 4), (s_evac, 1), (o_full, 2), (t_evac, 2), (o_evac, 1), (rope_free, 1)]):
                dve.drain().then_inc(s, n)
            dve.wait_ge(loaded, 64)
            nc.vector.tensor_scalar(half_g[:, 0, :], vec("ffn1_post_g"), 0.5, None, ALU.mult)
            nc.vector.tensor_scalar(half_g[:, 1, :], vec("ffn2_post_g"), 0.5, None, ALU.mult)
            r0 = plan["mod"][0]
            modf = mod[:, :, :, :, :].rearrange("p l s k c -> p (l s k c)")
            bm = vec("b_mod")
            with dve.Fori(0, 24) as i:
                for j in range(4):
                    dve.wait_ge(full[j], r0 + 1 + i)
                    nc.vector.tensor_tensor(modf[:, bass.ds(8 * i + 2 * j, 2)], bank[j][:, 0:2], bm[:, bass.ds(8 * i + 2 * j, 2)],
                                            ALU.add).then_inc(free[j], 1)
            dve.drain()
            for l in range(2):
                for w, g in ((0, "norm_mix"), (1, "norm_ffn")):
                    for st in range(2):
                        nc.vector.scalar_tensor_tensor(amod[:, l, w, st, :], mod[:, l, 3 * w + 1, :, st], 1.0,
                                                       vec(g)[:, l * KT:(l + 1) * KT], ALU.add, ALU.mult)
            phase.end()
            ffn(1, "ffn1_pre_g", half_g[:, 0, :])

            pre_norm(vec("mix_pre_g"), u1)
            lm = vec("lru_lambda")
            nc.vector.tensor_scalar(lam8[:, 2, :], lm, -1.0, 0.0, ALU.mult, ALU.max)
            nc.vector.tensor_scalar(lam8[:, 3, :], lm, -1.0, None, ALU.mult)
            dve.drain()
            nc.vector.tensor_tensor(lam8[:, 3, :], lam8[:, 3, :], lm, ALU.min)
            dve.drain().then_inc(cond_ready, 1)
            dve.wait_ge(cond_ready, 3)
            nc.vector.tensor_scalar(lam8[:, 5, :], lam8[:, 4, :], 2.0, None, ALU.add)
            dve.drain()
            nc.vector.reciprocal(lam8[:, 5, :], lam8[:, 5, :])
            dve.drain()
            nc.vector.tensor_tensor(lam8[:, 4, :], lam8[:, 4, :], lam8[:, 5, :], ALU.mult)
            dve.drain()
            nc.vector.tensor_tensor(lam8[:, 5, :], lam8[:, 4, :], lam8[:, 4, :], ALU.mult)
            nc.vector.memset(lam8[:, 6, :], 1.0 / 17)
            dve.drain()
            for odd in range(15, 0, -2):
                nc.vector.tensor_tensor(lam8[:, 6, :], lam8[:, 6, :], lam8[:, 5, :], ALU.mult)
                dve.drain()
                nc.vector.tensor_scalar(lam8[:, 6, :], lam8[:, 6, :], 1.0 / odd, None, ALU.add)
                dve.drain()
            nc.vector.tensor_tensor(lam8[:, 6, :], lam8[:, 6, :], lam8[:, 4, :], ALU.mult)
            dve.drain()
            nc.vector.scalar_tensor_tensor(lam8[:, 6, :], lam8[:, 6, :], 2.0, lam8[:, 2, :], ALU.mult, ALU.add)
            dve.drain()
            nc.vector.tensor_scalar(lam8[:, 0, :], lam8[:, 6, :], LRU_C, None, ALU.mult)
            nc.vector.tensor_scalar(lam8[:, 1, :], lam8[:, 6, :], -LRU_C, None, ALU.mult)
            nc.vector.memset(xbr[:, :, 0:CONV1 - 1], 0.0)
            dve.drain()
            dve.wait_ge(xbr_ready, 1)
            cw, cb = vec("conv_w"), vec("conv_b")
            for t in range(KT):
                nc.vector.tensor_scalar(xc[:, t, :], xbr[:, t, 0:S], cw[:, t:t + 1], cb[:, t:t + 1], ALU.mult, ALU.add)
                for k in range(1, CONV1):
                    dve.drain()
                    x = nc.vector.scalar_tensor_tensor(xc[:, t, :], xbr[:, t, k:k + S], cw[:, KT * k + t:KT * k + t + 1], xc[:, t, :],
                                                       ALU.mult, ALU.add)
                x.then_inc(xc_ready, 1)
            for t in range(KT):
                dve.wait_ge(decay_ready, t + 1)
                nc.vector.tensor_scalar(tmp[:, 0, :], gr[:, t, :], 1.0, None, ALU.add)
                nc.vector.tensor_tensor(gi[:, t, :], gi[:, t, :], xc[:, t, :], ALU.mult)
                dve.drain()
                nc.vector.reciprocal(tmp[:, 0, :], tmp[:, 0, :])
                dve.drain()
                nc.vector.scalar_tensor_tensor(gr[:, t, :], gr[:, t, :], 2.0, tmp[:, 0, :], ALU.mult, ALU.mult).then_inc(msq_ready, 1)
                dve.drain()
            rope([qt1[:, x, :] for x in range(KT)] + [kt1[:, x, :] for x in range(2)], const("cos1"), const("sin1"), 0)
            dve.wait_ge(gate_ready, 1)
            for t in range(KT):
                dve.wait_ge(mult_ready, t + 1)
                nc.vector.tensor_tensor(gi[:, t, :], gi[:, t, :], gr[:, t, :], ALU.mult)
                dve.drain()
                nc.vector.tensor_tensor_scan(xc[:, t, :], xbr[:, t, 0:S], gi[:, t, :], 0.0, ALU.mult, ALU.add)
                dve.drain()
                nc.vector.tensor_tensor(xc[:, t, :], xc[:, t, :], f[:, t, :], ALU.mult)
            phase.end()
            attend(False, 0, *att_views(o), vec("sinks1"), const("mask1"))
            phase.end()
            r0 = plan["merge"][0]
            with dve.Fori(0, 8) as i:
                for n in range(2):
                    dve.wait_ge(full[2 * n + 1], r0 + 1 + i)
                    dve.wait_ge(free[2 * n], r0 + 1 + i)
                    nc.vector.tensor_tensor(tmp[:, 2 + n, :], tmp[:, n, :], bank[2 * n + 1][:, :], ALU.mult).then_inc(free[2 * n + 1], 1)
                dve.drain()
                nc.vector.tensor_tensor(merged[:, bass.ds(i, 1), :].rearrange("p a t -> p (a t)"), tmp[:, 2, :], tmp[:, 3, :],
                                        ALU.add)
                dve.drain().then_inc(mrg_ready, 1)
            post_norm(vec("mix_post_g"))
            phase.end()
            ffn(2, "ffn2_pre_g", half_g[:, 1, :])

            mod_norm(0, 0, True)
            phase.end()
            w2 = vec("conv_w2")
            for t in range(4):
                bt, ct, ht, yc = pt[:, 4 + t, :], pt[:, 8 + t, :], pt[:, 12 + t, :], yt[:, 4 + t, :]
                nc.vector.tensor_tensor(ct, ct, ht, ALU.mult)
                dve.drain()
                nc.vector.tensor_scalar(yc, ct, w2[:, 4 + t:5 + t], None, ALU.mult)
                dve.drain()
                for a, n in ((0, S), (S, C)):
                    nc.vector.scalar_tensor_tensor(yc[:, a + 1:a + n], ct[:, a:a + n - 1], w2[:, t:t + 1], yc[:, a + 1:a + n], ALU.mult, ALU.add)
                dve.drain()
                for a, n in ((0, S), (S, C)):
                    nc.vector.scalar_tensor_tensor(yc[:, a:a + n - 1], ct[:, a + 1:a + n], w2[:, 8 + t:9 + t], yc[:, a:a + n - 1], ALU.mult, ALU.add)
                dve.drain()
                nc.vector.tensor_tensor(yc, yc, bt, ALU.mult)
            phase.end()

            def gated_add(name, l, its, context):
                r0 = plan[name][0]
                g1 = mod[:, l, 2, :, :].rearrange("p k c -> p (k c)")
                with dve.Fori(0, its) as i:
                    for j in range(4):
                        dve.wait_ge(full[j], r0 + 1 + i)
                        if context:
                            k, st = 2 * i + j // 2, j % 2
                        else:
                            k, st = 4 * i + j, 0
                        x, n = (lat, S) if st == 0 else (cxt, C)
                        xv = x[:, bass.ds(k, 1), :].rearrange("p a t -> p (a t)")
                        nc.vector.tensor_copy(small[:, 40 + j:41 + j], g1[:, bass.ds(2 * k + st, 1)])
                        dve.drain()
                        nc.vector.scalar_tensor_tensor(xv, bank[j][:, 0:n], small[:, 40 + j:41 + j], xv, ALU.mult,
                                                       ALU.add).then_inc(free[j], 1)

            gated_add("even_out", 0, 4, True)
            phase.end()
            mod_norm(0, 1, True)
            moe_layer(0)

            mod_norm(1, 0, True)
            heads = [qt2[:, x, :] for x in range(KT)] + [kt2[:, x, a:b] for x in range(2) for a, b in ((0, S), (S, SC))]
            for x, a in enumerate(heads):
                n = a.shape[1]
                dve.wait_ge(qstd_ready, x + 1)
                nc.vector.reciprocal(tmp[:, 2 + x % 2, 0:n], tmp[:, 2 + x % 2, 0:n])
                dve.drain()
                nc.vector.scalar_tensor_tensor(a, a, vec("q_g") if x < KT else vec("k_g"), tmp[:, 2 + x % 2, 0:n], ALU.mult,
                                               ALU.mult).then_inc(qn_ready, 1)
            dve.drain()
            rope([qt2[:, x, :] for x in range(KT)] + [kt2[:, x, 0:S] for x in range(2)], const("cos2"), const("sin2"), 10)
            phase.end()
            attend(True, 8, *att_views(att2), vec("sinks2"), const("mask2"))
            phase.end()
            gated_add("wo", 1, 2, False)
            phase.end()
            mod_norm(1, 1, False)
            moe_layer(1)
            dve.drain().then_inc(lat_final, 1)

        @block.gpsimd
        def _(pool):
            phase = Phase(pool)

            def attend(i0, qt, qs):
                for kv in range(2):
                    with pool.Fori(0, 4) as i:
                        for n in range(LT):
                            pool.wait_ge(s_full, 4 * (i0 + 4 * kv) + n + 1 + i * 4)
                            nc.gpsimd.tensor_copy(qs[:, n * P:(n + 1) * P],
                                                  qt[:, bass.ds(4 * kv + i, 1), n * P:(n + 1) * P].rearrange("p a t -> p (a t)")
                                                  ).then_inc(q_staged, 1)

            def moe_layer(l):
                q, nt = moe[l], TILES_OF[l]
                table = d["table"][l]
                nc.gpsimd.memset(tab_u[:, :], 0)
                nc.gpsimd.iota(tok_u[:, :], pattern=[[P, TT]], base=0, channel_multiplier=1)
                pool.drain()
                pool.dma_start(table.rearrange("(p n) o -> p (n o)", n=TABW), tab_u[:, :]).then_inc(q["zeros"], 16)
                for t in range(nt):
                    pool.wait_ge(q["xt_cp"], 2 * (t + 1))
                    pool.dma_start(d["rows"][l][t * P:(t + 1) * P, :], xg).then_inc(q["xt_out"], 16)
                pool.wait_ge(q["zeros"], 16)
                pool.wait_ge(q["pos"], 1)
                for t in range(nt):
                    for x in range(2):
                        pool.indirect_dma_start(out=table, out_offset=bass.IndirectOffsetOnAxis(ap=pos_u[:, 1, x, t:t + 1], axis=0),
                                                in_=tok_u[:, t:t + 1], in_offset=None).then_inc(q["scatter"], 16)
                pool.wait_ge(q["scatter"], 32 * nt)
                pool.dma_start(tab_u[:, :], table.rearrange("(p n) o -> p (n o)", n=TABW)).then_inc(q["table"], 16)
                pool.wait_ge(q["table"], 16)
                pool.wait_ge(yb_zeroed, 32)
                pool.wait_ge(q["xt_out"], 16 * nt)

                def gather(b, first=False):
                    if not first:
                        pool.wait_ge(q["xt_full"], b)
                    nc.gpsimd.tensor_copy(idx_u[:, :], tab_u[:, bass.ds(b, 1)])
                    pool.drain()
                    pool.indirect_dma_start(out=xg, out_offset=None, in_=d["rows"][l],
                                            in_offset=bass.IndirectOffsetOnAxis(ap=idx_u[:, :], axis=0)).then_inc(q["gathered"], 16)

                def write_y(b, written="y_written"):
                    pool.wait_ge(q["y_ready"], 2 * (b + 1))
                    pool.dma_start(d["yb"][l][bass.ds(b * MB, MB), :], ysb).then_inc(q[written], 16)

                phase.end()
                last = pool.value_load(exp_i[0:1, TABW:TABW + 1], min_val=2, max_val=NBMAX - 1)
                gather(0, first=True)
                gather(1)
                gather(2)
                write_y(0)
                with pool.Fori(2, last + 1) as b:
                    gather(b + 1)
                    write_y(b - 1)
                write_y(last, "y_last")
                pool.wait_ge(q["y_last"], 16)
                phase.end()
                for t in range(nt):
                    if t > 0:
                        pool.wait_ge(q["sum_ready"], t)
                    for x in range(2):
                        pool.indirect_dma_start(out=yget[x], out_offset=None, in_=d["yb"][l],
                                                in_offset=bass.IndirectOffsetOnAxis(ap=pos_u[:, 0, x, t:t + 1], axis=0)
                                                ).then_inc(q["got"], 16)
                phase.end()

            phase.end()
            nc.gpsimd.memset(zeros[:, :], 0.0)
            pool.drain()
            per = NBMAX * MB // P * (D // ZERO)
            for l in range(2):
                pool.dma_start(d["yb"][l].rearrange("(p n) (h c) -> p (n h) c", p=P, c=ZERO),
                               zeros[:, :].unsqueeze(1).to_broadcast([P, per, ZERO])).then_inc(yb_zeroed, 16)
            phase.end()
            phase.end()
            attend(0, qt1, att_views(o)[0])
            phase.end()
            for x in range(5):
                phase.end()
            moe_layer(0)
            phase.end()
            attend(8, qt2, att_views(att2)[0])
            phase.end()
            phase.end()
            moe_layer(1)


def tiles(w):
    n = w.shape[1] // P
    t = w.reshape(KT, P, n, P).transpose(2, 1, 0, 3).reshape(n // 2, 2, P, KT * P)
    return t.transpose(0, 2, 1, 3).reshape(n // 2, P, CHUNK)


def mixed(*ws):
    n = ws[0].shape[1] // P
    return tiles(np.stack([w.reshape(D, n, P) for w in ws], 2).reshape(D, -1))


def moving(w):
    return w.reshape(KT, P, C).transpose(1, 0, 2).reshape(1, P, CHUNK)


def columns(v):
    return np.ascontiguousarray(v).reshape(-1, P).T


def fields(named, spec):
    return np.ascontiguousarray(np.concatenate([named[n].reshape(P, w) for n, w in spec], 1))


def rope_table(pos, freqs):
    ang = pos.astype(np.float32)[:, None] * freqs.astype(np.float32)[None, :]
    return np.cos(ang), np.sin(ang)


def constants():
    p = np.arange(P)
    out = {"ident": np.eye(P), "ones": np.ones((P, P)), "headsum": p[:, None] // HD == p[None, :] // HD,
           "swap1": p[:, None] == (p ^ (HD // 2))[None, :], "swap2": p[:, None] == (p ^ (HD // 4))[None, :],
           "before": p[:, None] < p[None, :]}
    i, s1, s2 = p[:, None], np.arange(2 * P)[None, :], np.arange(3 * P)[None, :]
    out["mask1"] = np.where((P + i - s1 >= 0) & (P + i - s1 < P), 0.0, NEG)
    out["mask2"] = np.where(np.abs(s2 - P - i) <= P, 0.0, NEG)
    half = HD // 2
    c, s = rope_table(np.arange(S), np.float32(10000.0) ** (-np.arange(half, dtype=np.float32) / half))
    out["cos1"], out["sin1"] = c.T[p % half], s.T[p % half] * np.where(p % HD < half, -1.0, 1.0)[:, None]
    n = HD // 4
    freqs = np.float32(10000.0) ** (-np.arange(n, dtype=np.float32) / n)
    t = np.arange(S)
    by_axis = [rope_table(pos, freqs) for pos in (t // 64, t % 64)]
    axis = (p % HD) // half
    out["cos2"] = np.stack([by_axis[a][0][:, x % n] for a, x in zip(axis, p)])
    out["sin2"] = np.stack([by_axis[a][1][:, x % n] * (-1.0 if x % half < n else 1.0) for a, x in zip(axis, p)])
    out["eps"] = np.full((P, 1), EPS)
    out["gdesc"] = np.tile(np.arange(NG, 0, -1), (P, 1))
    out["edesc"] = np.tile(np.arange(NE, 0, -1), (P, 1))
    e = np.arange(NE)
    out["tri_lt"], out["tri_le"] = np.tile(e[:, None] < e, (P // NE, 1)), np.tile(e[:, None] <= e, (P // NE, 1))
    out["blocks"] = np.tile(np.arange(TABW), (P, 1))
    out["thr"] = np.tile(MB * np.arange(16), (P, 1))
    return fields({k: np.asarray(v, np.float32) for k, v in out.items()}, CONSTS)


def fourier():
    def pair(n):
        ang = 2 * np.pi * ((np.arange(n)[:, None] * np.arange(n)[None, :]) % n) / n
        return np.cos(ang) / np.sqrt(n), np.sin(ang) / np.sqrt(n)

    def rows(m):
        return m.reshape(-1, P, m.shape[1]).transpose(1, 0, 2).reshape(P, -1)

    (cd, sd), (cc, sc), (cl, sl) = pair(P), pair(C), pair(S)
    out = {"cs_d": np.concatenate([cd, sd], 1), "c_ctx": rows(cc), "s_ctx": rows(-sc), "c_lat": rows(cl), "s_lat": rows(-sl)}
    return fields({k: v.astype(np.float32) for k, v in out.items()}, DFT)


def kernel(**inputs):
    import concourse.bacc as bacc
    from concourse.bass_utils import run_bass_kernel_spmd

    x = {k: np.asarray(v) for k, v in inputs.items()}
    order = np.concatenate([np.arange(h * HD, (h + 1) * HD) for h in HEADS])
    w_in, w_in2, qkv = x["w_in"][0], x["w_in_even_2"][0], x["w_qkv_2"][0]
    a = 2 * D + D
    kvw = NH // 4 * HD
    gate, xb, wq = w_in[:, 0:D], w_in[:, D:2 * D], w_in[:, 2 * D:a][:, order]
    wk, wv, g_lru, g_att = w_in[:, a:a + kvw], w_in[:, a + kvw:a + 2 * kvw], w_in[:, a + 2 * kvw:a + 2 * kvw + D], w_in[:, a + 2 * kvw + D:]

    def ffn(n):
        gu = x[f"ffn{n}_w_gu"][0]
        g, u = (t.reshape(D, FF // 256, 256) for t in (gu[:, :FF], gu[:, FF:]))
        return tiles(np.stack([g, u], 2).reshape(D, 2 * FF))

    def down(n):
        return x[f"ffn{n}_w_down"][0].reshape(FT, P, KT, P).transpose(2, 1, 0, 3).reshape(KT, P, SLOT)

    w = np.concatenate([tiles(x["w_mod_2"][0]), tiles(x["w_mod_2"][1]), ffn(1), tiles(xb), tiles(wq), tiles(wk), moving(wv), tiles(gate),
                        mixed(g_lru, x["w_proj_lru"][0], g_att, x["w_proj_attn"][0][order]), tiles(x["w_out"][0]), ffn(2),
                        tiles(w_in2), tiles(x["w_out_even_2"][0]), tiles(qkv[:, 0:D][:, order]), tiles(qkv[:, D:D + kvw]),
                        moving(qkv[:, D + kvw:]), tiles(x["w_o_2"][0][order])])
    lru_w = np.zeros((2, KT, 2, HD, 2, HD), np.float32)
    for g, n in enumerate(("lru_w_a", "lru_w_x")):
        for h in range(2):
            lru_w[g, :, h, :, h, :] = x[n][0].reshape(KT, 2, HD, HD)[:, h]
    route_w = np.concatenate([x["w_router_g_2"], x["w_router_e_2"]], 2)
    route_b = np.concatenate([x["b_router_g_2"], x["b_router_e_2"]], 1)
    named = {n: columns(x[n][0]) for n in ("ffn1_pre_g", "ffn1_post_g", "mix_pre_g", "mix_post_g", "ffn2_pre_g", "ffn2_post_g",
                                           "conv_w", "conv_b", "lru_b_a", "lru_b_x", "lru_lambda")}
    named |= {"norm_mix": columns(x["norm_mix_g_2"]), "norm_ffn": columns(x["norm_ffn_g_2"]), "conv_w2": columns(x["conv_w_2"][0]),
              "q_g": np.tile(x["q_norm_g_2"][0], 2)[:, None], "k_g": np.tile(x["k_norm_g_2"][0], 2)[:, None],
              "cond": np.stack([columns(x["c_2"][0]), columns(x["c_ctx_2"])], 2),
              "b_mod": np.repeat(columns(x["b_mod_2"])[:, :, None], 2, 2),
              "sinks1": np.tile(x["attn_sinks"][0][HEADS], (P, 1)), "sinks2": np.tile(x["sink_logit_2"][0][HEADS], (P, 1)),
              "route_b": np.tile(route_b[None, :, None, :], (P, 1, TT, 1))}
    arrays = {"consts": constants(), "dft": fourier(), "vecs": fields(named, VECS),
              "x": x["x"][0].T.reshape(KT, P, S).transpose(1, 0, 2), "ctx": x["ctx_2"][0].T.reshape(KT, P, C).transpose(1, 0, 2),
              "w": w, "wd": np.concatenate([down(1), down(2)]),
              "lru_w": lru_w.reshape(2, KT, P, P).transpose(2, 0, 1, 3),
              "wr": route_w.reshape(2, KT, P, ROUTE).transpose(0, 2, 1, 3), "w1": x["w1_2"], "w3": x["w3_2"], "w2": x["w2_2"]}
    arrays = {f"in_{n}": np.ascontiguousarray(v) for n, v in arrays.items()}
    nc = bacc.Bacc("TRN2", target_bir_lowering=False, num_devices=1)
    d = {n[3:]: nc.dram_tensor(n, v.shape, F32, kind="ExternalInput").ap() for n, v in arrays.items()}
    d["out"] = nc.dram_tensor("out", (P, KT, S), F32, kind="ExternalOutput").ap()
    d["rows"] = [nc.dram_tensor(f"rows{l}", (t, D), F32, kind="Internal").ap() for l, t in enumerate((SC, S))]
    d["yb"] = [nc.dram_tensor(f"yb{l}", (NBMAX * MB, D), F32, kind="Internal").ap() for l in range(2)]
    d["table"] = [nc.dram_tensor(f"table{l}", (MB * TABW, 1), U32, kind="Internal").ap() for l in range(2)]
    program(nc, d)
    r = run_bass_kernel_spmd(nc, [arrays], core_ids=[0])
    out = np.asarray(r.results[0]["out"])
    return np.ascontiguousarray(out.transpose(2, 1, 0).reshape(1, S, D))
```

```python
from contextlib import ExitStack

import numpy as np

import concourse.bass as bass
from concourse import mybir

F32 = mybir.dt.float32
I32 = mybir.dt.int32
U32 = mybir.dt.uint32
ACT = mybir.ActivationFunctionType
ALU = mybir.AluOpType
AX = mybir.AxisListType

P = 128
D = 1024
KT = D // P
S = 512
C = 256
SC = S + C
FF = 2816
FT = FF // P
HD = 64
NH = 16
PAIRS = NH // 2
EPS = 1e-6
NE = 32
NG = 4
EF = 512
MB = 64
NBMAX = -(-2 * SC // MB) + NE
TABW = NBMAX + 1
CONV1 = 4
LRU_C = 8.0
SLOT = FT * P
CHUNK = 2 * KT * P
ROUTE = NG + NE
TT = SC // P
LT = S // P
ZERO = 512
XPAD = S + CONV1 - 1
SCALE = HD ** -0.5
NEG = -1e30

HEADS = [8 * (j // 4) + j % 4 + 4 * s for j in range(PAIRS) for s in range(2)]

MOD_GU, MOD_DOWN = 22, 2
DENSE = [("gu1", 22, 11), ("down1", 8, 2), ("xbr", 4, 2), ("q1", 4, 2), ("kv1", 2, 1),
         ("gate", 4, 2), ("merge", 16, 8), ("out1", 4, 2), ("gu2", 22, 11), ("down2", 8, 2),
         ("even_in", 8, 8), ("even_out", 4, 4), ("q2", 4, 2), ("kv2", 2, 2), ("wo", 4, 2)]


def dense_plan():
    rounds, loads, plan, at = 1, 0, {}, {"w": 0, "d": 0}
    for name, chunks, n in DENSE:
        kind = "d" if name.startswith("down") else "w"
        plan[name] = (rounds, loads, at[kind])
        rounds, loads = rounds + n, loads + chunks // 2
        at[kind] += chunks
    return plan


VECS = [("ffn1_pre_g", 8), ("ffn1_post_g", 8), ("mix_pre_g", 8), ("mix_post_g", 8), ("ffn2_pre_g", 8),
        ("ffn2_post_g", 8), ("conv_w", 32), ("conv_b", 8), ("lru_b_a", 8), ("lru_b_x", 8), ("lru_lambda", 8),
        ("norm_mix", 16), ("norm_ffn", 16), ("conv_w2", 12), ("q_g", 1), ("k_g", 1), ("cond", 16), ("b_mod", 192),
        ("sinks1", 16), ("sinks2", 16), ("route_b", 2 * TT * ROUTE)]
CONSTS = [("ident", 128), ("ones", 128), ("swap1", 128), ("swap2", 128), ("headsum", 128), ("before", 128),
          ("mask1", 256), ("mask2", 384), ("cos1", S), ("sin1", S), ("cos2", S), ("sin2", S),
          ("eps", 1), ("gdesc", NG), ("edesc", NE), ("tri_lt", NE), ("tri_le", NE), ("blocks", TABW), ("thr", 16)]
DFT = [("cs_d", 2 * P), ("c_ctx", 2 * C), ("s_ctx", 2 * C), ("c_lat", 4 * S), ("s_lat", 4 * S)]


def offsets(fields):
    at, out = 0, {}
    for name, n in fields:
        out[name] = (at, n)
        at += n
    return out, at


VEC_AT, VEC_N = offsets(VECS)
CONST_AT, CONST_N = offsets(CONSTS)
DFT_AT, DFT_N = offsets(DFT)


def program(nc, d):
    ctx = ExitStack()
    with ctx:
        def sb(name, shape, dt=F32):
            return ctx.enter_context(nc.sbuf_tensor(name, shape, dt))

        def sem(name):
            return ctx.enter_context(nc.semaphore(name))

        plan = dense_plan()

        lat = sb("lat", [P, KT, S])
        cxt = sb("cxt", [P, KT, C])
        vecs = sb("vecs", [P, VEC_N])
        consts = sb("consts", [P, CONST_N])
        mod = sb("mod", [P, 2, 6, KT, 2])
        amod = sb("amod", [P, 2, 2, 2, KT])
        slot = [sb(f"slot{s}", [P, SLOT]) for s in range(2)]
        half_g = sb("half_g", [P, 2, KT])
        lam8 = sb("lam8", [P, 8, KT])
        silu_c = sb("silu_c", [P, KT, 2])
        small = sb("small", [P, 96])

        ar_u = sb("ar_u", [P, KT * SC])
        ar_f = sb("ar_f", [P, KT * S])
        rs = sb("rs", [P, SC])
        tmp = sb("tmp", [P, 4, S])
        BIG = 22560
        big = sb("big", [P, BIG])

        def vec(name):
            a, n = VEC_AT[name]
            return vecs[:, a:a + n]

        def const(name):
            a, n = CONST_AT[name]
            return consts[:, a:a + n]

        def part(at, shape):
            n = int(np.prod(shape))
            assert at + n <= BIG, (at, shape)
            v = big[:, at:at + n]
            names = "abcd"[:len(shape)]
            return v.rearrange(f"p ({' '.join(names)}) -> p {' '.join(names)}",
                               **{c: x for c, x in zip(names, shape)}) if len(shape) > 1 else v

        ident, ones = const("ident"), const("ones")
        u1 = ar_u[:, 0:KT * S].rearrange("p (k t) -> p k t", k=KT)
        u2 = ar_u[:, :].rearrange("p (k t) -> p k t", k=KT)
        f = ar_f[:, :].rearrange("p (k t) -> p k t", k=KT)
        act_t = part(0, [FT, S])
        mslot = part(20000, [CHUNK])
        xbr = part(0, [KT, XPAD])
        xc = part(KT * XPAD, [KT, S])
        o = KT * (XPAD + S)
        gr = part(o, [KT, S])
        gi = part(o + KT * S, [KT, S])
        qt1 = part(o + 2 * KT * S, [KT, S])
        kt1 = part(o + 3 * KT * S, [2, S])
        v1 = part(o + 3 * KT * S + 2 * S, [LT, C])
        lru_w = ar_u[:, KT * S:KT * S + 2 * KT * P].rearrange("p (g k c) -> p g k c", g=2, k=KT)
        merged = gr
        qt2 = part(0, [KT, S])
        kt2 = part(KT * S, [2, SC])
        v2 = part(KT * S + 2 * SC, [TT, C])
        att2 = KT * S + 2 * SC + TT * C

        def att_views(at, keys):
            n = 2 * S
            return (part(at, [2, S]), part(at + n, [4, 2, keys]), part(at + n + 8 * keys, [2, 2 * keys]),
                    part(at + n + 12 * keys, [2, P]))

        pt = part(0, [16, SC])
        yt = part(16 * SC, [8, SC])
        ac = part(24 * SC, [TT, 2 * P])
        dft = part(24 * SC + TT * 2 * P, [DFT_AT["c_lat"][0]])
        csd = dft[:, 0:2 * P]
        c_ctx = dft[:, 2 * P:2 * P + 2 * C].rearrange("p (l t) -> p l t", l=2)
        s_ctx = dft[:, 2 * P + 2 * C:2 * P + 4 * C].rearrange("p (l t) -> p l t", l=2)
        c_lat = ar_f[:, 0:4 * S].rearrange("p (l t) -> p l t", l=4)
        s_lat = tmp[:, :, :]
        wslot = [part(2048 * c, [2048]) for c in range(6)]
        m0 = 6 * 2048
        xg = part(m0, [D])
        xT = part(m0 + D, [KT, MB])
        hsil = part(m0 + 2 * D, [EF])
        hmul = part(m0 + 2 * D + EF, [EF])
        hT = part(m0 + 3 * D, [EF // P, MB])
        ysb = part(m0 + 3 * D + EF, [EF])
        yget = [part(m0 + 4 * D + EF + n * D, [D]) for n in range(2)]
        fsum = part(m0 + 6 * D + EF, [D])
        rt = m0 + 7 * D + EF
        lg = part(rt, [TT, ROUTE])
        ge = part(rt + 216, [TT, NG])
        gsel = part(rt + 240, [TT, NG])
        ecand = part(rt + 264, [TT, NE])
        elog = part(rt + 456, [TT, NE])
        oh = [part(rt + 648 + 192 * n, [TT, NE]) for n in range(2)]
        both = part(rt + 1032, [TT, NE])
        rank = part(rt + 1224, [TT, NE])
        over = part(rt + 1416, [TT, NE])
        wr = part(rt + 1608, [KT, ROUTE])
        scal = part(rt + 1896, [12, TT])
        nbb = part(rt + 1968, [P])
        cmpb = part(rt + 2096, [TABW + 1])
        col = part(rt + 2096 + TABW + 1, [8])
        pos_f = part(rt + 2200, [2, 2, TT])
        pos_u = sb("pos_u", [P, 2, 2, TT], U32)
        tok_u = sb("tok_u", [P, TT], U32)
        tab_u = sb("tab_u", [MB, TABW], U32)
        zeros = sb("zeros", [P, ZERO])
        idx_u = sb("idx_u", [MB, 1], U32)
        exp_i = sb("exp_i", [1, TABW + 1], I32)

        bank = [ctx.enter_context(nc.psum_tensor(f"bank{i}", [P, 512], F32)) for i in range(8)]

        loaded = sem("loaded")
        lru_loaded, dft_loaded, wr_loaded = sem("lru_loaded"), sem("dft_loaded"), sem("wr_loaded")
        wload = [sem(f"wload{s}") for s in range(2)]
        full = [sem(f"full{j}") for j in range(4)]
        free = [sem(f"free{j}") for j in range(4)]
        phase_done = sem("phase_done")
        mod_load, mod_full, mod_free = sem("mod_load"), sem("mod_full"), sem("mod_free")
        zeros_ready = sem("zeros_ready")
        sq_ready, ssum_ready, std_ready, u_ready = (sem(n) for n in ("sq_ready", "ssum_ready", "std_ready", "u_ready"))
        cond_ready, act_ready = sem("cond_ready"), sem("act_ready")
        xbr_ready, xc_ready, raw_ready = sem("xbr_ready"), sem("xc_ready"), sem("raw_ready")
        lin_full, lin_free = sem("lin_full"), sem("lin_free")
        gates_ready, decay_ready, msq_ready, mult_ready = (sem(n) for n in ("gates_ready", "decay_ready", "msq_ready", "mult_ready"))
        gate_ready = sem("gate_ready")
        rope_full, rope_free, rope_ready = sem("rope_full"), sem("rope_free"), sem("rope_ready")
        qsq_ready, qsum_full, qstd_ready, qn_ready = (sem(n) for n in ("qsq_ready", "qsum_full", "qstd_ready", "qn_ready"))
        q_staged, s_full, s_evac, max_ready = (sem(n) for n in ("q_staged", "s_full", "s_evac", "max_ready"))
        exp_ready, t_full, t_evac = (sem(n) for n in ("exp_ready", "t_full", "t_evac"))
        o_full, y_norm, turn_full, o_evac = (sem(n) for n in ("o_full", "y_norm", "turn_full", "o_evac"))
        ac_full, ac_ready, dft_full, dft_evac, conv_ready = (sem(n) for n in ("ac_full", "ac_ready", "dft_full", "dft_evac", "conv_ready"))
        mrg_ready = sem("mrg_ready")
        moe = [{n: sem(f"{n}_{l}") for n in
                ("xt_tr", "xt_cp", "xt_out", "logits", "gexp_in", "gexp", "eexp_in", "eexp", "onehot", "counts", "nblk",
                 "starts", "cmp", "exp_row", "expert", "pos", "zeros", "scatter", "table", "gathered", "xt_full", "xt_ready", "gate_full",
                 "up_full", "sg_ready", "h_ready", "htp_full", "ht_ready", "y_full", "y_ready", "y_written", "y_last", "got",
                 "sum_ready", "sum_tr", "sum_read", "w2_done")} for l in range(2)]
        mload = [[sem(f"mload{c}_{l}") for c in range(6)] for l in range(2)]
        mdone = [[sem(f"mdone{c}_{l}") for c in range(2)] for l in range(2)]
        yb_zeroed, lat_final, stored = sem("yb_zeroed"), sem("lat_final"), sem("stored")

        block = ctx.enter_context(nc.Block())
        TILES_OF = [TT, LT]

        class Phase:
            def __init__(self, eng):
                self.eng, self.n = eng, 0

            def end(self):
                self.n += 1
                self.eng.drain().then_inc(phase_done, 1)
                self.eng.wait_ge(phase_done, 4 * self.n)

        def att_tiles(second, n):
            lo, hi = max(n - 1, 0), (min(n + 1, LT - 1) if second else n)
            return lo, hi + 1, (lo - n + 1) * P

        def att_groups(second, n):
            lo, hi, _ = att_tiles(second, n)
            per = hi - lo + (2 if second else 0)
            return per, -(-2 * per // 4)

        UNITS = 2 * LT
        ROUNDS = PAIRS // 2

        def unit_at(i, x):
            return i + x // UNITS, x % UNITS

        def att_schedule(eng, order, last):
            def steps(i, first):
                for m in range(UNITS):
                    for delay, step in order:
                        if not (first and m < delay):
                            step(*unit_at(i, m - delay))
            steps(0, True)
            with eng.Fori(1, ROUNDS) as i:
                steps(i, False)
            for m in range(UNITS, UNITS + last):
                for delay, step in order:
                    if m - delay < UNITS:
                        step(*unit_at(ROUNDS - 1, m - delay))

        def groups_before(second, i, m):
            per_round = 2 * sum(att_groups(second, n)[1] for n in range(LT))
            at = 2 * ROUNDS * LT if second else 0
            return at + sum(att_groups(second, x % LT)[1] for x in range(m)) + per_round * i

        @block.sync
        def _(sp):
            for dst, src in ((consts[:, :], d["consts"]), (vecs[:, :], d["vecs"]), (lat[:, :, :], d["x"]),
                             (cxt[:, :, :], d["ctx"])):
                sp.dma_start(dst, src).then_inc(loaded, 16)

            def load_mod(n):
                sp.wait_ge(mod_full, n + 1)
                sp.dma_start(mslot, d["wm"][bass.ds(n, 1)].rearrange("a p n -> (a p) n")).then_inc(mod_load, 16)

            def stream(name, its, mod=None):
                r0, l0, c0 = plan[name]
                with sp.Fori(0, its) as i:
                    for s in range(2):
                        sp.wait_ge(full[2 * s + 1], r0 + i)
                        sp.dma_start(slot[s][:, 0:CHUNK],
                                     d["w"][bass.ds(c0 + 2 * i + s, 1)].rearrange("a p n -> (a p) n")).then_inc(wload[s], 16)
                        if mod is not None:
                            load_mod(mod + s + 2 * i)

            def stream_down(name, mod):
                r0, l0, c0 = plan[name]
                with sp.Fori(0, 2) as i:
                    for t in range(4):
                        s = t % 2
                        if t < 2:
                            sp.wait_ge(full[2 * s + 1], r0 + i)
                        else:
                            sp.wait_ge(full[2 * s], r0 + i + 1)
                        sp.dma_start(slot[s][:, :],
                                     d["wd"][bass.ds(c0 + 4 * i + t, 1)].rearrange("a p n -> (a p) n")).then_inc(wload[s], 16)
                        if t == 1:
                            load_mod(mod + i)

            def stream_paired(name, its):
                r0, l0, c0 = plan[name]
                with sp.Fori(0, its) as i:
                    for s in range(2):
                        if s == 0:
                            sp.wait_ge(full[1], r0)
                        sp.wait_ge(full[3], r0 + 2 * i - 1 + s)
                        sp.dma_start(slot[s][:, 0:CHUNK],
                                     d["w"][bass.ds(c0 + 2 * i + s, 1)].rearrange("a p n -> (a p) n")).then_inc(wload[s], 16)

            def stream_experts(l):
                q = moe[l]
                w1 = d["w1"].rearrange("l e (p h k) f -> (l e) h p k f", h=2, p=P)
                w3 = d["w3"].rearrange("l e (p h k) f -> (l e) h p k f", h=2, p=P)
                w2 = d["w2"].rearrange("l e (p h k) f -> (l e) h p k f", h=2, p=P)

                def load(c, w, e, half):
                    dst = wslot[c].rearrange("p (k f) -> p k f", k=4 if c < 4 else 2)
                    sp.dma_start(dst, w[bass.ds(e + l * NE, 1), half].rearrange("e p k f -> (e p) k f")).then_inc(mload[l][c], 16)

                def up(b, first=False):
                    e = sp.value_load(exp_i[0:1, bass.ds(b, 1)], min_val=0, max_val=NE - 1)
                    for c in (0, 2, 1, 3):
                        if not first:
                            sp.wait_ge([mdone[l][0], q["gate_full"], mdone[l][1], q["up_full"]][c], b)
                        load(c, w1 if c < 2 else w3, e, c % 2)

                def down(b, first=False):
                    e = sp.value_load(exp_i[0:1, bass.ds(b, 1)], min_val=0, max_val=NE - 1)
                    if not first:
                        sp.wait_ge(q["w2_done"], b)
                    for c in range(4, 6):
                        load(c, w2, e, c % 2)

                sp.wait_ge(q["expert"], 1)
                last = sp.value_load(exp_i[0:1, TABW:TABW + 1], min_val=2, max_val=NBMAX - 1)
                up(0, first=True)
                down(0, first=True)
                up(1)
                down(1)
                with sp.Fori(2, last + 1) as b:
                    up(b)
                    down(b)

            per = MOD_GU + MOD_DOWN
            stream("gu1", 11, 0)
            stream_down("down1", MOD_GU)
            stream("xbr", 2)
            stream("q1", 2)
            stream("kv1", 1)
            stream("gate", 2)
            sp.wait_ge(zeros_ready, 1)
            runs = NBMAX * MB // P * (D // ZERO)
            for l in range(2):
                sp.dma_start(d["yb"][l].rearrange("(p n) (h c) -> p (n h) c", p=P, c=ZERO),
                             zeros[:, :].unsqueeze(1).to_broadcast([P, runs, ZERO])).then_inc(yb_zeroed, 16)
            stream("merge", 8)
            stream("out1", 2)
            sp.wait_ge(phase_done, 12)
            stream("gu2", 11, per)
            stream_down("down2", per + MOD_GU)
            stream_paired("even_in", 4)
            stream_paired("even_out", 2)
            stream_experts(0)
            stream("q2", 2)
            stream_paired("kv2", 1)
            stream("wo", 2)
            stream_experts(1)
            sp.wait_ge(lat_final, 1)
            sp.dma_start(d["out"], lat[:, :, :]).then_inc(stored, 16)
            sp.wait_ge(stored, 16)

        @block.tensor
        def _(pe):
            phase = Phase(pe)
            norms = [0]

            def modulate(n):
                pe.wait_ge(mod_load, 16 + n * 16)
                pe.wait_ge(mod_free, n + 1)
                for t in range(2):
                    for k in range(KT):
                        mm = nc.tensor.matmul(bank[5][:, 2 * t:2 * t + 2], mslot[:, (t * KT + k) * P:(t * KT + k + 1) * P], silu_c[:, k, :],
                                              start=(k == 0), stop=(k == KT - 1))
                mm.then_inc(mod_full, 1)

            def dense(name, its, rhs, mod=None):
                r0, l0, _ = plan[name]
                with pe.Fori(0, its) as i:
                    for j in range(4):
                        s = j // 2
                        if j % 2 == 0:
                            pe.wait_ge(wload[s], 16 * l0 + 16 + i * 16)
                        pe.wait_ge(free[j], r0 + i)
                        for k in range(KT):
                            w = slot[s][:, (j % 2) * KT * P + k * P:(j % 2) * KT * P + (k + 1) * P]
                            m = rhs(j, k)
                            mm = nc.tensor.matmul(bank[j][:, 0:m.shape[1]], w, m, start=(k == 0), stop=(k == KT - 1))
                        mm.then_inc(full[j], 1)
                        if mod is not None and j % 2:
                            modulate(mod + s + 2 * i)

            def down(name, mod):
                r0, l0, _ = plan[name]
                with pe.Fori(0, 2) as i:
                    for t in range(4):
                        s, j = t % 2, (0, 2, 1, 3)[t]
                        pe.wait_ge(wload[s], 16 * l0 + 16 + 16 * (t // 2) + i * 32)
                        pe.wait_ge(free[j], r0 + i)
                        for k in range(FT):
                            mm = nc.tensor.matmul(bank[j][:, :], slot[s][:, k * P:(k + 1) * P], act_t[:, k, :],
                                                  start=(k == 0), stop=(k == FT - 1))
                        mm.then_inc(full[j], 1)
                        if t == 1:
                            modulate(mod + i)

            def paired(name, its, rhs, first=0):
                r0, l0, _ = plan[name]
                with pe.Fori(0, its) as i:
                    for s in range(2):
                        pe.wait_ge(wload[s], 16 * l0 + 16 + i * 16)
                        for j in range(4):
                            pe.wait_ge(free[j], r0 + s + i * 2)
                            a, n = ((0, S), (S, C))[j % 2]
                            for k in range(KT):
                                w = slot[s][:, (j // 2) * KT * P + k * P:(j // 2) * KT * P + (k + 1) * P]
                                mm = nc.tensor.matmul(bank[j][:, 0:n], w, rhs[:, k, a:a + n],
                                                      start=(k == 0), stop=(k == KT - 1))
                            mm.then_inc(full[j], 1)

            def norm_sum(u, context=False):
                n = norms[0]
                norms[0] += 1
                for k in range(KT):
                    pe.wait_ge(sq_ready, KT * n + k + 1)
                    mm = nc.tensor.matmul(bank[4][:, :], ones, u[:, k, 0:S], start=(k == 0), stop=(k == KT - 1))
                    if context:
                        mm = nc.tensor.matmul(bank[5][:, 0:C], ones, u[:, k, S:SC], start=(k == 0), stop=(k == KT - 1))
                mm.then_inc(ssum_ready, 1)

            def normed(n):
                pe.wait_ge(u_ready, KT * n)

            def ffn(n, n_norm):
                norm_sum(u1)
                normed(n_norm)
                mod = (n - 1) * (MOD_GU + MOD_DOWN)
                dense(f"gu{n}", 11, lambda j, k: u1[:, k, :], mod)
                pe.wait_ge(act_ready, n)
                down(f"down{n}", mod + MOD_GU)
                norm_sum(u1)
                phase.end()

            def attend(second, u0, qs, sm, pT, yo, kt, v):
                def scores(i, m):
                    n, kv = m % LT, m // LT
                    lo, hi, _ = att_tiles(second, n)
                    at = 0 if second else 2 * (m % 2)
                    pe.wait_ge(q_staged, u0 + m + 1 + 8 * i)
                    pe.wait_ge(s_evac, u0 + m + (2 if second else 1) + 8 * i)
                    for s in range(2):
                        h = slice(64 * s, 64 * s + 64)
                        mm = nc.tensor.matmul(bank[at + s][:, 0:(hi - lo) * P], qs[h, kv, n * P:(n + 1) * P],
                                              kt[h, kv, lo * P:hi * P], start=True, stop=True)
                    if second:
                        for s in range(2):
                            h = slice(64 * s, 64 * s + 64)
                            mm = nc.tensor.matmul(bank[2 + s][:, 0:C], qs[h, kv, n * P:(n + 1) * P], kt[h, kv, S:SC],
                                                  start=True, stop=True)
                    mm.then_inc(s_full, 1)

                def spread(i, m, late=False):
                    per, groups = att_groups(second, m % LT)
                    if not late:
                        pe.wait_ge(exp_ready, u0 + m + 1 + 8 * i)
                    for g in range(2, groups) if late else range(min(groups, 2)):
                        at = groups_before(second, 0, m) + g
                        pe.wait_ge(t_evac, groups_before(second, i, m) + g + 1)
                        for x in range(4 * g, min(4 * g + 4, 2 * per)):
                            tr = nc.tensor.transpose(bank[4 + at % 2][:, (x % 4) * P:(x % 4 + 1) * P],
                                                     sm[:, m % 4, x // per, (x % per) * P:(x % per + 1) * P], ident)
                        tr.then_inc(t_full, 1)

                def values(i, m):
                    n, kv = m % LT, m // LT
                    lo, hi, _ = att_tiles(second, n)
                    per, groups = att_groups(second, n)
                    spread(i, m, late=True)
                    pe.wait_ge(t_evac, groups_before(second, i, m) + groups + 2)
                    pe.wait_ge(y_norm, u0 + m + 1 + 8 * i)
                    for s in range(2):
                        for x in range(per):
                            tile = lo + x if x < hi - lo else LT + x - (hi - lo)
                            mm = nc.tensor.matmul(bank[6 + m % 2][:, s * HD:(s + 1) * HD],
                                                  pT[:, m % 2, (s * per + x) * P:(s * per + x + 1) * P],
                                                  v[:, tile, (2 * kv + s) * HD:(2 * kv + s + 1) * HD],
                                                  start=(x == 0), stop=(x == per - 1))
                    mm.then_inc(o_full, 1)

                def turn(i, m):
                    pe.wait_ge(y_norm, u0 + m + 3 + 8 * i)
                    pe.wait_ge(o_evac, u0 + m + 1 + 8 * i)
                    nc.tensor.transpose(bank[6 + m % 2][:, P:2 * P], yo[:, m % 2, :], ident).then_inc(turn_full, 1)

                att_schedule(pe, [(2, spread), (0, scores), (2, values), (3, turn)], 3)

            def rope(at, src, swap, count0):
                for x, a in enumerate(src):
                    pe.wait_ge(rope_free, count0 + x + 1)
                    at(x)
                    nc.tensor.matmul(bank[6][:, 0:a.shape[1]], swap, a, start=True, stop=True).then_inc(rope_full, 1)

            def moe_layer(l):
                q, nt = moe[l], TILES_OF[l]
                for t in range(nt):
                    if t > 0:
                        pe.wait_ge(q["xt_cp"], 2 * t)
                    for k in range(KT):
                        tr = nc.tensor.transpose(bank[k // 4][:, (k % 4) * P:(k % 4 + 1) * P], u2[:, k, t * P:(t + 1) * P], ident)
                    tr.then_inc(q["xt_tr"], 1)
                pe.wait_ge(wr_loaded, 16 * (l + 1))
                for t in range(nt):
                    for k in range(KT):
                        mm = nc.tensor.matmul(bank[2][:, t * ROUTE:(t + 1) * ROUTE], u2[:, k, t * P:(t + 1) * P], wr[:, k, :],
                                              start=(k == 0), stop=(k == KT - 1))
                mm.then_inc(q["logits"], 1)
                pe.wait_ge(q["onehot"], 1)
                for t in range(nt):
                    for j in range(t + 1):
                        nc.tensor.matmul(bank[3][:, t * NE:(t + 1) * NE], ones if j < t else const("before"), both[:, j, :],
                                         start=(j == 0), stop=(j == t))
                for j in range(nt):
                    mm = nc.tensor.matmul(bank[4][0:NE, 0:2], both[:, j, :], ones[:, 0:2], start=(j == 0), stop=(j == nt - 1))
                mm.then_inc(q["counts"], 1)
                pe.wait_ge(q["nblk"], 1)
                nc.tensor.matmul(bank[5][:, 0:NE], nbb[0:NE, :], const("tri_lt")[0:NE, :], start=True, stop=True)
                nc.tensor.matmul(bank[6][0:NE, 0:2], const("tri_le")[0:NE, :], nbb[0:NE, 0:2], start=True, stop=True)
                nc.tensor.matmul(bank[7][0:2, TABW:TABW + 2], nbb[0:NE, 0:2], ones[0:NE, 0:2], start=True, stop=True).then_inc(q["starts"], 1)
                pe.wait_ge(q["cmp"], 1)
                nc.tensor.matmul(bank[6][0:2, 64:64 + TABW], ones[0:NE, 0:2], cmpb[0:NE, 0:TABW], start=True, stop=True).then_inc(q["exp_row"], 1)

                lo, hi = slice(0, MB), slice(MB, 2 * MB)

                def spread_x(b):
                    pe.wait_ge(q["gathered"], 16 * (b + 1))
                    nc.tensor.matmul(bank[2][:, 0:MB], xg[lo, 0:D:KT], ident[lo, lo], start=True, stop=True)
                    for k in range(1, KT):
                        tr = nc.tensor.transpose(bank[2][:, k * MB:(k + 1) * MB], xg[lo, k:D:KT], ident[lo, lo])
                    tr.then_inc(q["xt_full"], 1)

                def up(b, first=False):
                    pe.wait_ge(q["xt_ready"], b + 1)
                    if not first:
                        pe.wait_ge(q["h_ready"], b)
                    for c in range(2):
                        pe.wait_ge(mload[l][c], 16 * (b + 1))
                        pe.wait_ge(mload[l][2 + c], 16 * (b + 1))
                        for k in range(4):
                            flags = dict(start=(c == 0 and k == 0), stop=(c == 1 and k == 3))
                            ga = nc.tensor.matmul(bank[0][lo, :], xT[:, 4 * c + k, :], wslot[c][:, k * EF:(k + 1) * EF], **flags)
                            if k == 3:
                                ga.then_inc([mdone[l][0], q["gate_full"]][c], 1)
                            mm = nc.tensor.matmul(bank[0][hi, :], xT[:, 4 * c + k, :], wslot[2 + c][:, k * EF:(k + 1) * EF], **flags)
                        mm.then_inc([mdone[l][1], q["up_full"]][c], 1)

                def out(b, first=False):
                    pe.wait_ge(q["ht_ready"], b + 1)
                    if not first:
                        pe.wait_ge(q["y_ready"], b)
                    for c in range(2):
                        pe.wait_ge(mload[l][4 + c], 16 * (b + 1))
                        for k in range(2):
                            for n, half in enumerate((lo, hi)):
                                mm = nc.tensor.matmul(bank[4][half, :], hT[:, 2 * c + k, :],
                                                      wslot[4 + c][:, k * D + n * 512:k * D + (n + 1) * 512],
                                                      start=(c == 0 and k == 0), stop=(c == 1 and k == 1))
                    mm.then_inc(q["w2_done"], 1)

                def spread_h(b):
                    pe.wait_ge(q["h_ready"], b + 1)
                    nc.tensor.matmul(bank[6][:, 0:MB], hmul[hi, 0:EF:EF // P], ident[hi, hi], start=True, stop=True)
                    for k in range(1, EF // P):
                        tr = nc.tensor.transpose(bank[6][:, k * MB:(k + 1) * MB], hmul[hi, k:EF:EF // P], ident[hi, hi])
                    tr.then_inc(q["htp_full"], 1)

                phase.end()
                last = pe.value_load(exp_i[0:1, TABW:TABW + 1], min_val=2, max_val=NBMAX - 1)
                spread_x(0)
                up(0, first=True)
                spread_x(1)
                spread_h(0)
                out(0, first=True)
                up(1)
                spread_x(2)
                spread_h(1)
                with pe.Fori(2, last + 1) as b:
                    out(b - 1)
                    up(b)
                    spread_x(b + 1)
                    spread_h(b)
                out(last)
                phase.end()
                for t in range(nt):
                    pe.wait_ge(q["sum_ready"], t + 1)
                    if t > 0:
                        pe.wait_ge(q["sum_read"], t)
                    for k in range(KT):
                        tr = nc.tensor.transpose(bank[k // 4][:, (k % 4) * P:(k % 4 + 1) * P], fsum[:, k * P:(k + 1) * P], ident)
                    tr.then_inc(q["sum_tr"], 1)
                phase.end()

            pe.wait_ge(loaded, 64)
            for j in range(4):
                nc.tensor.matmul(bank[j][:, 0:P], ident, ident, start=True, stop=True).then_inc(full[j], 1)
            pe.wait_ge(cond_ready, 1)
            ffn(1, 1)

            norm_sum(u1)
            normed(3)
            dense("xbr", 2, lambda j, k: u1[:, k, :])
            dense("q1", 2, lambda j, k: u1[:, k, :])
            r0, l0, _ = plan["kv1"]
            pe.wait_ge(wload[0], 16 * (l0 + 1))
            for j in range(2):
                pe.wait_ge(free[j], r0)
                for k in range(KT):
                    mm = nc.tensor.matmul(bank[j][:, :], slot[0][:, j * KT * P + k * P:j * KT * P + (k + 1) * P], u1[:, k, :],
                                          start=(k == 0), stop=(k == KT - 1))
                mm.then_inc(full[j], 1)
            pe.wait_ge(wload[1], 16 * (l0 + 1))
            for j in range(2):
                pe.wait_ge(free[2 + j], r0)
                for t in range(2):
                    for k in range(KT):
                        mm = nc.tensor.matmul(bank[2 + j][:, t * C:(t + 1) * C], u1[:, k, (2 * j + t) * P:(2 * j + t + 1) * P],
                                              slot[1][:, k * C:(k + 1) * C], start=(k == 0), stop=(k == KT - 1))
                mm.then_inc(full[2 + j], 1)
            dense("gate", 2, lambda j, k: u1[:, k, :])
            pe.wait_ge(lru_loaded, 16)
            for t in range(KT):
                pe.wait_ge(xc_ready, t + 1)
                if t > 0:
                    pe.wait_ge(lin_free, t)
                nc.tensor.matmul(bank[4][:, :], lru_w[:, 0, t, :], xc[:, t, :], start=True, stop=True)
                nc.tensor.matmul(bank[5][:, :], lru_w[:, 1, t, :], xc[:, t, :], start=True, stop=True).then_inc(lin_full, 1)
            rope(lambda x: pe.wait_ge(raw_ready, 1 if x < KT else 2), [qt1[:, x, :] for x in range(KT)] + [kt1[:, x, :] for x in range(2)],
                 const("swap1"), 0)
            phase.end()
            attend(False, 0, *att_views(o, 2 * P), kt1, v1)
            phase.end()
            dense("merge", 8, lambda j, k: (u1, xc, u1, f)[j][:, k, :])
            pe.wait_ge(mrg_ready, 8)
            dense("out1", 2, lambda j, k: merged[:, k, :])
            norm_sum(u1)
            phase.end()
            ffn(2, 5)

            norm_sum(u2, context=True)
            normed(7)
            paired("even_in", 4, u2)
            phase.end()
            pe.wait_ge(dft_loaded, 80)
            for g in range(4):
                if g > 0:
                    pe.wait_ge(ac_ready, 3 * g)
                for t in range(TT):
                    mm = nc.tensor.matmul(bank[t // 2][:, (t % 2) * 2 * P:(t % 2 + 1) * 2 * P], pt[:, g, t * P:(t + 1) * P], csd,
                                          start=True, stop=True)
                    if t % 2:
                        mm.then_inc(ac_full, 1)
                if g > 0:
                    pe.wait_ge(dft_evac, g)
                pe.wait_ge(ac_ready, 3 * g + 3)
                for t in range(LT):
                    nc.tensor.matmul(bank[3][:, :], ac[:, t, 0:P], c_lat[:, t, :], start=(t == 0), stop=False)
                    nc.tensor.matmul(bank[3][:, :], ac[:, t, P:2 * P], s_lat[:, t, :], start=False, stop=(t == LT - 1))
                for t in range(2):
                    nc.tensor.matmul(bank[4][:, 0:C], ac[:, LT + t, 0:P], c_ctx[:, t, :], start=(t == 0), stop=False)
                    mm = nc.tensor.matmul(bank[4][:, 0:C], ac[:, LT + t, P:2 * P], s_ctx[:, t, :], start=False, stop=(t == 1))
                mm.then_inc(dft_full, 1)
            phase.end()
            paired("even_out", 2, yt)
            phase.end()
            norm_sum(u2, context=True)
            normed(8)
            moe_layer(0)

            norm_sum(u2, context=True)
            normed(9)
            dense("q2", 2, lambda j, k: u2[:, k, 0:S])
            r0, l0, _ = plan["kv2"]
            pe.wait_ge(wload[0], 16 * (l0 + 1))
            for j in range(4):
                pe.wait_ge(free[j], r0)
                a, n = ((0, S), (S, C))[j % 2]
                for k in range(KT):
                    mm = nc.tensor.matmul(bank[j][:, 0:n], slot[0][:, (j // 2) * KT * P + k * P:(j // 2) * KT * P + (k + 1) * P],
                                          u2[:, k, a:a + n], start=(k == 0), stop=(k == KT - 1))
                mm.then_inc(full[j], 1)
            pe.wait_ge(wload[1], 16 * (l0 + 1))
            for j in range(4):
                pe.wait_ge(free[j], r0 + 1)
                for t in ((0, 1), (2, 3), (4,), (5,))[j]:
                    for k in range(KT):
                        mm = nc.tensor.matmul(bank[j][:, (t % 2 if j < 2 else 0) * C:(t % 2 if j < 2 else 0) * C + C],
                                              u2[:, k, t * P:(t + 1) * P], slot[1][:, k * C:(k + 1) * C],
                                              start=(k == 0), stop=(k == KT - 1))
                mm.then_inc(full[j], 1)
            for x in range(KT + 4):
                pe.wait_ge(qsq_ready, x + 1)
                if x > 0:
                    pe.wait_ge(qstd_ready, x)
                n = C if x in (KT + 1, KT + 3) else S
                nc.tensor.matmul(bank[4][:, 0:n], const("headsum"), tmp[:, x % 2, 0:n], start=True, stop=True).then_inc(qsum_full, 1)
            rope(lambda x: pe.wait_ge(qn_ready, x + 1 if x <= KT else KT + 3), [qt2[:, x, :] for x in range(KT)] + [kt2[:, x, 0:S] for x in range(2)],
                 const("swap2"), 10)
            phase.end()
            attend(True, 32, *att_views(att2, 5 * P), kt2, v2)
            phase.end()
            dense("wo", 2, lambda j, k: f[:, k, :])
            phase.end()
            norm_sum(u2)
            normed(10)
            moe_layer(1)

        @block.scalar
        def _(act):
            phase = Phase(act)
            norms = [0]

            def squares(src, u, a=0, last=True):
                for k in range(KT):
                    i = nc.scalar.activation(u[:, k, a:a + src.shape[2]], src[:, k, :], ACT.Square)
                    if last:
                        i.then_inc(sq_ready, 1)

            def std(context=False):
                norms[0] += 1
                act.wait_ge(ssum_ready, norms[0])
                i = nc.scalar.activation(rs[:, 0:S], bank[4][:, :], ACT.Sqrt, bias=const("eps"), scale=1.0 / D)
                if context:
                    i = nc.scalar.activation(rs[:, S:SC], bank[5][:, 0:C], ACT.Sqrt, bias=const("eps"), scale=1.0 / D)
                i.then_inc(std_ready, 1)

            def before_norm(name, its, order=(0, 1, 2, 3)):
                r0 = plan[name][0]
                with act.Fori(0, its) as i:
                    for n, j in enumerate(order):
                        act.wait_ge(full[j], r0 + 1 + i)
                        nc.scalar.activation(f[:, bass.ds(4 * i + n, 1), :].rearrange("p a t -> p (a t)"), bank[j][:, :], ACT.Copy)
                        nc.scalar.activation(u1[:, bass.ds(4 * i + n, 1), :].rearrange("p a t -> p (a t)"), bank[j][:, :],
                                             ACT.Square).then_inc(free[j], 1)
                act.drain().then_inc(sq_ready, KT)

            def evacuate(name, its, dst, n=S):
                r0 = plan[name][0]
                with act.Fori(0, its) as i:
                    for j in range(4):
                        act.wait_ge(full[j], r0 + 1 + i)
                        nc.scalar.activation(dst(4 * i + j), bank[j][:, 0:n], ACT.Copy).then_inc(free[j], 1)

            def ffn(n):
                squares(lat[:, :, :], u1)
                std()
                r0 = plan[f"gu{n}"][0]
                with act.Fori(0, 11) as i:
                    for j in range(2):
                        act.wait_ge(full[j], r0 + 1 + i)
                        act.wait_ge(free[2 + j], r0 + i)
                        nc.scalar.activation(tmp[:, j, :], bank[j][:, :], ACT.Silu).then_inc(free[j], 1)
                before_norm(f"down{n}", 2, (0, 2, 1, 3))
                std()
                phase.end()

            def attend(second, u0, qs, sm, pT, yo):
                def exps(i, m):
                    per, _ = att_groups(second, m % LT)
                    st = small[:, 16 * (m % 4):16 * (m % 4) + 16]
                    act.wait_ge(max_ready, u0 + m + 1 + 8 * i)
                    for s in range(2):
                        nc.scalar.activation(sm[:, m % 4, s, 0:per * P], sm[:, m % 4, s, 0:per * P], ACT.Exp,
                                             bias=st[:, 4 + s:5 + s], accum_out=st[:, 6 + s:7 + s])
                    nc.scalar.activation(st[:, 8:10], st[:, 10:12], ACT.Exp)
                    act.drain().then_inc(exp_ready, 1)

                def copies(i, m):
                    per, groups = att_groups(second, m % LT)
                    for g in range(groups):
                        at = groups_before(second, 0, m) + g
                        w = min(4, 2 * per - 4 * g) * P
                        act.wait_ge(t_full, groups_before(second, i, m) + g + 1)
                        nc.scalar.activation(pT[:, m % 2, 4 * g * P:4 * g * P + w], bank[4 + at % 2][:, 0:w],
                                             ACT.Copy).then_inc(t_evac, 1)

                def outputs(i, m):
                    n, kv = m % LT, m // LT
                    act.wait_ge(turn_full, u0 + m + 3 + 8 * i)
                    nc.scalar.activation(f[:, bass.ds(4 * kv + i, 1), n * P:(n + 1) * P].rearrange("p a t -> p (a t)"),
                                         bank[6 + m % 2][:, P:2 * P], ACT.Copy).then_inc(o_evac, 1)

                att_schedule(act, [(2, copies), (3, outputs), (0, exps)], 3)

            def moe_layer(l):
                q, nt = moe[l], TILES_OF[l]
                act.dma_start(wr, d["wr"][l]).then_inc(wr_loaded, 16)
                for t in range(nt):
                    act.wait_ge(q["xt_tr"], t + 1)
                    if t > 0:
                        act.wait_ge(q["xt_out"], 16 * t)
                    nc.scalar.activation(xg[:, 0:512], bank[0][:, :], ACT.Copy).then_inc(q["xt_cp"], 1)
                act.wait_ge(q["gexp_in"], 1)
                nc.scalar.activation(ge[:, 0:nt, :], ge[:, 0:nt, :], ACT.Exp).then_inc(q["gexp"], 1)
                act.wait_ge(q["eexp_in"], 1)
                nc.scalar.activation(scal[:, 5, 0:nt], scal[:, 4, 0:nt], ACT.Exp).then_inc(q["eexp"], 1)

                def silu(b, first=False):
                    act.wait_ge(q["gate_full"], b + 1)
                    if not first:
                        act.wait_ge(q["h_ready"], b)
                    nc.scalar.activation(hsil[MB:2 * MB, :], bank[0][0:MB, :], ACT.Silu).then_inc(q["sg_ready"], 1)

                def copy_y(b, first=False):
                    act.wait_ge(q["w2_done"], b + 1)
                    if not first:
                        act.wait_ge(q["y_written"], 32 * b)
                    nc.scalar.activation(ysb, bank[4][:, :], ACT.Copy).then_inc(q["y_ready"], 1)

                def write_y(b, written="y_written"):
                    act.wait_ge(q["y_ready"], b + 1)
                    for n in range(2):
                        act.dma_start(d["yb"][l][bass.ds(b * MB, MB), n * 512:(n + 1) * 512], ysb[n * MB:(n + 1) * MB, :]
                                      ).then_inc(q[written], 16)

                act.wait_ge(yb_zeroed, 32)
                phase.end()
                last = act.value_load(exp_i[0:1, TABW:TABW + 1], min_val=2, max_val=NBMAX - 1)
                silu(0, first=True)
                copy_y(0, first=True)
                write_y(0)
                silu(1)
                with act.Fori(2, last + 1) as b:
                    copy_y(b - 1)
                    write_y(b - 1)
                    silu(b)
                copy_y(last)
                write_y(last, "y_last")
                act.wait_ge(q["y_last"], 32)
                phase.end()
                phase.end()

            act.wait_ge(loaded, 64)
            nc.scalar.activation(silu_c[:, :, :], vec("cond").rearrange("p (k s) -> p k s", k=KT), ACT.Silu).then_inc(cond_ready, 1)
            ffn(1)

            act.dma_start(lru_w, d["lru_w"]).then_inc(lru_loaded, 16)
            squares(lat[:, :, :], u1)
            std()
            act.wait_ge(cond_ready, 2)
            nc.scalar.activation(lam8[:, 4, :], lam8[:, 3, :], ACT.Exp).then_inc(cond_ready, 1)
            r0 = plan["xbr"][0]
            with act.Fori(0, 2) as i:
                for j in range(4):
                    act.wait_ge(full[j], r0 + 1 + i)
                    nc.scalar.activation(xbr[:, bass.ds(4 * i + j, 1), CONV1 - 1:XPAD].rearrange("p a t -> p (a t)"),
                                         bank[j][:, :], ACT.Copy).then_inc(free[j], 1)
            act.drain().then_inc(xbr_ready, 1)
            evacuate("q1", 2, lambda x: qt1[:, bass.ds(x, 1), :].rearrange("p a t -> p (a t)"))
            act.drain().then_inc(raw_ready, 1)
            r0 = plan["kv1"][0]
            for j in range(4):
                act.wait_ge(full[j], r0 + 1)
                nc.scalar.activation(kt1[:, j, :] if j < 2 else v1[:, 2 * (j - 2):2 * (j - 2) + 2, :], bank[j][:, :],
                                     ACT.Copy).then_inc(free[j], 1)
            act.drain().then_inc(raw_ready, 1)
            r0 = plan["gate"][0]
            with act.Fori(0, 2) as i:
                for j in range(4):
                    act.wait_ge(full[j], r0 + 1 + i)
                    nc.scalar.activation(f[:, bass.ds(4 * i + j, 1), :].rearrange("p a t -> p (a t)"), bank[j][:, :],
                                         ACT.Gelu_apprx_tanh).then_inc(free[j], 1)
            act.drain().then_inc(gate_ready, 1)
            ba, bx = vec("lru_b_a"), vec("lru_b_x")
            for t in range(KT):
                act.wait_ge(lin_full, t + 1)
                nc.scalar.activation(gr[:, t, :], bank[4][:, :], ACT.Sigmoid, bias=ba[:, t:t + 1])
                nc.scalar.activation(gi[:, t, :], bank[5][:, :], ACT.Sigmoid, bias=bx[:, t:t + 1]).then_inc(lin_free, 1)
            act.drain()
            for t in range(KT):
                nc.scalar.activation(xbr[:, t, 0:S], gr[:, t, :], ACT.Exp, scale=lam8[:, 1, t:t + 1])
                nc.scalar.activation(gr[:, t, :], gr[:, t, :], ACT.Tanh, scale=lam8[:, 0, t:t + 1])
                act.drain().then_inc(decay_ready, 1)
            for t in range(KT):
                act.wait_ge(msq_ready, t + 1)
                nc.scalar.activation(gr[:, t, :], gr[:, t, :], ACT.Sqrt).then_inc(mult_ready, 1)
            phase.end()
            attend(False, 0, *att_views(o, 2 * P))
            phase.end()
            r0 = plan["merge"][0]
            with act.Fori(0, 8) as i:
                for n in range(2):
                    act.wait_ge(full[2 * n], r0 + 1 + i)
                    act.wait_ge(free[2 * n + 1], r0 + i)
                    nc.scalar.activation(tmp[:, n, :], bank[2 * n][:, :], ACT.Sigmoid).then_inc(free[2 * n], 1)
            before_norm("out1", 2)
            std()
            phase.end()
            ffn(2)

            for dst, name in ((csd, "cs_d"), (c_ctx, "c_ctx"), (s_ctx, "s_ctx"), (c_lat, "c_lat"), (s_lat, "s_lat")):
                a, n = DFT_AT[name]
                src = d["dft"][:, a:a + n]
                if len(dst.shape) == 3:
                    src = src.rearrange("p (l t) -> p l t", l=dst.shape[1])
                act.dma_start(dst, src).then_inc(dft_loaded, 16)
            squares(cxt[:, :, :], u2, S, last=False)
            squares(lat[:, :, :], u2)
            std(context=True)
            r0 = plan["even_in"][0]
            with act.Fori(0, 8) as i:
                for j in range(4):
                    act.wait_ge(full[j], r0 + 1 + i)
                    a, n = ((0, S), (S, C))[j % 2]
                    nc.scalar.activation(pt[:, bass.ds(2 * i + j // 2, 1), a:a + n].rearrange("p a t -> p (a t)"), bank[j][:, 0:n],
                                         ACT.Copy).then_inc(free[j], 1)
            phase.end()
            for g in range(4):
                if g > 0:
                    act.wait_ge(dft_full, g)
                for h in range(3):
                    act.wait_ge(ac_full, 3 * g + h + 1)
                    nc.scalar.activation(ac[:, 2 * h:2 * h + 2, :], bank[h][:, :], ACT.Copy).then_inc(ac_ready, 1)
                act.wait_ge(dft_full, g + 1)
                nc.scalar.activation(yt[:, g, 0:S], bank[3][:, :], ACT.Copy)
                nc.scalar.activation(yt[:, g, S:SC], bank[4][:, 0:C], ACT.Copy).then_inc(dft_evac, 1)
            phase.end()
            phase.end()
            squares(cxt[:, :, :], u2, S, last=False)
            squares(lat[:, :, :], u2)
            std(context=True)
            moe_layer(0)

            squares(cxt[:, :, :], u2, S, last=False)
            squares(lat[:, :, :], u2)
            std(context=True)
            evacuate("q2", 2, lambda x: qt2[:, bass.ds(x, 1), :].rearrange("p a t -> p (a t)"))
            r0 = plan["kv2"][0]
            for j in range(4):
                act.wait_ge(full[j], r0 + 1)
                a, n = ((0, S), (S, C))[j % 2]
                nc.scalar.activation(kt2[:, j // 2, a:a + n], bank[j][:, 0:n], ACT.Copy).then_inc(free[j], 1)
            for j in range(4):
                act.wait_ge(full[j], r0 + 2)
                a, n = ((0, 2), (2, 2), (4, 1), (5, 1))[j]
                nc.scalar.activation(v2[:, a:a + n, :], bank[j][:, 0:n * C], ACT.Copy).then_inc(free[j], 1)
            act.drain()
            heads = [qt2[:, x, :] for x in range(KT)] + [kt2[:, x, a:b] for x in range(2) for a, b in ((0, S), (S, SC))]
            for x, a in enumerate(heads):
                n = a.shape[1]
                if x > 1:
                    act.wait_ge(qsum_full, x - 1)
                nc.scalar.activation(tmp[:, x % 2, 0:n], a, ACT.Square).then_inc(qsq_ready, 1)
                act.wait_ge(qsum_full, x + 1)
                if x > 1:
                    act.wait_ge(qn_ready, x - 1)
                nc.scalar.activation(tmp[:, 2 + x % 2, 0:n], bank[4][:, 0:n], ACT.Sqrt, bias=const("eps"),
                                     scale=1.0 / HD).then_inc(qstd_ready, 1)
            phase.end()
            attend(True, 32, *att_views(att2, 5 * P))
            phase.end()
            phase.end()
            squares(lat[:, :, :], u2)
            std()
            moe_layer(1)

        @block.vector
        def _(dve):
            phase = Phase(dve)
            norms = [0]
            modf = mod[:, :, :, :, :].rearrange("p l s k c -> p (l s k c)")
            bm = vec("b_mod")

            def rsqrt(n):
                norms[0] += 1
                dve.wait_ge(std_ready, norms[0])
                nc.vector.reciprocal(rs[:, 0:n], rs[:, 0:n])
                dve.drain()

            def pre_norm(g, u):
                rsqrt(S)
                for k in range(KT):
                    nc.vector.scalar_tensor_tensor(u[:, k, :], lat[:, k, :], g[:, k:k + 1], rs[:, 0:S], ALU.mult,
                                                   ALU.mult).then_inc(u_ready, 1)

            def post_norm(g):
                rsqrt(S)
                for k in range(KT):
                    nc.vector.scalar_tensor_tensor(f[:, k, :], f[:, k, :], g[:, k:k + 1], rs[:, 0:S], ALU.mult, ALU.mult)
                    dve.drain()
                    nc.vector.tensor_tensor(lat[:, k, :], lat[:, k, :], f[:, k, :], ALU.add).then_inc(u_ready, 1)

            def mod_norm(l, which, context):
                rsqrt(SC if context else S)
                for k in range(KT):
                    parts = [(0, lat, 0, S)] + ([(1, cxt, S, C)] if context else [])
                    for st, src, a, n in parts:
                        nc.vector.scalar_tensor_tensor(u2[:, k, a:a + n], src[:, k, :], amod[:, l, which, st, k:k + 1],
                                                       rs[:, a:a + n], ALU.mult, ALU.mult)
                    dve.drain()
                    for st, src, a, n in parts:
                        i = nc.vector.tensor_scalar(u2[:, k, a:a + n], u2[:, k, a:a + n], mod[:, l, 3 * which, k, st:st + 1], None,
                                                    ALU.add)
                    i.then_inc(u_ready, 1)

            def modulation(n):
                dve.wait_ge(mod_full, n + 2)
                nc.vector.tensor_tensor(modf[:, bass.ds(4 * n, 4)], bank[5][:, 0:4], bm[:, bass.ds(4 * n, 4)], ALU.add).then_inc(mod_free, 1)

            def ffn(n, pre, post):
                pre_norm(vec(pre), u1)
                r0 = plan[f"gu{n}"][0]
                mod = (n - 1) * (MOD_GU + MOD_DOWN)
                with dve.Fori(0, 11) as i:
                    modulation(mod + 2 * i)
                    for j in range(2):
                        dve.wait_ge(full[2 + j], r0 + 1 + i)
                        dve.wait_ge(free[j], r0 + 1 + i)
                        nc.vector.tensor_tensor(act_t[:, bass.ds(2 * i + j, 1), :].rearrange("p a t -> p (a t)"), tmp[:, j, :],
                                                bank[2 + j][:, :], ALU.mult).then_inc(free[2 + j], 1)
                    modulation(mod + 1 + 2 * i)
                dve.drain().then_inc(act_ready, 1)
                for x in range(MOD_DOWN):
                    modulation(mod + MOD_GU + x)
                post_norm(post)
                phase.end()

            def attend(second, u0, qs, sm, pT, yo, sinks, mask):
                def stats(i, m):
                    n, kv = m % LT, m // LT
                    lo, hi, m0 = att_tiles(second, n)
                    per, _ = att_groups(second, n)
                    at = 0 if second else 2 * (m % 2)
                    w = (hi - lo) * P
                    st = small[:, 16 * (m % 4):16 * (m % 4) + 16]
                    dve.wait_ge(s_full, u0 + m + 9 + 8 * i)
                    for s in range(2):
                        x = nc.vector.scalar_tensor_tensor(sm[:, m % 4, s, 0:w], bank[at + s][:, 0:w], SCALE, mask[:, m0:m0 + w],
                                                           ALU.mult, ALU.add)
                        if second:
                            x = nc.vector.tensor_scalar(sm[:, m % 4, s, w:w + C], bank[2 + s][:, 0:C], SCALE, None, ALU.mult)
                    x.then_inc(s_evac, 1)
                    dve.drain()
                    nc.vector.tensor_reduce(st[:, 0:2], sm[:, m % 4, :, 0:per * P], AX.X, ALU.max)
                    dve.drain()
                    sk = sinks[:, bass.ds(8 * kv + 2 * i, 2)]
                    nc.vector.tensor_tensor(st[:, 2:4], st[:, 0:2], sk, ALU.max)
                    dve.drain()
                    nc.vector.tensor_scalar(st[:, 4:6], st[:, 2:4], -1.0, None, ALU.mult)
                    nc.vector.tensor_tensor(st[:, 10:12], sk, st[:, 2:4], ALU.subtract)
                    dve.drain().then_inc(max_ready, 1)

                def normalise(i, m):
                    st = small[:, 16 * (m % 4):16 * (m % 4) + 16]
                    dve.wait_ge(o_full, u0 + m + 1 + 8 * i)
                    nc.vector.tensor_tensor(st[:, 12:14], st[:, 6:8], st[:, 8:10], ALU.add)
                    dve.drain()
                    nc.vector.reciprocal(st[:, 14:16], st[:, 12:14])
                    dve.drain()
                    dve.wait_ge(turn_full, u0 + m + 1 + 8 * i)
                    for s in range(2):
                        x = nc.vector.tensor_scalar(yo[:, m % 2, s * HD:(s + 1) * HD], bank[6 + m % 2][:, s * HD:(s + 1) * HD],
                                                    st[:, 14 + s:15 + s], None, ALU.mult)
                    x.then_inc(y_norm, 1)

                att_schedule(dve, [(0, stats), (2, normalise)], 2)

            def rope(src, cos, sin, count0):
                for x, a in enumerate(src):
                    dve.wait_ge(rope_full, count0 + x + 1)
                    nc.vector.tensor_tensor(rs[:, 0:S], bank[6][:, :], sin, ALU.mult).then_inc(rope_free, 1)
                    nc.vector.tensor_tensor(a, a, cos, ALU.mult)
                    dve.drain()
                    nc.vector.tensor_tensor(a, a, rs[:, 0:S], ALU.add)
                    dve.drain()

            def moe_layer(l):
                q, nt = moe[l], TILES_OF[l]
                for t in range(nt):
                    dve.wait_ge(q["xt_tr"], t + 1)
                    if t > 0:
                        dve.wait_ge(q["xt_out"], 16 * t)
                    nc.vector.tensor_copy(xg[:, 512:D], bank[1][:, :]).then_inc(q["xt_cp"], 1)

                def bc(x, n):
                    return x.unsqueeze(2).to_broadcast([P, x.shape[1], n])

                def over_last(dst, src, op):
                    nc.vector.tensor_reduce(dst, src, AX.X, op)
                    dve.drain()

                def first_max(dst, cand, src, best, desc, n):
                    nc.vector.tensor_tensor(cand, src, bc(best, n), ALU.is_equal)
                    dve.drain()
                    nc.vector.tensor_tensor(cand, cand, desc.unsqueeze(1).to_broadcast([P, nt, n]), ALU.mult)
                    dve.drain()
                    over_last(scal[:, 11, 0:nt], cand, ALU.max)
                    nc.vector.tensor_tensor(dst, cand, bc(scal[:, 11, 0:nt], n), ALU.is_equal)
                    dve.drain()

                sc = lambda x: scal[:, x, 0:nt]
                lgv, gev, gsv, elv, ecv = lg[:, 0:nt, :], ge[:, 0:nt, :], gsel[:, 0:nt, :], elog[:, 0:nt, :], ecand[:, 0:nt, :]
                dve.wait_ge(q["logits"], 1)
                rb = vec("route_b")[:, l * TT * ROUTE:l * TT * ROUTE + nt * ROUTE]
                nc.vector.tensor_tensor(lgv.rearrange("p t r -> p (t r)"), bank[2][:, 0:nt * ROUTE], rb, ALU.add)
                dve.drain()
                over_last(sc(0), lgv[:, :, 0:NG], ALU.max)
                nc.vector.tensor_tensor(gev, lgv[:, :, 0:NG], bc(sc(0), NG), ALU.subtract)
                dve.drain().then_inc(q["gexp_in"], 1)
                dve.wait_ge(q["gexp"], 1)
                over_last(sc(1), gev, ALU.add)
                over_last(sc(2), gev, ALU.max)
                nc.vector.reciprocal(sc(1), sc(1))
                dve.drain()
                nc.vector.tensor_tensor(sc(1), sc(1), sc(2), ALU.mult)
                first_max(gsv, gev, gev, sc(2), const("gdesc"), NG)
                elg = elv.rearrange("p t (g e) -> p t g e", g=NG)
                for g in range(NG):
                    nc.vector.tensor_tensor(elg[:, :, g, :], lgv[:, :, NG + 8 * g:NG + 8 * g + 8], bc(gsv[:, :, g], 8), ALU.mult)
                nc.vector.tensor_scalar(gev, gsv, -NEG, NEG, ALU.mult, ALU.add)
                dve.drain()
                for g in range(NG):
                    nc.vector.tensor_tensor(elg[:, :, g, :], elg[:, :, g, :], bc(gev[:, :, g], 8), ALU.add)
                dve.drain()
                over_last(sc(2), elv, ALU.max)
                first_max(oh[0][:, 0:nt, :], ecv, elv, sc(2), const("edesc"), NE)
                nc.vector.scalar_tensor_tensor(elv, oh[0][:, 0:nt, :], 2 * NEG, elv, ALU.mult, ALU.add)
                dve.drain()
                over_last(sc(3), elv, ALU.max)
                first_max(oh[1][:, 0:nt, :], ecv, elv, sc(3), const("edesc"), NE)
                nc.vector.tensor_tensor(both[:, 0:nt, :], oh[0][:, 0:nt, :], oh[1][:, 0:nt, :], ALU.add)
                dve.drain().then_inc(q["onehot"], 1)
                nc.vector.tensor_tensor(sc(4), sc(3), sc(2), ALU.subtract)
                dve.drain().then_inc(q["eexp_in"], 1)
                dve.wait_ge(q["eexp"], 1)
                nc.vector.tensor_scalar(sc(6), sc(5), 1.0, None, ALU.add)
                dve.drain()
                nc.vector.reciprocal(sc(6), sc(6))
                dve.drain()
                nc.vector.tensor_tensor(sc(7), sc(6), sc(1), ALU.mult)
                dve.drain()
                nc.vector.tensor_tensor(sc(8), sc(7), sc(5), ALU.mult)
                dve.wait_ge(q["counts"], 1)
                nc.vector.tensor_scalar(col[0:NE, 0:1], bank[4][0:NE, 0:1], 1.0, None, ALU.mult)
                dve.drain()
                nthr = -(-2 * SC // 2 // MB)
                nc.vector.tensor_scalar(cmpb[0:NE, 0:nthr], const("thr")[0:NE, 0:nthr], col[0:NE, 0:1], None, ALU.is_lt)
                dve.drain()
                nc.vector.tensor_reduce(col[0:NE, 1:2], cmpb[0:NE, 0:nthr], AX.X, ALU.add)
                dve.drain()
                nc.vector.tensor_scalar(nbb[0:NE, :], ones[0:NE, :], col[0:NE, 1:2], None, ALU.mult)
                dve.drain().then_inc(q["nblk"], 1)
                dve.wait_ge(q["starts"], 1)
                nc.vector.tensor_copy(col[0:NE, 2:3], bank[6][0:NE, 0:1])
                dve.drain()
                nc.vector.tensor_scalar(cmpb[0:NE, 0:TABW], const("blocks")[0:NE, :], col[0:NE, 2:3], None, ALU.is_ge)
                dve.drain().then_inc(q["cmp"], 1)
                rkv = rank[:, 0:nt, :]
                nc.vector.tensor_copy(rkv.rearrange("p t e -> p (t e)"), bank[3][:, 0:nt * NE])
                dve.drain()
                ovi = over[:, 0:nt, :].bitcast(I32)
                nc.vector.tensor_copy(ovi, rkv)
                dve.drain()
                nc.vector.tensor_scalar(ovi, ovi, MB.bit_length() - 1, None, ALU.logical_shift_right)
                dve.drain()
                ovv = lg[:, 0:nt, 0:NE]
                nc.vector.tensor_copy(ovv, ovi)
                dve.drain()
                nc.vector.tensor_copy(nbb[:, 0:NE], bank[5][:, 0:NE])
                dve.drain()
                start = nbb[:, 0:NE].unsqueeze(1).to_broadcast([P, nt, NE])
                nc.vector.scalar_tensor_tensor(ecv, rkv, float(TABW), start, ALU.mult, ALU.add)
                nc.vector.scalar_tensor_tensor(elv, start, float(MB), rkv, ALU.mult, ALU.add)
                dve.drain()
                nc.vector.scalar_tensor_tensor(ecv, ovv, 1.0 - MB * TABW, ecv, ALU.mult, ALU.add)
                dve.drain()
                for which, src in ((0, elv), (1, ecv)):
                    for x in range(2):
                        nc.vector.tensor_tensor(lg[:, 0:nt, 0:NE], oh[x][:, 0:nt, :], src, ALU.mult)
                        dve.drain()
                        over_last(pos_f[:, which, x, 0:nt], lg[:, 0:nt, 0:NE], ALU.add)
                        nc.vector.tensor_copy(pos_u[:, which, x, 0:nt], pos_f[:, which, x, 0:nt])
                dve.drain().then_inc(q["pos"], 1)
                dve.wait_ge(q["exp_row"], 1)
                nc.vector.tensor_scalar(exp_i[0:1, 0:TABW], bank[6][0:1, 64:64 + TABW], float(NE - 1), None, ALU.min)
                nc.vector.tensor_scalar(exp_i[0:1, TABW:TABW + 1], bank[7][0:1, TABW:TABW + 1], -1.0, None, ALU.add)
                dve.drain().then_inc(q["expert"], 1)

                def copy_x(b):
                    dve.wait_ge(q["xt_full"], b + 1)
                    nc.vector.tensor_copy(xT, bank[2][:, :]).then_inc(q["xt_ready"], 1)

                def mul(b, first=False):
                    dve.wait_ge(q["up_full"], b + 1)
                    dve.wait_ge(q["sg_ready"], b + 1)
                    if not first:
                        dve.wait_ge(q["htp_full"], b)
                    nc.vector.tensor_tensor(hmul[MB:2 * MB, :], hsil[MB:2 * MB, :], bank[0][MB:2 * MB, :], ALU.mult).then_inc(q["h_ready"], 1)

                def copy_h(b):
                    dve.wait_ge(q["htp_full"], b + 1)
                    nc.vector.tensor_copy(hT, bank[6][:, 0:EF // P * MB]).then_inc(q["ht_ready"], 1)

                phase.end()
                last = dve.value_load(exp_i[0:1, TABW:TABW + 1], min_val=2, max_val=NBMAX - 1)
                copy_x(0)
                mul(0, first=True)
                copy_x(1)
                copy_h(0)
                mul(1)
                copy_x(2)
                copy_h(1)
                with dve.Fori(2, last + 1) as b:
                    mul(b)
                    copy_x(b + 1)
                    copy_h(b)
                phase.end()
                for t in range(nt):
                    dve.wait_ge(q["got"], 32 * (t + 1))
                    if t > 0:
                        dve.wait_ge(q["sum_tr"], t)
                    nc.vector.tensor_scalar(fsum, yget[0], scal[:, 7, t:t + 1], None, ALU.mult)
                    dve.drain()
                    nc.vector.scalar_tensor_tensor(fsum, yget[1], scal[:, 8, t:t + 1], fsum, ALU.mult, ALU.add).then_inc(q["sum_ready"], 1)
                    dve.wait_ge(q["sum_tr"], t + 1)
                    st, dst = (0, lat[:, :, t * P:(t + 1) * P]) if t < LT else (1, cxt[:, :, (t - LT) * P:(t - LT + 1) * P])
                    for k in range(KT):
                        x = nc.vector.scalar_tensor_tensor(dst[:, k, :], bank[k // 4][:, (k % 4) * P:(k % 4 + 1) * P],
                                                           mod[:, l, 5, k, st:st + 1], dst[:, k, :], ALU.mult, ALU.add)
                    x.then_inc(q["sum_read"], 1)
                phase.end()

            for s, n in ([(x, 1) for x in free] + [(mod_full, 1), (mod_free, 1), (s_full, UNITS), (s_evac, 2), (y_norm, 2), (turn_full, 2), (t_evac, 2), (o_evac, 2), (rope_free, 1)]):
                dve.drain().then_inc(s, n)
            dve.wait_ge(loaded, 64)
            nc.vector.tensor_scalar(half_g[:, 0, :], vec("ffn1_post_g"), 0.5, None, ALU.mult)
            nc.vector.tensor_scalar(half_g[:, 1, :], vec("ffn2_post_g"), 0.5, None, ALU.mult)
            ffn(1, "ffn1_pre_g", half_g[:, 0, :])

            pre_norm(vec("mix_pre_g"), u1)
            lm = vec("lru_lambda")
            nc.vector.tensor_scalar(lam8[:, 2, :], lm, -1.0, 0.0, ALU.mult, ALU.max)
            nc.vector.tensor_scalar(lam8[:, 3, :], lm, -1.0, None, ALU.mult)
            dve.drain()
            nc.vector.tensor_tensor(lam8[:, 3, :], lam8[:, 3, :], lm, ALU.min)
            dve.drain().then_inc(cond_ready, 1)
            dve.wait_ge(cond_ready, 3)
            nc.vector.tensor_scalar(lam8[:, 5, :], lam8[:, 4, :], 2.0, None, ALU.add)
            dve.drain()
            nc.vector.reciprocal(lam8[:, 5, :], lam8[:, 5, :])
            dve.drain()
            nc.vector.tensor_tensor(lam8[:, 4, :], lam8[:, 4, :], lam8[:, 5, :], ALU.mult)
            dve.drain()
            nc.vector.tensor_tensor(lam8[:, 5, :], lam8[:, 4, :], lam8[:, 4, :], ALU.mult)
            nc.vector.memset(lam8[:, 6, :], 1.0 / 17)
            dve.drain()
            for odd in range(15, 0, -2):
                nc.vector.tensor_tensor(lam8[:, 6, :], lam8[:, 6, :], lam8[:, 5, :], ALU.mult)
                dve.drain()
                nc.vector.tensor_scalar(lam8[:, 6, :], lam8[:, 6, :], 1.0 / odd, None, ALU.add)
                dve.drain()
            nc.vector.tensor_tensor(lam8[:, 6, :], lam8[:, 6, :], lam8[:, 4, :], ALU.mult)
            dve.drain()
            nc.vector.scalar_tensor_tensor(lam8[:, 6, :], lam8[:, 6, :], 2.0, lam8[:, 2, :], ALU.mult, ALU.add)
            dve.drain()
            nc.vector.tensor_scalar(lam8[:, 0, :], lam8[:, 6, :], LRU_C, None, ALU.mult)
            nc.vector.tensor_scalar(lam8[:, 1, :], lam8[:, 6, :], -LRU_C, None, ALU.mult)
            nc.vector.memset(xbr[:, :, 0:CONV1 - 1], 0.0)
            dve.drain()
            dve.wait_ge(xbr_ready, 1)
            cw, cb = vec("conv_w"), vec("conv_b")
            for t in range(KT):
                nc.vector.tensor_scalar(xc[:, t, :], xbr[:, t, 0:S], cw[:, t:t + 1], cb[:, t:t + 1], ALU.mult, ALU.add)
                for k in range(1, CONV1):
                    dve.drain()
                    x = nc.vector.scalar_tensor_tensor(xc[:, t, :], xbr[:, t, k:k + S], cw[:, KT * k + t:KT * k + t + 1], xc[:, t, :],
                                                       ALU.mult, ALU.add)
                x.then_inc(xc_ready, 1)
            for t in range(KT):
                dve.wait_ge(decay_ready, t + 1)
                nc.vector.tensor_scalar(tmp[:, 0, :], gr[:, t, :], 1.0, None, ALU.add)
                nc.vector.tensor_tensor(gi[:, t, :], gi[:, t, :], xc[:, t, :], ALU.mult)
                dve.drain()
                nc.vector.reciprocal(tmp[:, 0, :], tmp[:, 0, :])
                dve.drain()
                nc.vector.scalar_tensor_tensor(gr[:, t, :], gr[:, t, :], 2.0, tmp[:, 0, :], ALU.mult, ALU.mult).then_inc(msq_ready, 1)
                dve.drain()
            rope([qt1[:, x, :] for x in range(KT)] + [kt1[:, x, :] for x in range(2)], const("cos1"), const("sin1"), 0)
            dve.wait_ge(gate_ready, 1)
            for t in range(KT):
                dve.wait_ge(mult_ready, t + 1)
                nc.vector.tensor_tensor(gi[:, t, :], gi[:, t, :], gr[:, t, :], ALU.mult)
                dve.drain()
                nc.vector.tensor_tensor_scan(xc[:, t, :], xbr[:, t, 0:S], gi[:, t, :], 0.0, ALU.mult, ALU.add)
                dve.drain()
                nc.vector.tensor_tensor(xc[:, t, :], xc[:, t, :], f[:, t, :], ALU.mult)
            phase.end()
            attend(False, 0, *att_views(o, 2 * P), vec("sinks1"), const("mask1"))
            phase.end()
            r0 = plan["merge"][0]
            with dve.Fori(0, 8) as i:
                for n in range(2):
                    dve.wait_ge(full[2 * n + 1], r0 + 1 + i)
                    dve.wait_ge(free[2 * n], r0 + 1 + i)
                    nc.vector.tensor_tensor(tmp[:, 2 + n, :], tmp[:, n, :], bank[2 * n + 1][:, :], ALU.mult).then_inc(free[2 * n + 1], 1)
                dve.drain()
                nc.vector.tensor_tensor(merged[:, bass.ds(i, 1), :].rearrange("p a t -> p (a t)"), tmp[:, 2, :], tmp[:, 3, :],
                                        ALU.add)
                dve.drain().then_inc(mrg_ready, 1)
            post_norm(vec("mix_post_g"))
            phase.end()
            ffn(2, "ffn2_pre_g", half_g[:, 1, :])
            for l in range(2):
                for w, g in ((0, "norm_mix"), (1, "norm_ffn")):
                    for st in range(2):
                        nc.vector.scalar_tensor_tensor(amod[:, l, w, st, :], mod[:, l, 3 * w + 1, :, st], 1.0,
                                                       vec(g)[:, l * KT:(l + 1) * KT], ALU.add, ALU.mult)
            dve.drain()

            mod_norm(0, 0, True)
            phase.end()
            w2 = vec("conv_w2")
            for t in range(4):
                bt, ct, ht, yc = pt[:, 4 + t, :], pt[:, 8 + t, :], pt[:, 12 + t, :], yt[:, 4 + t, :]
                nc.vector.tensor_tensor(ct, ct, ht, ALU.mult)
                dve.drain()
                nc.vector.tensor_scalar(yc, ct, w2[:, 4 + t:5 + t], None, ALU.mult)
                dve.drain()
                for a, n in ((0, S), (S, C)):
                    nc.vector.scalar_tensor_tensor(yc[:, a + 1:a + n], ct[:, a:a + n - 1], w2[:, t:t + 1], yc[:, a + 1:a + n], ALU.mult, ALU.add)
                dve.drain()
                for a, n in ((0, S), (S, C)):
                    nc.vector.scalar_tensor_tensor(yc[:, a:a + n - 1], ct[:, a + 1:a + n], w2[:, 8 + t:9 + t], yc[:, a:a + n - 1], ALU.mult, ALU.add)
                dve.drain()
                nc.vector.tensor_tensor(yc, yc, bt, ALU.mult)
            phase.end()

            def gated_add(name, l, its, context):
                r0 = plan[name][0]
                g1 = mod[:, l, 2, :, :].rearrange("p k c -> p (k c)")
                with dve.Fori(0, its) as i:
                    for j in range(4):
                        dve.wait_ge(full[j], r0 + 1 + i)
                        if context:
                            k, st = 2 * i + j // 2, j % 2
                        else:
                            k, st = 4 * i + j, 0
                        x, n = (lat, S) if st == 0 else (cxt, C)
                        xv = x[:, bass.ds(k, 1), :].rearrange("p a t -> p (a t)")
                        nc.vector.tensor_copy(small[:, 64 + j:65 + j], g1[:, bass.ds(2 * k + st, 1)])
                        dve.drain()
                        nc.vector.scalar_tensor_tensor(xv, bank[j][:, 0:n], small[:, 64 + j:65 + j], xv, ALU.mult,
                                                       ALU.add).then_inc(free[j], 1)

            gated_add("even_out", 0, 4, True)
            phase.end()
            mod_norm(0, 1, True)
            moe_layer(0)

            mod_norm(1, 0, True)
            heads = [qt2[:, x, :] for x in range(KT)] + [kt2[:, x, a:b] for x in range(2) for a, b in ((0, S), (S, SC))]
            for x, a in enumerate(heads):
                n = a.shape[1]
                dve.wait_ge(qstd_ready, x + 1)
                nc.vector.reciprocal(tmp[:, 2 + x % 2, 0:n], tmp[:, 2 + x % 2, 0:n])
                dve.drain()
                nc.vector.scalar_tensor_tensor(a, a, vec("q_g") if x < KT else vec("k_g"), tmp[:, 2 + x % 2, 0:n], ALU.mult,
                                               ALU.mult).then_inc(qn_ready, 1)
            dve.drain()
            rope([qt2[:, x, :] for x in range(KT)] + [kt2[:, x, 0:S] for x in range(2)], const("cos2"), const("sin2"), 10)
            phase.end()
            attend(True, 32, *att_views(att2, 5 * P), vec("sinks2"), const("mask2"))
            phase.end()
            gated_add("wo", 1, 2, False)
            phase.end()
            mod_norm(1, 1, False)
            moe_layer(1)
            dve.drain().then_inc(lat_final, 1)

        @block.gpsimd
        def _(pool):
            phase = Phase(pool)

            def attend(u0, qt, qs):
                with pool.Fori(0, ROUNDS) as i:
                    for m in range(UNITS):
                        n, kv = m % LT, m // LT
                        pool.wait_ge(s_full, u0 + m + 1 + 8 * i)
                        nc.gpsimd.tensor_copy(qs[:, kv, n * P:(n + 1) * P],
                                              qt[:, bass.ds(4 * kv + i, 1), n * P:(n + 1) * P].rearrange("p a t -> p (a t)")
                                              ).then_inc(q_staged, 1)

            def moe_layer(l):
                q, nt = moe[l], TILES_OF[l]
                table = d["table"][l]
                nc.gpsimd.memset(tab_u[:, :], 0)
                nc.gpsimd.iota(tok_u[:, :], pattern=[[P, TT]], base=0, channel_multiplier=1)
                pool.drain()
                pool.dma_start(table.rearrange("(p n) o -> p (n o)", n=TABW), tab_u[:, :]).then_inc(q["zeros"], 16)
                for t in range(nt):
                    pool.wait_ge(q["xt_cp"], 2 * (t + 1))
                    pool.dma_start(d["rows"][l][t * P:(t + 1) * P, :], xg).then_inc(q["xt_out"], 16)
                pool.wait_ge(q["zeros"], 16)
                pool.wait_ge(q["pos"], 1)
                for t in range(nt):
                    for x in range(2):
                        pool.indirect_dma_start(out=table, out_offset=bass.IndirectOffsetOnAxis(ap=pos_u[:, 1, x, t:t + 1], axis=0),
                                                in_=tok_u[:, t:t + 1], in_offset=None).then_inc(q["scatter"], 16)
                pool.wait_ge(q["scatter"], 32 * nt)
                pool.dma_start(tab_u[:, :], table.rearrange("(p n) o -> p (n o)", n=TABW)).then_inc(q["table"], 16)
                pool.wait_ge(q["table"], 16)
                pool.wait_ge(q["xt_out"], 16 * nt)

                def gather(b, first=False):
                    if not first:
                        pool.wait_ge(q["xt_full"], b)
                    nc.gpsimd.tensor_copy(idx_u[:, :], tab_u[:, bass.ds(b, 1)])
                    pool.drain()
                    pool.indirect_dma_start(out=xg[0:MB, :], out_offset=None, in_=d["rows"][l],
                                            in_offset=bass.IndirectOffsetOnAxis(ap=idx_u[:, :], axis=0)).then_inc(q["gathered"], 16)

                phase.end()
                last = pool.value_load(exp_i[0:1, TABW:TABW + 1], min_val=2, max_val=NBMAX - 1)
                gather(0, first=True)
                gather(1)
                gather(2)
                with pool.Fori(2, last + 1) as b:
                    gather(b + 1)
                phase.end()
                for t in range(nt):
                    if t > 0:
                        pool.wait_ge(q["sum_ready"], t)
                    for x in range(2):
                        pool.indirect_dma_start(out=yget[x], out_offset=None, in_=d["yb"][l],
                                                in_offset=bass.IndirectOffsetOnAxis(ap=pos_u[:, 0, x, t:t + 1], axis=0)
                                                ).then_inc(q["got"], 16)
                phase.end()

            nc.gpsimd.memset(zeros[:, :], 0.0)
            pool.drain().then_inc(zeros_ready, 1)
            phase.end()
            phase.end()
            attend(0, qt1, att_views(o, 2 * P)[0])
            phase.end()
            for x in range(5):
                phase.end()
            moe_layer(0)
            phase.end()
            attend(32, qt2, att_views(att2, 5 * P)[0])
            phase.end()
            phase.end()
            moe_layer(1)


def tiles(w):
    n = w.shape[1] // P
    t = w.reshape(KT, P, n, P).transpose(2, 1, 0, 3).reshape(n // 2, 2, P, KT * P)
    return t.transpose(0, 2, 1, 3).reshape(n // 2, P, CHUNK)


def mixed(*ws):
    n = ws[0].shape[1] // P
    return tiles(np.stack([w.reshape(D, n, P) for w in ws], 2).reshape(D, -1))


def moving(w):
    return w.reshape(KT, P, C).transpose(1, 0, 2).reshape(1, P, CHUNK)


def columns(v):
    return np.ascontiguousarray(v).reshape(-1, P).T


def fields(named, spec):
    return np.ascontiguousarray(np.concatenate([named[n].reshape(P, w) for n, w in spec], 1))


def rope_table(pos, freqs):
    ang = pos.astype(np.float32)[:, None] * freqs.astype(np.float32)[None, :]
    return np.cos(ang), np.sin(ang)


def constants():
    p = np.arange(P)
    out = {"ident": np.eye(P), "ones": np.ones((P, P)), "headsum": p[:, None] // HD == p[None, :] // HD,
           "swap1": p[:, None] == (p ^ (HD // 2))[None, :], "swap2": p[:, None] == (p ^ (HD // 4))[None, :],
           "before": p[:, None] < p[None, :]}
    i, s1, s2 = p[:, None], np.arange(2 * P)[None, :], np.arange(3 * P)[None, :]
    out["mask1"] = np.where((P + i - s1 >= 0) & (P + i - s1 < P), 0.0, NEG)
    out["mask2"] = np.where(np.abs(s2 - P - i) <= P, 0.0, NEG)
    half = HD // 2
    c, s = rope_table(np.arange(S), np.float32(10000.0) ** (-np.arange(half, dtype=np.float32) / half))
    out["cos1"], out["sin1"] = c.T[p % half], s.T[p % half] * np.where(p % HD < half, -1.0, 1.0)[:, None]
    n = HD // 4
    freqs = np.float32(10000.0) ** (-np.arange(n, dtype=np.float32) / n)
    t = np.arange(S)
    by_axis = [rope_table(pos, freqs) for pos in (t // 64, t % 64)]
    axis = (p % HD) // half
    out["cos2"] = np.stack([by_axis[a][0][:, x % n] for a, x in zip(axis, p)])
    out["sin2"] = np.stack([by_axis[a][1][:, x % n] * (-1.0 if x % half < n else 1.0) for a, x in zip(axis, p)])
    out["eps"] = np.full((P, 1), EPS)
    out["gdesc"] = np.tile(np.arange(NG, 0, -1), (P, 1))
    out["edesc"] = np.tile(np.arange(NE, 0, -1), (P, 1))
    e = np.arange(NE)
    out["tri_lt"], out["tri_le"] = np.tile(e[:, None] < e, (P // NE, 1)), np.tile(e[:, None] <= e, (P // NE, 1))
    out["blocks"] = np.tile(np.arange(TABW), (P, 1))
    out["thr"] = np.tile(MB * np.arange(16), (P, 1))
    return fields({k: np.asarray(v, np.float32) for k, v in out.items()}, CONSTS)


def fourier():
    def pair(n):
        ang = 2 * np.pi * ((np.arange(n)[:, None] * np.arange(n)[None, :]) % n) / n
        return np.cos(ang) / np.sqrt(n), np.sin(ang) / np.sqrt(n)

    def rows(m):
        return m.reshape(-1, P, m.shape[1]).transpose(1, 0, 2).reshape(P, -1)

    (cd, sd), (cc, sc), (cl, sl) = pair(P), pair(C), pair(S)
    out = {"cs_d": np.concatenate([cd, sd], 1), "c_ctx": rows(cc), "s_ctx": rows(-sc), "c_lat": rows(cl), "s_lat": rows(-sl)}
    return fields({k: v.astype(np.float32) for k, v in out.items()}, DFT)


def kernel(**inputs):
    import concourse.bacc as bacc
    from concourse.bass_utils import run_bass_kernel_spmd

    x = {k: np.asarray(v) for k, v in inputs.items()}
    order = np.concatenate([np.arange(h * HD, (h + 1) * HD) for h in HEADS])
    w_in, w_in2, qkv = x["w_in"][0], x["w_in_even_2"][0], x["w_qkv_2"][0]
    a = 2 * D + D
    kvw = NH // 4 * HD
    gate, xb, wq = w_in[:, 0:D], w_in[:, D:2 * D], w_in[:, 2 * D:a][:, order]
    wk, wv, g_lru, g_att = w_in[:, a:a + kvw], w_in[:, a + kvw:a + 2 * kvw], w_in[:, a + 2 * kvw:a + 2 * kvw + D], w_in[:, a + 2 * kvw + D:]

    def ffn(n):
        gu = x[f"ffn{n}_w_gu"][0]
        g, u = (t.reshape(D, FF // 256, 256) for t in (gu[:, :FF], gu[:, FF:]))
        return tiles(np.stack([g, u], 2).reshape(D, 2 * FF))

    def down(n):
        return x[f"ffn{n}_w_down"][0].reshape(FT, P, KT, P).transpose(2, 1, 0, 3).reshape(KT, P, SLOT)

    w = np.concatenate([ffn(1), tiles(xb), tiles(wq), tiles(wk), moving(wv), tiles(gate),
                        mixed(g_lru, x["w_proj_lru"][0], g_att, x["w_proj_attn"][0][order]), tiles(x["w_out"][0]), ffn(2),
                        tiles(w_in2), tiles(x["w_out_even_2"][0]), tiles(qkv[:, 0:D][:, order]), tiles(qkv[:, D:D + kvw]),
                        moving(qkv[:, D + kvw:]), tiles(x["w_o_2"][0][order])])
    lru_w = np.zeros((2, KT, 2, HD, 2, HD), np.float32)
    for g, n in enumerate(("lru_w_a", "lru_w_x")):
        for h in range(2):
            lru_w[g, :, h, :, h, :] = x[n][0].reshape(KT, 2, HD, HD)[:, h]
    route_w = np.concatenate([x["w_router_g_2"], x["w_router_e_2"]], 2)
    route_b = np.concatenate([x["b_router_g_2"], x["b_router_e_2"]], 1)
    named = {n: columns(x[n][0]) for n in ("ffn1_pre_g", "ffn1_post_g", "mix_pre_g", "mix_post_g", "ffn2_pre_g", "ffn2_post_g",
                                           "conv_w", "conv_b", "lru_b_a", "lru_b_x", "lru_lambda")}
    named |= {"norm_mix": columns(x["norm_mix_g_2"]), "norm_ffn": columns(x["norm_ffn_g_2"]), "conv_w2": columns(x["conv_w_2"][0]),
              "q_g": np.tile(x["q_norm_g_2"][0], 2)[:, None], "k_g": np.tile(x["k_norm_g_2"][0], 2)[:, None],
              "cond": np.stack([columns(x["c_2"][0]), columns(x["c_ctx_2"])], 2),
              "b_mod": np.repeat(columns(x["b_mod_2"])[:, :, None], 2, 2),
              "sinks1": np.tile(x["attn_sinks"][0][HEADS], (P, 1)), "sinks2": np.tile(x["sink_logit_2"][0][HEADS], (P, 1)),
              "route_b": np.tile(route_b[None, :, None, :], (P, 1, TT, 1))}
    arrays = {"consts": constants(), "dft": fourier(), "vecs": fields(named, VECS),
              "x": x["x"][0].T.reshape(KT, P, S).transpose(1, 0, 2), "ctx": x["ctx_2"][0].T.reshape(KT, P, C).transpose(1, 0, 2),
              "w": w, "wm": np.concatenate([tiles(x["w_mod_2"][0]), tiles(x["w_mod_2"][1])]), "wd": np.concatenate([down(1), down(2)]),
              "lru_w": lru_w.reshape(2, KT, P, P).transpose(2, 0, 1, 3),
              "wr": route_w.reshape(2, KT, P, ROUTE).transpose(0, 2, 1, 3), "w1": x["w1_2"], "w3": x["w3_2"], "w2": x["w2_2"]}
    arrays = {f"in_{n}": np.ascontiguousarray(v) for n, v in arrays.items()}
    nc = bacc.Bacc("TRN2", target_bir_lowering=False, num_devices=1)
    d = {n[3:]: nc.dram_tensor(n, v.shape, F32, kind="ExternalInput").ap() for n, v in arrays.items()}
    d["out"] = nc.dram_tensor("out", (P, KT, S), F32, kind="ExternalOutput").ap()
    d["rows"] = [nc.dram_tensor(f"rows{l}", (t, D), F32, kind="Internal").ap() for l, t in enumerate((SC, S))]
    d["yb"] = [nc.dram_tensor(f"yb{l}", (NBMAX * MB, D), F32, kind="Internal").ap() for l in range(2)]
    d["table"] = [nc.dram_tensor(f"table{l}", (MB * TABW, 1), U32, kind="Internal").ap() for l in range(2)]
    program(nc, d)
    r = run_bass_kernel_spmd(nc, [arrays], core_ids=[0])
    out = np.asarray(r.results[0]["out"])
    return np.ascontiguousarray(out.transpose(2, 1, 0).reshape(1, S, D))
```

```python
from contextlib import ExitStack

import numpy as np

import concourse.bass as bass
from concourse import mybir

F32 = mybir.dt.float32
F32R = mybir.dt.float32r
I32 = mybir.dt.int32
U32 = mybir.dt.uint32
ACT = mybir.ActivationFunctionType
ALU = mybir.AluOpType
AX = mybir.AxisListType

P = 128
D = 1024
KT = D // P
S = 512
C = 256
SC = S + C
FF = 2816
FT = FF // P
HD = 64
NH = 16
PAIRS = NH // 2
EPS = 1e-6
NE = 32
NG = 4
EF = 512
MB = 64
NBMAX = -(-2 * SC // MB) + NE
TABW = NBMAX + 1
CONV1 = 4
LRU_C = 8.0
SLOT = FT * P
CHUNK = 2 * KT * P
PIECE = KT * P
DOWN_PIECES = -(-SLOT // PIECE)
GU_ROUNDS = FF // P // 2
FFN_PIECES = 4 * GU_ROUNDS + KT * DOWN_PIECES
MERGE_PIECES = 4 * KT
PIECES_BEFORE, _n = {}, 0
for _name, _pieces in ((1, FFN_PIECES), ("mixer", 2 * KT), ("merge", MERGE_PIECES), (2, FFN_PIECES), ("even_in", 2 * KT),
                       ("even_out", KT), ("qkv", KT + 4)):
    PIECES_BEFORE[_name] = _n
    _n += _pieces
ROUTE = NG + NE
TT = SC // P
LT = S // P
ZERO = 256
XPAD = S + CONV1 - 1
QUAD = 32
MODC = 512
SCALE = HD ** -0.5
NEG = -1e30

HEADS = [8 * (j // 4) + j % 4 + 4 * s for j in range(PAIRS) for s in range(2)]

MOD_GROUPS = 2 * 6 * D // MODC // 2
DENSE = [("gu1", 22, 11), ("down1", 8, 2), ("xbr", 4, 2), ("q1", 4, 2), ("kv1", 2, 1),
         ("gate", 4, 2), ("merge", 16, 8), ("out1", 4, 2), ("gu2", 22, 11), ("down2", 8, 2),
         ("even_in", 8, 8), ("even_out", 4, 4), ("q2", 4, 2), ("kv2", 2, 2), ("wo", 4, 2)]


def dense_plan():
    rounds, loads, plan, at = 1, 0, {}, {"w": 0, "d": 0}
    for name, chunks, n in DENSE:
        kind = "d" if name.startswith("down") else "w"
        plan[name] = (rounds, loads, at[kind])
        rounds, loads = rounds + n, loads + chunks // 2
        at[kind] += chunks
    return plan


VECS = [("ffn1_pre_g", 8), ("ffn1_post_g", 8), ("mix_pre_g", 8), ("mix_post_g", 8), ("ffn2_pre_g", 8),
        ("ffn2_post_g", 8), ("conv_w", 32), ("conv_b", 8), ("lru_b_a", 8), ("lru_b_x", 8), ("lru_lambda", 8),
        ("norm_mix", 16), ("norm_ffn", 16), ("conv_w2", 12), ("q_g", 1), ("k_g", 1), ("cond", 16), ("b_mod", 192),
        ("sinks1", 16), ("sinks2", 16), ("route_b", 2 * TT * ROUTE)]
CONSTS = [("ident", 128), ("ones", 128), ("swap1", 128), ("swap2", 128), ("headsum", 128), ("before", 128),
          ("mask1", 256), ("mask2", 384), ("cos1", S), ("sin1", S), ("cos2", S), ("sin2", S),
          ("eps", 1), ("quads", 2), ("gdesc", NG), ("edesc", NE), ("tri_lt", NE), ("tri_le", NE), ("count", max(TABW, MB)), ("tok", TT), ("thr", 16)]
DFT = [("cs_d", 2 * P), ("c_ctx", 2 * C), ("s_ctx", 2 * C), ("c_lat", 4 * S), ("s_lat", 4 * S)]


def offsets(fields):
    at, out = 0, {}
    for name, n in fields:
        out[name] = (at, n)
        at += n
    return out, at


VEC_AT, VEC_N = offsets(VECS)
CONST_AT, CONST_N = offsets(CONSTS)
DFT_AT, DFT_N = offsets(DFT)


def program(nc, d):
    ctx = ExitStack()
    with ctx:
        def sb(name, shape, dt=F32):
            return ctx.enter_context(nc.sbuf_tensor(name, shape, dt))

        def sem(name):
            return ctx.enter_context(nc.semaphore(name))

        plan = dense_plan()

        BIG = 22560
        with ExitStack() as plain:
            def shared(name, n):
                return plain.enter_context(nc.sbuf_tensor(name, [P, n], F32))
            slot = [shared(f"slot{s}", SLOT) for s in range(2)]
            ar_u = shared("ar_u", KT * SC)
            ar_f = shared("ar_f", KT * S)
            cxt_s = shared("cxt", KT * C)
            big = shared("big", BIG)
        w_low = [sb(f"w_low{s}", [P, SLOT], F32R) for s in range(2)]
        u_split = sb("u_split", [P, KT * SC], F32R)
        u_high = u_split[:, 0:KT * S].rearrange("p (k t) -> p k t", k=KT)
        u_low = sb("u_low", [P, KT, S], F32R)
        w_high = sb("w_high", [P, 2, PIECE], F32R)
        act_high = sb("act_high", [P, FT, S], F32R)
        act_low = sb("act_low", [P, FT, S], F32R)
        sb("big_rest", [P, BIG - 2 * FT * S])
        cxt = cxt_s[:, :].rearrange("p (k t) -> p k t", k=KT)

        lat = sb("lat", [P, KT, S])
        vecs = sb("vecs", [P, VEC_N])
        consts = sb("consts", [P, CONST_N])
        mod = sb("mod", [P, 2, 6, KT, 2])
        amod = sb("amod", [P, 2, 2, 2, KT])
        half_g = sb("half_g", [P, 2, KT])
        lam8 = sb("lam8", [P, 8, KT])
        silu_c = sb("silu_c", [P, KT, QUAD])
        small = sb("small", [P, 96])

        rs = sb("rs", [P, SC])
        tmp = sb("tmp", [P, 4, S])

        def vec(name):
            a, n = VEC_AT[name]
            return vecs[:, a:a + n]

        def const(name):
            a, n = CONST_AT[name]
            return consts[:, a:a + n]

        def part(at, shape):
            n = int(np.prod(shape))
            assert at + n <= BIG, (at, shape)
            v = big[:, at:at + n]
            names = "abcd"[:len(shape)]
            return v.rearrange(f"p ({' '.join(names)}) -> p {' '.join(names)}",
                               **{c: x for c, x in zip(names, shape)}) if len(shape) > 1 else v

        ident, ones = const("ident"), const("ones")
        u1 = ar_u[:, 0:KT * S].rearrange("p (k t) -> p k t", k=KT)
        u2 = ar_u[:, :].rearrange("p (k t) -> p k t", k=KT)
        f = ar_f[:, :].rearrange("p (k t) -> p k t", k=KT)
        mslot = ar_u[:, KT * S:KT * S + CHUNK]
        mrow = tmp[:, 2, :]
        xbr = part(0, [KT, XPAD])
        xc = part(KT * XPAD, [KT, S])
        o = KT * (XPAD + S)
        gr = part(o, [KT, S])
        gi = part(o + KT * S, [KT, S])
        qt1 = part(o + 2 * KT * S, [KT, S])
        kt1 = part(o + 3 * KT * S, [2, S])
        qk1 = part(o + 2 * KT * S, [KT + 2, S])
        v1 = part(o + 3 * KT * S + 2 * S, [LT, C])
        flat = [v[:, :, :].rearrange("p k t -> p (k t)") for v in (act_high, act_low)]

        def split_view(at):
            v = flat[at // (FT * S)]
            at %= FT * S
            return v[:, at:at + KT * S].rearrange("p (k t) -> p k t", k=KT)
        lru_low = split_view(KT * XPAD)
        u1_low, att_low = u_high, u_low
        u1_high, lru_high, att_high = split_view(0), split_view(o + KT * S), split_view(o + 2 * KT * S)
        p1_high = split_view(o + KT * S)
        p1_low = [flat[a // (FT * S)][:, a % (FT * S):a % (FT * S) + S] for a in
                  [o + k * S for k in range(5)] + [FT * S + k * S for k in range(2)] + [o + 3 * KT * S]]
        assert o + 5 * S <= FT * S and FT * S + 2 * S <= o + KT * S
        lru_w = ar_u[:, KT * S:KT * S + 2 * KT * P].rearrange("p (g k c) -> p g k c", g=2, k=KT)
        merged = gr
        qt2 = part(0, [KT, S])
        kt2 = part(KT * S, [2, SC])
        v2 = part(KT * S + 2 * SC, [TT, C])
        att2 = KT * S + 2 * SC + TT * C

        def att_views(at, keys):
            n = 2 * S
            return (part(at, [2, S]), part(at + n, [4, 2, keys]), part(at + n + 8 * keys, [2, 2 * keys]),
                    part(at + n + 12 * keys, [2, P]))

        pt = part(0, [16, SC])
        yt = part(16 * SC, [8, SC])
        ac = part(24 * SC, [TT, 2 * P])
        u2_low = u_split[:, :].rearrange("p (k t) -> p k t", k=KT)
        y_at = 16 * SC - FT * S
        y_low = flat[1][:, y_at:y_at + KT * SC].rearrange("p (k t) -> p k t", k=KT)
        u2_high = y_low
        y_high = flat[0][:, 0:KT * SC].rearrange("p (k t) -> p k t", k=KT)
        ring_at = 24 * SC - FT * S, FT * S - PIECE
        assert TT * 2 * P >= PIECE and 24 * SC + TT * 2 * P + DFT_AT["c_lat"][0] <= FT * S + ring_at[1]
        even_ring = [flat[1][:, a:a + PIECE] for a in ring_at]
        ffn_ring = [w_high[:, h, :] for h in range(2)]
        dft = part(24 * SC + TT * 2 * P, [DFT_AT["c_lat"][0]])
        csd = dft[:, 0:2 * P]
        c_ctx = dft[:, 2 * P:2 * P + 2 * C].rearrange("p (l t) -> p l t", l=2)
        s_ctx = dft[:, 2 * P + 2 * C:2 * P + 4 * C].rearrange("p (l t) -> p l t", l=2)
        c_lat = ar_f[:, 0:4 * S].rearrange("p (l t) -> p l t", l=4)
        s_lat = tmp[:, :, :]
        assert att2 <= FT * S and KT * SC <= ring_at[0]
        h_high, h_low = flat[1][:, 0:KT * SC].rearrange("p (k t) -> p k t", k=KT), u2_low
        wslot = [part(2048 * c, [2048]) for c in range(6)]
        m0 = 6 * 2048
        xg = part(m0, [D])
        xT = part(m0 + D, [KT, MB])
        hsil = part(m0 + 2 * D, [EF])
        hmul = part(m0 + 2 * D + EF, [EF])
        hT = part(m0 + 3 * D, [EF // P, MB])
        ysb = part(m0 + 3 * D + EF, [EF])
        yrows = [[part((2 * t + x) * D, [D]) for x in range(2)] for t in range(TT)]
        row_bufs = [xg] + [part(m0 + 4 * D + EF + n * D, [D]) for n in range(2)]
        rt = m0 + 7 * D + EF
        lg = part(rt, [TT, ROUTE])
        lgT = part(m0 + D, [SC])
        ge = part(rt + 216, [TT, NG])
        gsel = part(rt + 240, [TT, NG])
        ecand = part(rt + 264, [TT, NE])
        elog = part(rt + 456, [TT, NE])
        oh = [part(rt + 648 + 192 * n, [TT, NE]) for n in range(2)]
        both = part(rt + 1032, [TT, NE])
        rank = part(rt + 1224, [TT, NE])
        over = part(rt + 1416, [TT, NE])
        wr = part(rt + 1608, [KT, ROUTE])
        scal = part(rt + 1896, [12, TT])
        nbb = part(rt + 1968, [P])
        cmpb = part(rt + 2096, [TABW + 1])
        col = part(rt + 2096 + TABW + 1, [8])
        pos_f = part(rt + 2200, [2, 2, TT])
        place = part(rt + 2200 + 4 * TT, [2, TT])
        at_place = part(m0 + 2 * D, [2 * TT, MB])
        in_block = part(m0 + 2 * D + 2 * TT * MB, [2 * TT, TABW])
        pos_u = sb("pos_u", [P, 2, TT], U32)
        tab_u = sb("tab_u", [MB, TABW], U32)
        zeros = sb("zeros", [P, ZERO])
        idx_u = sb("idx_u", [MB, 1], U32)
        exp_i = sb("exp_i", [1, TABW + 1], I32)

        bank = [ctx.enter_context(nc.psum_tensor(f"bank{i}", [P, 512], F32)) for i in range(8)]

        loaded = sem("loaded")
        lru_loaded, dft_loaded, wr_loaded = sem("lru_loaded"), sem("dft_loaded"), sem("wr_loaded")
        wload = [sem(f"wload{s}") for s in range(2)]
        full = [sem(f"full{j}") for j in range(4)]
        free = [sem(f"free{j}") for j in range(4)]
        phase_done = sem("phase_done")
        mod_load, mod_full, mod_free, mrow_ready, mod_turned = (sem(n) for n in ("mod_load", "mod_full", "mod_free", "mrow_ready", "mod_turned"))
        zeros_ready = sem("zeros_ready")
        sq_ready, ssum_ready, std_ready, u_ready = (sem(n) for n in ("sq_ready", "ssum_ready", "std_ready", "u_ready"))
        cond_ready, cxt_loaded = sem("cond_ready"), sem("cxt_loaded")
        wh_ready, wh_used, wl_ready = sem("wh_ready"), sem("wh_used"), sem("wl_ready")
        mh_ready, mu_ready, mx_ready = (sem(n) for n in ("mh_ready", "mu_ready", "mx_ready"))
        un_ready, uh_ready, ah_ready, act_ready = (sem(n) for n in ("un_ready", "uh_ready", "ah_ready", "act_ready"))
        xbr_ready, xc_ready, raw_ready = sem("xbr_ready"), sem("xc_ready"), sem("raw_ready")
        lin_full, lin_free = sem("lin_full"), sem("lin_free")
        gates_ready, decay_ready, msq_ready, mult_ready = (sem(n) for n in ("gates_ready", "decay_ready", "msq_ready", "mult_ready"))
        gate_ready = sem("gate_ready")
        rope_full, rope_free = sem("rope_full"), sem("rope_free")
        qsq_ready, qsum_full, qstd_ready, qn_ready = (sem(n) for n in ("qsq_ready", "qsum_full", "qstd_ready", "qn_ready"))
        q_staged, s_full, s_evac, max_ready = (sem(n) for n in ("q_staged", "s_full", "s_evac", "max_ready"))
        exp_ready, t_full, t_evac = (sem(n) for n in ("exp_ready", "t_full", "t_evac"))
        o_full, y_norm, turn_full, o_evac = (sem(n) for n in ("o_full", "y_norm", "turn_full", "o_evac"))
        ac_full, ac_ready, dft_full, dft_evac, conv_ready = (sem(n) for n in ("ac_full", "ac_ready", "dft_full", "dft_evac", "conv_ready"))
        mrg_ready = sem("mrg_ready")
        routing = {n: sem(n) for n in ("lg_full", "lg_copied", "logits", "gexp_in", "gexp", "eexp_in", "eexp", "onehot", "counts", "nblk", "starts", "cmp",
                                       "exp_row", "expert", "ranks", "tab_in", "tab_full", "table")}
        moe = [routing | {n: sem(f"{n}_{l}") for n in
                          ("xt_tr", "xt_cp", "xt_out", "gathered", "xt_full", "xt_ready", "gate_full",
                           "up_full", "sg_ready", "h_ready", "htp_full", "ht_ready", "y_ready", "y_written", "y_last", "got0", "got1",
                           "sum_ready", "sum_tr", "sum_read", "w2_done")} for l in range(2)]
        mload = [[sem(f"mload{c}_{l}") for c in range(6)] for l in range(2)]
        mdone = [[sem(f"mdone{c}_{l}") for c in range(2)] for l in range(2)]
        yb_zeroed, stored = sem("yb_zeroed"), sem("stored")

        block = ctx.enter_context(nc.Block())
        TILES_OF = [TT, LT]
        EARLY_ROWS = 3

        class Phase:
            def __init__(self, eng):
                self.eng, self.n = eng, 0

            def end(self):
                self.n += 1
                self.eng.drain().then_inc(phase_done, 1)
                self.eng.wait_ge(phase_done, 4 * self.n)

        def att_tiles(second, n):
            lo, hi = max(n - 1, 0), (min(n + 1, LT - 1) if second else n)
            return lo, hi + 1, (lo - n + 1) * P

        def att_groups(second, n):
            lo, hi, _ = att_tiles(second, n)
            per = hi - lo + (2 if second else 0)
            return per, -(-2 * per // 4)

        UNITS = 2 * LT
        ROUNDS = PAIRS // 2

        def unit_at(i, x):
            return i + x // UNITS, x % UNITS

        def att_schedule(eng, order, last):
            def steps(i, first):
                for m in range(UNITS):
                    for delay, step in order:
                        if not (first and m < delay):
                            step(*unit_at(i, m - delay))
            steps(0, True)
            with eng.Fori(1, ROUNDS) as i:
                steps(i, False)
            for m in range(UNITS, UNITS + last):
                for delay, step in order:
                    if m - delay < UNITS:
                        step(*unit_at(ROUNDS - 1, m - delay))

        HEAD_TILES = [qt2[:, x, :] for x in range(KT)] + [kt2[:, x, a:b] for x in range(2) for a, b in ((0, S), (S, SC))]
        ROTATED = list(range(KT + 1)) + [KT + 2]
        ROPE_LAG = 2

        def groups_before(second, i, m):
            per_round = 2 * sum(att_groups(second, n)[1] for n in range(LT))
            at = 2 * ROUNDS * LT if second else 0
            return at + sum(att_groups(second, x % LT)[1] for x in range(m)) + per_round * i

        def down_piece(T, p):
            return slice(p * PIECE, min((p + 1) * PIECE, SLOT)), (DOWN_PIECES * T + p) % 2

        @block.sync
        def _(sp):
            for dst, src in ((consts[:, :], d["consts"]), (vecs[:, :], d["vecs"]), (lat[:, :, :], d["x"])):
                sp.dma_start(dst, src).then_inc(loaded, 16)

            def load_mod(n):
                sp.wait_ge(mod_full, n + 1)
                sp.dma_start(mslot, d["wm"][bass.ds(n, 1)].rearrange("a p n -> (a p) n")).then_inc(mod_load, 16)

            def stream(name, its, mod=None):
                r0, l0, c0 = plan[name]
                with sp.Fori(0, its) as i:
                    for s in range(2):
                        sp.wait_ge(full[2 * s + 1], r0 + i)
                        sp.dma_start(slot[s][:, 0:CHUNK],
                                     d["w"][bass.ds(c0 + 2 * i + s, 1)].rearrange("a p n -> (a p) n")).then_inc(wload[s], 16)
                        if mod is not None:
                            load_mod(2 * mod + s + 2 * i)

            def stream_down(name):
                r0, l0, c0 = plan[name]
                with sp.Fori(0, 2) as i:
                    for t in range(4):
                        s = t % 2
                        if t < 2:
                            sp.wait_ge(full[2 * s + 1], r0 + i)
                        else:
                            sp.wait_ge(full[2 * s], r0 + i + 1)
                        sp.dma_start(slot[s][:, :],
                                     d["wd"][bass.ds(c0 + 4 * i + t, 1)].rearrange("a p n -> (a p) n")).then_inc(wload[s], 16)

            def stream_paired(name, its):
                r0, l0, c0 = plan[name]
                with sp.Fori(0, its) as i:
                    for s in range(2):
                        if s == 0:
                            sp.wait_ge(full[1], r0)
                        sp.wait_ge(full[3], r0 + 2 * i - 1 + s)
                        sp.dma_start(slot[s][:, 0:CHUNK],
                                     d["w"][bass.ds(c0 + 2 * i + s, 1)].rearrange("a p n -> (a p) n")).then_inc(wload[s], 16)

            def stream_experts(l):
                q = moe[l]
                w1 = d["w1"].rearrange("l e (p h k) f -> (l e) h p k f", h=2, p=P)
                w3 = d["w3"].rearrange("l e (p h k) f -> (l e) h p k f", h=2, p=P)
                w2 = d["w2"].rearrange("l e (p h k) f -> (l e) h p k f", h=2, p=P)

                def load(c, w, e, half):
                    dst = wslot[c].rearrange("p (k f) -> p k f", k=4 if c < 4 else 2)
                    sp.dma_start(dst, w[bass.ds(e + l * NE, 1), half].rearrange("e p k f -> (e p) k f")).then_inc(mload[l][c], 16)

                def up(b, first=False):
                    e = sp.value_load(exp_i[0:1, bass.ds(b, 1)], min_val=0, max_val=NE - 1)
                    for c in (0, 2, 1, 3):
                        if not first:
                            sp.wait_ge([mdone[l][0], q["gate_full"], mdone[l][1], q["up_full"]][c], b)
                        load(c, w1 if c < 2 else w3, e, c % 2)

                def down(b, first=False):
                    e = sp.value_load(exp_i[0:1, bass.ds(b, 1)], min_val=0, max_val=NE - 1)
                    if not first:
                        sp.wait_ge(q["w2_done"], b)
                    for c in range(4, 6):
                        load(c, w2, e, c % 2)

                sp.wait_ge(q["expert"], l + 1)
                last = sp.value_load(exp_i[0:1, TABW:TABW + 1], min_val=2, max_val=NBMAX - 1)
                up(0, first=True)
                down(0, first=True)
                up(1)
                down(1)
                with sp.Fori(2, last + 1) as b:
                    up(b)
                    down(b)

            load_mod(0)
            load_mod(1)
            stream("gu1", 11, 1)
            stream_down("down1")
            stream("xbr", 2)
            stream("q1", 2)
            stream("kv1", 1)
            stream("gate", 2)
            sp.wait_ge(zeros_ready, 1)
            runs = NBMAX * MB // P * (D // ZERO)
            for l in range(2):
                sp.dma_start(d["yb"][l].rearrange("(p n) (h c) -> p (n h) c", p=P, c=ZERO),
                             zeros[:, :].unsqueeze(1).to_broadcast([P, runs, ZERO])).then_inc(yb_zeroed, 16)
            stream("merge", 8)
            stream("out1", 2)
            sp.wait_ge(phase_done, 12)
            load_mod(2 * MOD_GROUPS)
            load_mod(2 * MOD_GROUPS + 1)
            stream("gu2", 11, MOD_GROUPS + 1)
            stream_down("down2")
            stream_paired("even_in", 4)
            stream_paired("even_out", 2)
            stream_experts(0)
            stream("q2", 2)
            stream_paired("kv2", 1)
            stream("wo", 2)
            stream_experts(1)
            for t in range(LT):
                sp.wait_ge(moe[1]["sum_read"], t + 1)
                sp.dma_start(d["out"][:, :, t * P:(t + 1) * P], lat[:, :, t * P:(t + 1) * P]).then_inc(stored, 16)
            sp.wait_ge(stored, 16 * LT)

        @block.tensor
        def _(pe):
            phase = Phase(pe)
            norms = [0]

            def modulate(g, half):
                pe.wait_ge(mod_load, 16 + 16 * half + g * 32)
                if half == 0:
                    pe.wait_ge(mod_free, 1 + g)
                for j in range(4):
                    mm = nc.tensor.matmul(bank[5][j * QUAD:(j + 1) * QUAD, :], silu_c[:, 4 * half + j, :], mslot[:, j * MODC:(j + 1) * MODC],
                                          start=(half == 0), stop=(half == 1))
                mm.then_inc(mod_full, 1)

            def turn_modulation(g):
                pe.wait_ge(mrow_ready, 1 + g)
                for t in range(4):
                    mm = nc.tensor.matmul(bank[6][:, 2 * t:2 * t + 2], mrow[:, t * P:(t + 1) * P], const("quads"), start=True, stop=True)
                mm.then_inc(mod_turned, 1)

            def dense(name, its, rhs, after=None):
                r0, l0, _ = plan[name]
                with pe.Fori(0, its) as i:
                    for j in range(4):
                        s = j // 2
                        if j % 2 == 0:
                            pe.wait_ge(wload[s], 16 * l0 + 16 + i * 16)
                        pe.wait_ge(free[j], r0 + i)
                        for k in range(KT):
                            w = slot[s][:, (j % 2) * KT * P + k * P:(j % 2) * KT * P + (k + 1) * P]
                            m = rhs(j, k)
                            mm = nc.tensor.matmul(bank[j][:, 0:m.shape[1]], w, m, start=(k == 0), stop=(k == KT - 1))
                        mm.then_inc(full[j], 1)
                        if after:
                            after(i, j)

            def split_products(out, piece, low, high, ready, first, last, free_piece=True):
                n = len(high)
                for k in range(n):
                    if ready:
                        ready(k)
                    for part_of, flag in ((high, first and k == 0), (low, False)):
                        mm = nc.tensor.matmul(out, piece[0][k], part_of[k], start=flag, stop=False)
                if free_piece:
                    mm.then_inc(wh_used, 1)
                for k in range(n):
                    mm = nc.tensor.matmul(out, piece[1][k], high[k], start=False, stop=(last and k == n - 1))
                return mm

            def tiles_of(view, n):
                return [view[:, k * P:(k + 1) * P] for k in range(n)]

            def gate_up(n, mod, norm):
                r0, _, _ = plan[f"gu{n}"]
                w0 = PIECES_BEFORE[n]
                uh, ul = ([u[:, k, :] for k in range(KT)] for u in (u_high, u_low))
                with pe.Fori(0, GU_ROUNDS) as i:
                    for j in range(4):
                        s, h = j // 2, j % 2
                        pe.wait_ge(wl_ready, w0 + j + 1 + i * 4)
                        pe.wait_ge(free[j], r0 + i)
                        piece = tiles_of(w_high[:, h, :], KT), tiles_of(w_low[s][:, h * PIECE:(h + 1) * PIECE], KT)
                        split_products(bank[j][:, :], piece, ul, uh, (lambda k: normed(norm, k)) if j == 0 else None, True, True).then_inc(full[j], 1)
                        if j < 2:
                            modulate(mod + i, j)
                    turn_modulation(mod + i)

            def split_dense(name, its, w0, parts, ready, rings=ffn_ring):
                r0, _, _ = plan[name]
                with pe.Fori(0, its) as i:
                    for j in range(4):
                        s, h = j // 2, j % 2
                        pe.wait_ge(wl_ready, w0 + j + 1 + i * 4)
                        pe.wait_ge(free[j], r0 + i)
                        piece = tiles_of(rings[h], KT), tiles_of(w_low[s][:, h * PIECE:(h + 1) * PIECE], KT)
                        split_products(bank[j][:, :], piece, *parts[j], ready[j], True, True).then_inc(full[j], 1)

            def down(n):
                r0, _, _ = plan[f"down{n}"]
                w0 = PIECES_BEFORE[n] + 4 * GU_ROUNDS
                with pe.Fori(0, 2) as i:
                    for t in range(4):
                        s, j = t % 2, (0, 2, 1, 3)[t]
                        pe.wait_ge(free[j], r0 + i)
                        for p in range(DOWN_PIECES):
                            at, ring = down_piece(t, p)
                            pe.wait_ge(wl_ready, w0 + DOWN_PIECES * t + p + 1 + i * (4 * DOWN_PIECES))
                            ks = range(at.start // P, at.stop // P)
                            pe.wait_ge(act_ready, 2 + FT * (n - 1) + ks.stop)
                            piece = tiles_of(w_high[:, ring, :], len(ks)), tiles_of(w_low[s][:, at], len(ks))
                            mm = split_products(bank[j][:, :], piece, [act_low[:, k, :] for k in ks], [act_high[:, k, :] for k in ks],
                                                None, p == 0, p == DOWN_PIECES - 1)
                        mm.then_inc(full[j], 1)

            def paired(name, its, low, high, ready):
                r0, _, _ = plan[name]
                w0 = PIECES_BEFORE[name]
                with pe.Fori(0, its) as i:
                    for s in range(2):
                        for j in range(4):
                            h = j // 2
                            a, n = ((0, S), (S, C))[j % 2]
                            if j % 2 == 0:
                                pe.wait_ge(wl_ready, w0 + 2 * s + h + 1 + i * 4)
                            pe.wait_ge(free[j], r0 + s + i * 2)
                            piece = tiles_of(even_ring[h], KT), tiles_of(w_low[s][:, h * PIECE:(h + 1) * PIECE], KT)
                            split_products(bank[j][:, 0:n], piece, [low[:, k, a:a + n] for k in range(KT)],
                                           [high[:, k, a:a + n] for k in range(KT)], ready if s + j == 0 else None, True, True,
                                           free_piece=j % 2).then_inc(full[j], 1)

            def norm_sum(u, context=False):
                n = norms[0]
                norms[0] += 1
                for k in range(KT):
                    pe.wait_ge(sq_ready, KT * n + k + 1)
                    mm = nc.tensor.matmul(bank[4][:, :], ones, u[:, k, 0:S], start=(k == 0), stop=(k == KT - 1))
                    if context:
                        mm = nc.tensor.matmul(bank[5][:, 0:C], ones, u[:, k, S:SC], start=(k == 0), stop=(k == KT - 1))
                mm.then_inc(ssum_ready, 1)

            def normed(n, k):
                pe.wait_ge(u_ready, KT * (n - 1) + k + 1)

            def ffn(n, n_norm):
                mod = (n - 1) * MOD_GROUPS
                for half in range(2):
                    modulate(mod, half)
                norm_sum(u1)
                turn_modulation(mod)
                gate_up(n, mod + 1, n_norm)
                down(n)
                norm_sum(u1)
                phase.end()

            def attend(second, u0, qs, sm, pT, yo, kt, v):
                def scores(i, m):
                    n, kv = m % LT, m // LT
                    lo, hi, _ = att_tiles(second, n)
                    at = 0 if second else 2 * (m % 2)
                    pe.wait_ge(q_staged, u0 + m + 1 + 8 * i)
                    pe.wait_ge(s_evac, u0 + m + (2 if second else 1) + 8 * i)
                    for s in range(2):
                        h = slice(64 * s, 64 * s + 64)
                        mm = nc.tensor.matmul(bank[at + s][:, 0:(hi - lo) * P], qs[h, kv, n * P:(n + 1) * P],
                                              kt[h, kv, lo * P:hi * P], start=True, stop=True)
                    if second:
                        for s in range(2):
                            h = slice(64 * s, 64 * s + 64)
                            mm = nc.tensor.matmul(bank[2 + s][:, 0:C], qs[h, kv, n * P:(n + 1) * P], kt[h, kv, S:SC],
                                                  start=True, stop=True)
                    mm.then_inc(s_full, 1)

                def spread(i, m, late=False):
                    per, groups = att_groups(second, m % LT)
                    if not late:
                        pe.wait_ge(exp_ready, u0 + m + 1 + 8 * i)
                    for g in range(2, groups) if late else range(min(groups, 2)):
                        at = groups_before(second, 0, m) + g
                        pe.wait_ge(t_evac, groups_before(second, i, m) + g + 1)
                        for x in range(4 * g, min(4 * g + 4, 2 * per)):
                            tr = nc.tensor.transpose(bank[4 + at % 2][:, (x % 4) * P:(x % 4 + 1) * P],
                                                     sm[:, m % 4, x // per, (x % per) * P:(x % per + 1) * P], ident)
                        tr.then_inc(t_full, 1)

                def spread_late(i, m):
                    spread(i, m, late=True)

                def values(i, m):
                    n, kv = m % LT, m // LT
                    lo, hi, _ = att_tiles(second, n)
                    per, groups = att_groups(second, n)
                    pe.wait_ge(t_evac, groups_before(second, i, m) + groups + 2)
                    pe.wait_ge(y_norm, u0 + m + 1 + 8 * i)
                    pe.wait_ge(o_evac, u0 + m + 1 + 8 * i)
                    for s in range(2):
                        for x in range(per):
                            tile = lo + x if x < hi - lo else LT + x - (hi - lo)
                            mm = nc.tensor.matmul(bank[6 + m % 2][:, s * HD:(s + 1) * HD],
                                                  pT[:, m % 2, (s * per + x) * P:(s * per + x + 1) * P],
                                                  v[:, tile, (2 * kv + s) * HD:(2 * kv + s + 1) * HD],
                                                  start=(x == 0), stop=(x == per - 1))
                    mm.then_inc(o_full, 1)

                def turn(i, m):
                    pe.wait_ge(y_norm, u0 + m + 3 + 8 * i)
                    nc.tensor.transpose(bank[6 + m % 2][:, P:2 * P], yo[:, m % 2, :], ident).then_inc(turn_full, 1)

                att_schedule(pe, [(2, spread), (0, scores), (2, spread_late), (3, values), (4, turn)], 4)

            def moe_layer(l):
                q, nt = moe[l], TILES_OF[l]
                pe.wait_ge(wr_loaded, 16 * (l + 1))
                for k in range(KT):
                    normed(8 + l, k)
                    mm = nc.tensor.matmul(bank[2][0:ROUTE, :], wr[:, k, :], u2[:, k, 0:S], start=(k == 0), stop=(k == KT - 1))
                    if nt == TT:
                        mm = nc.tensor.matmul(bank[3][0:ROUTE, 0:C], wr[:, k, :], u2[:, k, S:SC], start=(k == 0), stop=(k == KT - 1))
                mm.then_inc(q["lg_full"], 1)
                pe.wait_ge(q["lg_copied"], l + 1)
                for t in range(nt):
                    mm = nc.tensor.transpose(bank[4][:, t * ROUTE:(t + 1) * ROUTE], lgT[0:ROUTE, t * P:(t + 1) * P], ident[0:ROUTE, 0:ROUTE])
                mm.then_inc(q["logits"], 1)
                def rows(t):
                    if t > 0:
                        pe.wait_ge(q["xt_cp"], t)
                    for k in range(KT):
                        tr = nc.tensor.transpose(bank[k // 4][:, (k % 4) * P:(k % 4 + 1) * P], u2[:, k, t * P:(t + 1) * P], ident)
                    tr.then_inc(q["xt_tr"], 1)

                for t in range(EARLY_ROWS):
                    rows(t)
                pe.wait_ge(q["onehot"], l + 1)
                for j in range(nt):
                    mm = nc.tensor.matmul(bank[4][0:NE, 0:2], both[:, j, :], ones[:, 0:2], start=(j == 0), stop=(j == nt - 1))
                mm.then_inc(q["counts"], 1)
                pe.wait_ge(q["nblk"], l + 1)
                nc.tensor.matmul(bank[5][:, 0:NE], nbb[0:NE, :], const("tri_lt")[0:NE, :], start=True, stop=True)
                nc.tensor.matmul(bank[6][0:NE, 0:2], const("tri_le")[0:NE, :], nbb[0:NE, 0:2], start=True, stop=True)
                nc.tensor.matmul(bank[7][0:2, TABW:TABW + 2], nbb[0:NE, 0:2], ones[0:NE, 0:2], start=True, stop=True).then_inc(q["starts"], 1)
                pe.wait_ge(q["cmp"], l + 1)
                nc.tensor.matmul(bank[6][0:2, 64:64 + TABW], ones[0:NE, 0:2], cmpb[0:NE, 0:TABW], start=True, stop=True).then_inc(q["exp_row"], 1)
                for t in range(nt):
                    for j in range(t + 1):
                        mm = nc.tensor.matmul(bank[3][:, t * NE:(t + 1) * NE], ones if j < t else const("before"), both[:, j, :],
                                         start=(j == 0), stop=(j == t))
                mm.then_inc(q["ranks"], 1)
                for t in range(EARLY_ROWS, nt):
                    rows(t)
                    if t == EARLY_ROWS:
                        pe.wait_ge(q["tab_in"], l + 1)
                        for x in range(2 * nt):
                            mm = nc.tensor.matmul(bank[2][0:MB, 0:TABW], at_place[:, x, :], in_block[:, x, :],
                                                  start=(x == 0), stop=(x == 2 * nt - 1))
                        mm.then_inc(q["tab_full"], 1)

                lo, hi = slice(0, MB), slice(MB, 2 * MB)

                def spread_x(b):
                    pe.wait_ge(q["gathered"], 16 * (b + 1))
                    nc.tensor.matmul(bank[2][:, 0:MB], xg[lo, 0:D:KT], ident[lo, lo], start=True, stop=True)
                    for k in range(1, KT):
                        tr = nc.tensor.transpose(bank[2][:, k * MB:(k + 1) * MB], xg[lo, k:D:KT], ident[lo, lo])
                    tr.then_inc(q["xt_full"], 1)

                def up(b, first=False):
                    pe.wait_ge(q["xt_ready"], b + 1)
                    if not first:
                        pe.wait_ge(q["h_ready"], b)
                    for c in range(2):
                        pe.wait_ge(mload[l][c], 16 * (b + 1))
                        pe.wait_ge(mload[l][2 + c], 16 * (b + 1))
                        for k in range(4):
                            flags = dict(start=(c == 0 and k == 0), stop=(c == 1 and k == 3))
                            ga = nc.tensor.matmul(bank[0][lo, :], xT[:, 4 * c + k, :], wslot[c][:, k * EF:(k + 1) * EF], **flags)
                            if k == 3:
                                ga.then_inc([mdone[l][0], q["gate_full"]][c], 1)
                            mm = nc.tensor.matmul(bank[0][hi, :], xT[:, 4 * c + k, :], wslot[2 + c][:, k * EF:(k + 1) * EF], **flags)
                        mm.then_inc([mdone[l][1], q["up_full"]][c], 1)

                def out(b, first=False):
                    pe.wait_ge(q["ht_ready"], b + 1)
                    if not first:
                        pe.wait_ge(q["y_ready"], b)
                    for c in range(2):
                        pe.wait_ge(mload[l][4 + c], 16 * (b + 1))
                        for k in range(2):
                            for n, half in enumerate((lo, hi)):
                                mm = nc.tensor.matmul(bank[4][half, :], hT[:, 2 * c + k, :],
                                                      wslot[4 + c][:, k * D + n * 512:k * D + (n + 1) * 512],
                                                      start=(c == 0 and k == 0), stop=(c == 1 and k == 1))
                    mm.then_inc(q["w2_done"], 1)

                def spread_h(b):
                    pe.wait_ge(q["h_ready"], b + 1)
                    nc.tensor.matmul(bank[6][:, 0:MB], hmul[hi, 0:EF:EF // P], ident[hi, hi], start=True, stop=True)
                    for k in range(1, EF // P):
                        tr = nc.tensor.transpose(bank[6][:, k * MB:(k + 1) * MB], hmul[hi, k:EF:EF // P], ident[hi, hi])
                    tr.then_inc(q["htp_full"], 1)

                phase.end()
                last = pe.value_load(exp_i[0:1, TABW:TABW + 1], min_val=2, max_val=NBMAX - 1)
                spread_x(0)
                up(0, first=True)
                spread_x(1)
                spread_h(0)
                out(0, first=True)
                up(1)
                spread_x(2)
                spread_h(1)
                with pe.Fori(2, last + 1) as b:
                    out(b - 1)
                    up(b)
                    spread_x(b + 1)
                    spread_h(b)
                out(last)
                phase.end()
                for t in range(nt):
                    pe.wait_ge(q["sum_ready"], t + 1)
                    if t > 1:
                        pe.wait_ge(q["sum_read"], t - 1)
                    for k in range(KT):
                        tr = nc.tensor.transpose(bank[2 * (t % 2) + k // 4][:, (k % 4) * P:(k % 4 + 1) * P],
                                                 yrows[t][0][:, k * P:(k + 1) * P], ident)
                    tr.then_inc(q["sum_tr"], 1)
                phase.end()

            pe.wait_ge(loaded, 48)
            for j in range(4):
                nc.tensor.matmul(bank[j][:, 0:P], ident, ident, start=True, stop=True).then_inc(full[j], 1)
            pe.wait_ge(cond_ready, 1)
            ffn(1, 1)

            norm_sum(u1)
            for n, name in enumerate(("xbr", "q1")):
                split_dense(name, 2, PIECES_BEFORE["mixer"] + n * KT, [(p1_low, [p1_high[:, k, :] for k in range(KT)])] * 4,
                            [lambda k: pe.wait_ge(mu_ready, k + 1), None, None, None])
            pe.wait_ge(lru_loaded, 16)
            for t in range(KT):
                pe.wait_ge(xc_ready, t + 1)
                if t > 0:
                    pe.wait_ge(lin_free, t)
                nc.tensor.matmul(bank[4][:, :], lru_w[:, 0, t, :], xc[:, t, :], start=True, stop=True)
                nc.tensor.matmul(bank[5][:, :], lru_w[:, 1, t, :], xc[:, t, :], start=True, stop=True).then_inc(lin_full, 1)

            def partner(x, raw):
                pe.wait_ge(raw_ready, raw)
                pe.wait_ge(rope_free, x + 1)
                nc.tensor.matmul(bank[6][:, :], const("swap1"), qk1[:, bass.ds(x, 1), :].rearrange("p a t -> p (a t)"),
                                 start=True, stop=True).then_inc(rope_full, 1)

            r0, l0, _ = plan["kv1"]
            pe.wait_ge(wload[0], 16 * (l0 + 1))
            for j in range(2):
                pe.wait_ge(free[j], r0)
                for k in range(KT):
                    mm = nc.tensor.matmul(bank[j][:, :], slot[0][:, j * KT * P + k * P:j * KT * P + (k + 1) * P], u1[:, k, :],
                                          start=(k == 0), stop=(k == KT - 1))
                mm.then_inc(full[j], 1)
                partner(j, 1)
            pe.wait_ge(wload[1], 16 * (l0 + 1))
            for j in range(2):
                pe.wait_ge(free[2 + j], r0)
                for t in range(2):
                    for k in range(KT):
                        mm = nc.tensor.matmul(bank[2 + j][:, t * C:(t + 1) * C], u1[:, k, (2 * j + t) * P:(2 * j + t + 1) * P],
                                              slot[1][:, k * C:(k + 1) * C], start=(k == 0), stop=(k == KT - 1))
                mm.then_inc(full[2 + j], 1)
                partner(2 + j, 1)
            dense("gate", 2, lambda j, k: u1[:, k, :], after=lambda i, j: partner(4 + j + 3 * i, 2) if j < 3 else None)
            phase.end()
            attend(False, 0, *att_views(o, 2 * P), kt1, v1)
            phase.end()
            w0 = PIECES_BEFORE["merge"]
            parts = [[[v[:, k, :] for k in range(KT)] for v in pair] for pair in
                     ((u1_low, u1_high), (lru_low, lru_high), (u1_low, u1_high), (att_low, att_high))]
            split_dense("merge", KT, w0, parts, (lambda k: pe.wait_ge(mu_ready, KT + k + 1), lambda k: pe.wait_ge(mx_ready, k + 1), None,
                                                 lambda k: pe.wait_ge(mx_ready, KT + k + 1)))
            pe.wait_ge(mrg_ready, 8)
            dense("out1", 2, lambda j, k: merged[:, k, :])
            norm_sum(u1)
            phase.end()
            ffn(2, 5)

            norm_sum(u2, context=True)
            paired("even_in", 4, u2_low, u2_high, lambda k: pe.wait_ge(mu_ready, 2 * KT + k + 1))
            phase.end()
            pe.wait_ge(dft_loaded, 80)
            for g in range(4):
                if g > 0:
                    pe.wait_ge(ac_ready, 3 * g)
                for t in range(TT):
                    mm = nc.tensor.matmul(bank[t // 2][:, (t % 2) * 2 * P:(t % 2 + 1) * 2 * P], pt[:, g, t * P:(t + 1) * P], csd,
                                          start=True, stop=True)
                    if t % 2:
                        mm.then_inc(ac_full, 1)
                if g > 0:
                    pe.wait_ge(dft_evac, g)
                pe.wait_ge(ac_ready, 3 * g + 3)
                for t in range(LT):
                    nc.tensor.matmul(bank[3][:, :], ac[:, t, 0:P], c_lat[:, t, :], start=(t == 0), stop=False)
                    nc.tensor.matmul(bank[3][:, :], ac[:, t, P:2 * P], s_lat[:, t, :], start=False, stop=(t == LT - 1))
                for t in range(2):
                    nc.tensor.matmul(bank[4][:, 0:C], ac[:, LT + t, 0:P], c_ctx[:, t, :], start=(t == 0), stop=False)
                    mm = nc.tensor.matmul(bank[4][:, 0:C], ac[:, LT + t, P:2 * P], s_ctx[:, t, :], start=False, stop=(t == 1))
                mm.then_inc(dft_full, 1)
            phase.end()
            paired("even_out", 2, y_low, y_high, lambda k: pe.wait_ge(mx_ready if k % 2 else mu_ready, (2 if k % 2 else 3) * KT + k // 2 + 1))
            phase.end()
            norm_sum(u2, context=True)
            moe_layer(0)

            norm_sum(u2, context=True)
            w0 = PIECES_BEFORE["qkv"]
            split_dense("q2", 2, w0, [[[v[:, k, 0:S] for k in range(KT)] for v in (h_low, h_high)]] * 4,
                        [lambda k: pe.wait_ge(mu_ready, 3 * KT + KT // 2 + k + 1), None, None, None], even_ring)
            r0 = plan["kv2"][0]

            def keys(j):
                h = j // 2
                a, n = ((0, S), (S, C))[j % 2]
                if j % 2 == 0:
                    pe.wait_ge(wl_ready, w0 + KT + h + 1)
                piece = tiles_of(even_ring[h], KT), tiles_of(w_low[0][:, h * PIECE:(h + 1) * PIECE], KT)
                split_products(bank[j][:, 0:n], piece, [h_low[:, k, a:a + n] for k in range(KT)],
                               [h_high[:, k, a:a + n] for k in range(KT)], None, True, True, free_piece=j % 2).then_inc(full[j], 1)

            def values(j):
                if j == 0:
                    pe.wait_ge(wl_ready, w0 + KT + 4)
                for at, t in enumerate(((0, 1), (2, 3), (4,), (5,))[j]):
                    out, tok = bank[j][:, at * C:(at + 1) * C], slice(t * P, (t + 1) * P)
                    for k in range(KT):
                        wh = even_ring[k // 4][:, (k % 4) * C:(k % 4 + 1) * C]
                        nc.tensor.matmul(out, h_high[:, k, tok], wh, start=(k == 0), stop=False)
                        nc.tensor.matmul(out, h_high[:, k, tok], w_low[1][:, k * C:(k + 1) * C], start=False, stop=False)
                        mm = nc.tensor.matmul(out, h_low[:, k, tok], wh, start=False, stop=(k == KT - 1))
                mm.then_inc(full[j], 1)

            for x in range(len(HEAD_TILES) + ROPE_LAG):
                if x < 8:
                    pe.wait_ge(free[x % 4], r0 + x // 4)
                    (keys, values)[x // 4](x % 4)
                if x < len(HEAD_TILES):
                    pe.wait_ge(qsq_ready, x + 1)
                    if x > 0:
                        pe.wait_ge(qstd_ready, x)
                    n = HEAD_TILES[x].shape[1]
                    nc.tensor.matmul(bank[4][:, 0:n], const("headsum"), tmp[:, x % 2, 0:n], start=True, stop=True).then_inc(qsum_full, 1)
                if x - ROPE_LAG in ROTATED:
                    pe.wait_ge(qn_ready, x - ROPE_LAG + 1)
                    pe.wait_ge(rope_free, 10 + ROTATED.index(x - ROPE_LAG) + 1)
                    nc.tensor.matmul(bank[6][:, :], const("swap2"), HEAD_TILES[x - ROPE_LAG], start=True, stop=True).then_inc(rope_full, 1)
            phase.end()
            attend(True, 32, *att_views(att2, 5 * P), kt2, v2)
            phase.end()
            dense("wo", 2, lambda j, k: f[:, k, :])
            phase.end()
            norm_sum(u2)
            moe_layer(1)

        @block.scalar
        def _(act):
            phase = Phase(act)
            norms = [0]

            def squares(src, u, a=0, last=True, after=None):
                for k in range(KT):
                    if after:
                        act.wait_ge(u_ready, KT * (after - 1) + k + 1)
                    i = nc.scalar.activation(u[:, k, a:a + src.shape[2]], src[:, k, :], ACT.Square)
                    if last:
                        i.then_inc(sq_ready, 1)

            def std(context=False):
                norms[0] += 1
                act.wait_ge(ssum_ready, norms[0])
                i = nc.scalar.activation(rs[:, 0:S], bank[4][:, :], ACT.Sqrt, bias=const("eps"), scale=1.0 / D)
                if context:
                    i = nc.scalar.activation(rs[:, S:SC], bank[5][:, 0:C], ACT.Sqrt, bias=const("eps"), scale=1.0 / D)
                i.then_inc(std_ready, 1)

            def shifts(l, which, n_norm, context):
                for k in range(KT):
                    act.wait_ge(un_ready, KT * (n_norm - 6) + k + 1)
                    for st, a, n in ((0, 0, S), (1, S, C))[:1 + context]:
                        i = nc.scalar.activation(u2[:, k, a:a + n], u2[:, k, a:a + n], ACT.Identity, bias=mod[:, l, 3 * which, k, st:st + 1])
                    i.then_inc(u_ready, 1)

            def before_norm(name, its):
                r0 = plan[name][0]
                with act.Fori(0, its) as i:
                    for j in range(4):
                        act.wait_ge(full[j], r0 + 1 + i)
                        nc.scalar.activation(f[:, bass.ds(4 * i + j, 1), :].rearrange("p a t -> p (a t)"), bank[j][:, :], ACT.Copy)
                        nc.scalar.activation(u1[:, bass.ds(4 * i + j, 1), :].rearrange("p a t -> p (a t)"), bank[j][:, :],
                                             ACT.Square).then_inc(free[j], 1)
                act.drain().then_inc(sq_ready, KT)

            def high(s, at, ring, load, used, rings=ffn_ring):
                if load is not None:
                    act.wait_ge(wload[s], load)
                if used is not None:
                    act.wait_ge(wh_used, used)
                nc.scalar.activation(rings[ring][:, 0:at.stop - at.start], slot[s][:, at], ACT.Copy).then_inc(wh_ready, 1)

            def paired_first(name, stream=None):
                _, l0, _ = plan[stream or name]
                for h in range(2):
                    high(0, slice(h * PIECE, (h + 1) * PIECE), h, 16 * (l0 + 1), PIECES_BEFORE[name] - 1 + h, even_ring)

            def paired_highs(name, its, evac=None):
                r0, l0, _ = plan[name]
                w0 = PIECES_BEFORE[name]

                def chunk(i, s, last=False):
                    for j in range(4):
                        h = j // 2
                        if j % 2 == 0 and not last:
                            high(1 - s, slice(h * PIECE, (h + 1) * PIECE), h, 16 * (l0 + 1 + s) + i * 16, w0 + 2 * s + h + 1 + i * 4, even_ring)
                        if evac:
                            evac(i, s, j)

                with act.Fori(0, its - 1) as i:
                    for s in range(2):
                        chunk(i, s)
                chunk(its - 1, 0)
                chunk(its - 1, 1, last=True)

            def ffn(n):
                w0 = PIECES_BEFORE[n]
                r0, l0, _ = plan[f"gu{n}"]

                halves = [slice(h * PIECE, (h + 1) * PIECE) for h in range(2)]
                for h in range(2):
                    high(0, halves[h], h, 16 * (l0 + 1), w0 - 1 + h if n > 1 else None)
                squares(lat[:, :, :], u1, after=4 * (n - 1))
                std()
                for k in range(KT):
                    act.wait_ge(un_ready, KT * (n - 1) + k + 1)
                    nc.scalar.activation(u_high[:, k, :], tmp[:, k % 2, :], ACT.Copy).then_inc(uh_ready, 1)
                with act.Fori(0, GU_ROUNDS) as i:
                    for j in range(4):
                        s, nxt = (1, 0) if j < 2 else (0, 1)
                        high(s, halves[j % 2], j % 2, 16 * (l0 + 1) + 16 * nxt + i * 16, w0 + j + 1 + i * 4)
                        if j < 2:
                            act.wait_ge(full[j], r0 + 1 + i)
                            act.wait_ge(act_ready, FT * (n - 1) + j + 1 + i * 2)
                            nc.scalar.activation(tmp[:, j, :], bank[j][:, :], ACT.Silu).then_inc(free[j], 1)
                        else:
                            act.wait_ge(free[j], r0 + 1 + i)
                            nc.scalar.activation(act_high[:, bass.ds(2 * i + j - 2, 1), :].rearrange("p a t -> p (a t)"), tmp[:, j - 2, :],
                                                 ACT.Copy).then_inc(ah_ready, 1)
                r0, l0, _ = plan[f"down{n}"]
                w0 += 4 * GU_ROUNDS
                for T in range(KT):
                    for ahead in range(2, 2 + DOWN_PIECES):
                        t, p = T + ahead // DOWN_PIECES, ahead % DOWN_PIECES
                        if t < KT:
                            at, ring = down_piece(t, p)
                            high(t % 2, at, ring, 16 * (l0 + 1 + t // 2), w0 + DOWN_PIECES * t + p - 1)
                    j = (0, 2, 1, 3)[T % 4]
                    act.wait_ge(full[j], r0 + 1 + T // 4)
                    nc.scalar.activation(f[:, T, :], bank[j][:, :], ACT.Copy)
                    nc.scalar.activation(u1[:, T, :], bank[j][:, :], ACT.Square).then_inc(free[j], 1)
                act.drain().then_inc(sq_ready, KT)
                std()
                phase.end()

            def attend(second, u0, qs, sm, pT, yo):
                def exps(i, m):
                    per, _ = att_groups(second, m % LT)
                    st = small[:, 16 * (m % 4):16 * (m % 4) + 16]
                    act.wait_ge(max_ready, u0 + m + 1 + 8 * i)
                    for s in range(2):
                        nc.scalar.activation(sm[:, m % 4, s, 0:per * P], sm[:, m % 4, s, 0:per * P], ACT.Exp,
                                             bias=st[:, 4 + s:5 + s], accum_out=st[:, 6 + s:7 + s])
                    nc.scalar.activation(st[:, 8:10], st[:, 10:12], ACT.Exp)
                    act.drain().then_inc(exp_ready, 1)

                def copies(i, m, late=False):
                    per, groups = att_groups(second, m % LT)
                    for g in range(2, groups) if late else range(min(groups, 2)):
                        at = groups_before(second, 0, m) + g
                        w = min(4, 2 * per - 4 * g) * P
                        act.wait_ge(t_full, groups_before(second, i, m) + g + 1)
                        nc.scalar.activation(pT[:, m % 2, 4 * g * P:4 * g * P + w], bank[4 + at % 2][:, 0:w],
                                             ACT.Copy).then_inc(t_evac, 1)

                def copies_late(i, m):
                    copies(i, m, late=True)

                def outputs(i, m):
                    n, kv = m % LT, m // LT
                    act.wait_ge(turn_full, u0 + m + 3 + 8 * i)
                    nc.scalar.activation(f[:, bass.ds(4 * kv + i, 1), n * P:(n + 1) * P].rearrange("p a t -> p (a t)"),
                                         bank[6 + m % 2][:, P:2 * P], ACT.Copy).then_inc(o_evac, 1)

                att_schedule(act, [(2, copies), (1, exps), (2, copies_late), (4, outputs)], 4)

            def moe_layer(l):
                q, nt = moe[l], TILES_OF[l]
                act.dma_start(wr, d["wr"][l]).then_inc(wr_loaded, 16)
                shifts(l, 1, 8 + 2 * l, nt == TT)
                act.wait_ge(q["lg_full"], l + 1)
                i = nc.scalar.activation(lgT[0:ROUTE, 0:S], bank[2][0:ROUTE, :], ACT.Copy)
                if nt == TT:
                    i = nc.scalar.activation(lgT[0:ROUTE, S:SC], bank[3][0:ROUTE, 0:C], ACT.Copy)
                i.then_inc(q["lg_copied"], 1)
                act.wait_ge(q["gexp_in"], l + 1)
                nc.scalar.activation(ge[:, 0:nt, :], ge[:, 0:nt, :], ACT.Exp).then_inc(q["gexp"], 1)
                def rows(t):
                    row = row_bufs[t % len(row_bufs)]
                    act.wait_ge(q["xt_tr"], t + 1)
                    if t > 0 and t % len(row_bufs) == 0:
                        act.wait_ge(q["xt_out"], 16 * t)
                    nc.scalar.activation(row[:, 0:512], bank[0][:, :], ACT.Copy)
                    nc.scalar.activation(row[:, 512:D], bank[1][:, :], ACT.Copy).then_inc(q["xt_cp"], 1)
                    act.wait_ge(q["xt_cp"], t + 1)
                    act.dma_start(d["rows"][l][t * P:(t + 1) * P, :], row).then_inc(q["xt_out"], 16)

                for t in range(EARLY_ROWS):
                    rows(t)
                act.wait_ge(q["eexp_in"], l + 1)
                nc.scalar.activation(scal[:, 5, 0:nt], scal[:, 4, 0:nt], ACT.Exp).then_inc(q["eexp"], 1)
                for t in range(EARLY_ROWS, nt):
                    rows(t)

                def silu(b, first=False):
                    act.wait_ge(q["gate_full"], b + 1)
                    if not first:
                        act.wait_ge(q["h_ready"], b)
                    nc.scalar.activation(hsil[MB:2 * MB, :], bank[0][0:MB, :], ACT.Silu).then_inc(q["sg_ready"], 1)

                def copy_y(b, first=False):
                    act.wait_ge(q["w2_done"], b + 1)
                    if not first:
                        act.wait_ge(q["y_written"], 32 * b)
                    nc.scalar.activation(ysb, bank[4][:, :], ACT.Copy).then_inc(q["y_ready"], 1)

                def write_y(b, written="y_written"):
                    act.wait_ge(q["y_ready"], b + 1)
                    for n in range(2):
                        act.dma_start(d["yb"][l][bass.ds(b * MB, MB), n * 512:(n + 1) * 512], ysb[n * MB:(n + 1) * MB, :]
                                      ).then_inc(q[written], 16)

                act.wait_ge(yb_zeroed, 32)
                phase.end()
                last = act.value_load(exp_i[0:1, TABW:TABW + 1], min_val=2, max_val=NBMAX - 1)
                silu(0, first=True)
                copy_y(0, first=True)
                write_y(0)
                silu(1)
                with act.Fori(2, last + 1) as b:
                    copy_y(b - 1)
                    write_y(b - 1)
                    silu(b)
                copy_y(last)
                write_y(last, "y_last")
                act.wait_ge(q["y_last"], 32)
                phase.end()
                phase.end()

            act.wait_ge(loaded, 48)
            act.wait_ge(zeros_ready, 1)
            nc.scalar.activation(silu_c[:, :, 0:2], vec("cond").rearrange("p (k s) -> p k s", k=KT), ACT.Silu).then_inc(cond_ready, 1)
            ffn(1)

            act.dma_start(lru_w, d["lru_w"]).then_inc(lru_loaded, 16)
            halves = [slice(h * PIECE, (h + 1) * PIECE) for h in range(2)]
            r0, l0, _ = plan["xbr"]
            w0 = PIECES_BEFORE["mixer"]
            for h in range(2):
                high(0, halves[h], h, 16 * (l0 + 1), w0 - 1 + h)
            squares(lat[:, :, :], u1, after=2)
            std()
            act.wait_ge(cond_ready, 2)
            nc.scalar.activation(lam8[:, 4, :], lam8[:, 3, :], ACT.Exp).then_inc(cond_ready, 1)
            for k in range(KT):
                act.wait_ge(u_ready, KT * 2 + k + 1)
                nc.scalar.activation(p1_high[:, k, :], u1[:, k, :], ACT.Copy).then_inc(mh_ready, 1)

            def projection(i, dst):
                for j in range(4):
                    if i < 3 or j < 2:
                        s, nxt = (1, 0) if j < 2 else (0, 1)
                        high(s, halves[j % 2], j % 2, 16 * (l0 + 1 + nxt + i), w0 + 4 * i + j + 1)
                    act.wait_ge(full[j], r0 + 1 + i)
                    nc.scalar.activation(dst(4 * (i % 2) + j), bank[j][:, :], ACT.Copy).then_inc(free[j], 1)

            for i in range(2):
                projection(i, lambda x: xbr[:, x, CONV1 - 1:XPAD])
            act.drain().then_inc(xbr_ready, 1)
            for i in range(2, 4):
                projection(i, lambda x: qt1[:, x, :])
            act.drain().then_inc(raw_ready, 1)
            ba, bx = vec("lru_b_a"), vec("lru_b_x")
            for t in range(KT):
                act.wait_ge(lin_full, t + 1)
                nc.scalar.activation(gr[:, t, :], bank[4][:, :], ACT.Sigmoid, bias=ba[:, t:t + 1])
                nc.scalar.activation(gi[:, t, :], bank[5][:, :], ACT.Sigmoid, bias=bx[:, t:t + 1]).then_inc(lin_free, 1)
            act.drain()
            for t in range(KT):
                nc.scalar.activation(xbr[:, t, 0:S], gr[:, t, :], ACT.Exp, scale=lam8[:, 1, t:t + 1])
                nc.scalar.activation(gr[:, t, :], gr[:, t, :], ACT.Tanh, scale=lam8[:, 0, t:t + 1])
                act.drain().then_inc(decay_ready, 1)
            r0 = plan["kv1"][0]
            for j in range(4):
                act.wait_ge(full[j], r0 + 1)
                nc.scalar.activation(kt1[:, j, :] if j < 2 else v1[:, 2 * (j - 2):2 * (j - 2) + 2, :], bank[j][:, :],
                                     ACT.Copy).then_inc(free[j], 1)
            act.drain().then_inc(raw_ready, 1)
            r0 = plan["gate"][0]
            with act.Fori(0, 2) as i:
                for j in range(4):
                    act.wait_ge(msq_ready, j + 1 + i * 4)
                    grv = gr[:, bass.ds(4 * i + j, 1), :].rearrange("p a t -> p (a t)")
                    nc.scalar.activation(grv, grv, ACT.Sqrt).then_inc(mult_ready, 1)
                for j in range(4):
                    act.wait_ge(full[j], r0 + 1 + i)
                    nc.scalar.activation(f[:, bass.ds(4 * i + j, 1), :].rearrange("p a t -> p (a t)"), bank[j][:, :],
                                         ACT.Gelu_apprx_tanh).then_inc(free[j], 1)
            act.drain().then_inc(gate_ready, 1)
            phase.end()
            attend(False, 0, *att_views(o, 2 * P))
            phase.end()
            r0, l0, _ = plan["merge"]
            w0 = PIECES_BEFORE["merge"]
            halves = [slice(h * PIECE, (h + 1) * PIECE) for h in range(2)]
            for h in range(2):
                high(0, halves[h], h, 16 * (l0 + 1), w0 - 1 + h)
            for k in range(KT):
                nc.scalar.activation(u1_high[:, k, :], u1[:, k, :], ACT.Copy).then_inc(mh_ready, 1)

            def merge_round(i, last=False):
                for j in range(4):
                    if j < 2 or not last:
                        s, nxt = (1, 0) if j < 2 else (0, 1)
                        high(s, halves[j % 2], j % 2, 16 * (l0 + 1) + 16 * nxt + i * 16, w0 + j + 1 + i * 4)
                    if j % 2 == 0:
                        act.wait_ge(full[j], r0 + 1 + i)
                        act.wait_ge(free[j + 1], r0 + i)
                        nc.scalar.activation(tmp[:, j // 2, :], bank[j][:, :], ACT.Sigmoid).then_inc(free[j], 1)

            with act.Fori(0, KT - 1) as i:
                merge_round(i)
            merge_round(KT - 1, last=True)
            before_norm("out1", 2)
            std()
            phase.end()
            ffn(2)

            act.dma_start(cxt, d["ctx"]).then_inc(cxt_loaded, 16)
            paired_first("even_in")
            act.wait_ge(cxt_loaded, 16)
            squares(cxt[:, :, :], u2, S, last=False)
            squares(lat[:, :, :], u2, after=6)
            for dst, name in ((csd, "cs_d"), (c_ctx, "c_ctx"), (s_ctx, "s_ctx"), (c_lat, "c_lat"), (s_lat, "s_lat")):
                a, n = DFT_AT[name]
                src = d["dft"][:, a:a + n]
                if len(dst.shape) == 3:
                    src = src.rearrange("p (l t) -> p l t", l=dst.shape[1])
                act.dma_start(dst, src).then_inc(dft_loaded, 16)
            std(context=True)
            for k in range(KT):
                act.wait_ge(u_ready, KT * 6 + k + 1)
                nc.scalar.activation(u2_high[:, k, :], u2[:, k, :], ACT.Copy).then_inc(mh_ready, 1)
            r0 = plan["even_in"][0]

            def evac(i, s, j):
                act.wait_ge(full[j], r0 + 1 + s + i * 2)
                a, n = ((0, S), (S, C))[j % 2]
                nc.scalar.activation(pt[:, bass.ds(4 * i + 2 * s + j // 2, 1), a:a + n].rearrange("p a t -> p (a t)"), bank[j][:, 0:n],
                                     ACT.Copy).then_inc(free[j], 1)

            paired_highs("even_in", 4, evac)
            phase.end()
            for g in range(4):
                if g > 0:
                    act.wait_ge(dft_full, g)
                for h in range(3):
                    act.wait_ge(ac_full, 3 * g + h + 1)
                    nc.scalar.activation(ac[:, 2 * h:2 * h + 2, :], bank[h][:, :], ACT.Copy).then_inc(ac_ready, 1)
                act.wait_ge(dft_full, g + 1)
                nc.scalar.activation(yt[:, g, 0:S], bank[3][:, :], ACT.Copy)
                nc.scalar.activation(yt[:, g, S:SC], bank[4][:, 0:C], ACT.Copy).then_inc(dft_evac, 1)
            phase.end()
            paired_first("even_out")
            for k in range(KT):
                nc.scalar.activation(y_high[:, k, :], yt[:, k, :], ACT.Copy).then_inc(mh_ready, 1)
            paired_highs("even_out", 2)
            phase.end()
            squares(cxt[:, :, :], u2, S, last=False)
            squares(lat[:, :, :], u2)
            std(context=True)
            moe_layer(0)

            paired_first("qkv", "q2")
            squares(cxt[:, :, :], u2, S, last=False)
            squares(lat[:, :, :], u2)
            std(context=True)
            for k in range(KT):
                act.wait_ge(un_ready, KT * 3 + k + 1)
                nc.scalar.activation(u2[:, k, 0:S], u2[:, k, 0:S], ACT.Identity, bias=mod[:, 1, 0, k, 0:1])
                act.drain()
                nc.scalar.activation(h_high[:, k, :], u2[:, k, :], ACT.Copy).then_inc(mh_ready, 1)
            r0, l0, _ = plan["q2"]
            w0 = PIECES_BEFORE["qkv"]
            with act.Fori(0, 2) as i:
                for j in range(4):
                    s, nxt = (1, 0) if j < 2 else (0, 1)
                    high(s, halves[j % 2], j % 2, 16 * (l0 + 1 + nxt) + i * 16, w0 + j + 1 + i * 4, even_ring)
                    act.wait_ge(full[j], r0 + 1 + i)
                    nc.scalar.activation(qt2[:, bass.ds(4 * i + j, 1), :].rearrange("p a t -> p (a t)"), bank[j][:, :],
                                         ACT.Copy).then_inc(free[j], 1)
            act.drain()
            r0, l0, _ = plan["kv2"]

            def head_squares(x):
                if x > 1:
                    act.wait_ge(qsum_full, x - 1)
                if x == KT:
                    act.drain()
                nc.scalar.activation(tmp[:, x % 2, 0:HEAD_TILES[x].shape[1]], HEAD_TILES[x], ACT.Square).then_inc(qsq_ready, 1)

            head_squares(0)
            for x in range(len(HEAD_TILES)):
                if x in (1, 3):
                    high(1, halves[x // 2], x // 2, 16 * (l0 + 1), w0 + KT + x // 2 + 1, even_ring)
                if x < 8:
                    j = x % 4
                    act.wait_ge(full[j], r0 + 1 + x // 4)
                    if x < 4:
                        a, n = ((0, S), (S, C))[j % 2]
                        dst = kt2[:, j // 2, a:a + n]
                    else:
                        a, t = ((0, 2), (2, 2), (4, 1), (5, 1))[j]
                        dst, n = v2[:, a:a + t, :], t * C
                    nc.scalar.activation(dst, bank[j][:, 0:n], ACT.Copy).then_inc(free[j], 1)
                if x + 1 < len(HEAD_TILES):
                    head_squares(x + 1)
                n = HEAD_TILES[x].shape[1]
                act.wait_ge(qsum_full, x + 1)
                if x > 1:
                    act.wait_ge(qn_ready, x - 1)
                nc.scalar.activation(tmp[:, 2 + x % 2, 0:n], bank[4][:, 0:n], ACT.Sqrt, bias=const("eps"),
                                     scale=1.0 / HD).then_inc(qstd_ready, 1)
            phase.end()
            attend(True, 32, *att_views(att2, 5 * P))
            phase.end()
            phase.end()
            squares(lat[:, :, :], u2)
            std()
            moe_layer(1)

        @block.vector
        def _(dve):
            phase = Phase(dve)
            norms = [0]
            modf = mod[:, :, :, :, :].rearrange("p l s k c -> p (l s k c)")
            bm = vec("b_mod")

            def rsqrt(n):
                norms[0] += 1
                dve.wait_ge(std_ready, norms[0])
                nc.vector.reciprocal(rs[:, 0:n], rs[:, 0:n])
                dve.drain()

            def pre_norm(g, u):
                rsqrt(S)
                for k in range(KT):
                    nc.vector.scalar_tensor_tensor(u[:, k, :], lat[:, k, :], g[:, k:k + 1], rs[:, 0:S], ALU.mult,
                                                   ALU.mult).then_inc(u_ready, 1)

            def post_norm(g):
                for k in range(KT):
                    nc.vector.scalar_tensor_tensor(f[:, k, :], f[:, k, :], g[:, k:k + 1], rs[:, 0:S], ALU.mult, ALU.mult)
                    dve.drain()
                    nc.vector.tensor_tensor(lat[:, k, :], lat[:, k, :], f[:, k, :], ALU.add).then_inc(u_ready, 1)

            def mod_norm(l, which, context, shift=0):
                rsqrt(SC if context else S)
                for k in range(KT):
                    parts = [(0, lat, 0, S)] + ([(1, cxt, S, C)] if context else [])
                    for st, src, a, n in parts:
                        i = nc.vector.scalar_tensor_tensor(u2[:, k, a:a + n], src[:, k, :], amod[:, l, which, st, k:k + 1],
                                                       rs[:, a:a + n], ALU.mult, ALU.mult)
                    if shift:
                        dve.drain()
                        for st, src, a, n in parts[2 - shift:]:
                            i = nc.vector.tensor_scalar(u2[:, k, a:a + n], u2[:, k, a:a + n], mod[:, l, 3 * which, k, st:st + 1], None,
                                                        ALU.add)
                    i.then_inc(u_ready if shift == 2 else un_ready, 1)

            def modulation_rows(g):
                dve.wait_ge(mod_full, 3 + g * 2)
                dve.wait_ge(mod_turned, 1 + g)
                nc.vector.tensor_copy(mrow, bank[5][:, :]).then_inc(mrow_ready, 1)

            def modulation(g):
                dve.wait_ge(mod_turned, 2 + g)
                nc.vector.tensor_tensor(modf[:, bass.ds(8 * g, 8)], bank[6][:, 0:8], bm[:, bass.ds(8 * g, 8)], ALU.add).then_inc(mod_free, 1)

            def ffn(n, pre, post):
                mod = (n - 1) * MOD_GROUPS
                modulation_rows(mod)
                rsqrt(S)
                g = vec(pre)
                for k in range(KT):
                    if k > 1:
                        dve.wait_ge(u_ready, KT * 4 * (n - 1) + k - 1)
                    nc.vector.scalar_tensor_tensor(tmp[:, k % 2, :], lat[:, k, :], g[:, k:k + 1], rs[:, 0:S], ALU.mult,
                                                   ALU.mult).then_inc(un_ready, 1)
                modulation(mod)
                r0 = plan[f"gu{n}"][0]
                with dve.Fori(0, 11) as i:
                    modulation_rows(mod + 1 + i)
                    for j in range(2):
                        dve.wait_ge(full[2 + j], r0 + 1 + i)
                        dve.wait_ge(free[j], r0 + 1 + i)
                        nc.vector.tensor_tensor(tmp[:, j, :], tmp[:, j, :], bank[2 + j][:, :], ALU.mult).then_inc(free[2 + j], 1)
                    modulation(mod + 1 + i)
                rsqrt(S)
                phase.end()
                post_norm(post)

            def attend(second, u0, qs, sm, pT, yo, sinks, mask):
                def stats(i, m):
                    n, kv = m % LT, m // LT
                    lo, hi, m0 = att_tiles(second, n)
                    per, _ = att_groups(second, n)
                    at = 0 if second else 2 * (m % 2)
                    w = (hi - lo) * P
                    st = small[:, 16 * (m % 4):16 * (m % 4) + 16]
                    dve.wait_ge(s_full, u0 + m + 9 + 8 * i)
                    for s in range(2):
                        x = nc.vector.scalar_tensor_tensor(sm[:, m % 4, s, 0:w], bank[at + s][:, 0:w], SCALE, mask[:, m0:m0 + w],
                                                           ALU.mult, ALU.add)
                        if second:
                            x = nc.vector.tensor_scalar(sm[:, m % 4, s, w:w + C], bank[2 + s][:, 0:C], SCALE, None, ALU.mult)
                    x.then_inc(s_evac, 1)
                    dve.drain()
                    nc.vector.tensor_reduce(st[:, 0:2], sm[:, m % 4, :, 0:per * P], AX.X, ALU.max)
                    dve.drain()
                    sk = sinks[:, bass.ds(8 * kv + 2 * i, 2)]
                    nc.vector.tensor_tensor(st[:, 2:4], st[:, 0:2], sk, ALU.max)
                    dve.drain()
                    nc.vector.tensor_scalar(st[:, 4:6], st[:, 2:4], -1.0, None, ALU.mult)
                    nc.vector.tensor_tensor(st[:, 10:12], sk, st[:, 2:4], ALU.subtract)
                    dve.drain().then_inc(max_ready, 1)

                def normalise(i, m):
                    st = small[:, 16 * (m % 4):16 * (m % 4) + 16]
                    dve.wait_ge(o_full, u0 + m + 1 + 8 * i)
                    nc.vector.tensor_tensor(st[:, 12:14], st[:, 6:8], st[:, 8:10], ALU.add)
                    dve.drain()
                    nc.vector.reciprocal(st[:, 14:16], st[:, 12:14])
                    dve.drain()
                    dve.wait_ge(turn_full, u0 + m + 1 + 8 * i)
                    for s in range(2):
                        x = nc.vector.tensor_scalar(yo[:, m % 2, s * HD:(s + 1) * HD], bank[6 + m % 2][:, s * HD:(s + 1) * HD],
                                                    st[:, 14 + s:15 + s], None, ALU.mult)
                    x.then_inc(y_norm, 1)

                att_schedule(dve, [(0, stats), (3, normalise)], 3)

            def rope(src, cos, sin, count0):
                for x, a in enumerate(src):
                    dve.wait_ge(rope_full, count0 + x + 1)
                    nc.vector.tensor_tensor(rs[:, 0:S], bank[6][:, :], sin, ALU.mult).then_inc(rope_free, 1)
                    nc.vector.tensor_tensor(a, a, cos, ALU.mult)
                    dve.drain()
                    nc.vector.tensor_tensor(a, a, rs[:, 0:S], ALU.add)
                    dve.drain()

            def moe_layer(l):
                q, nt = moe[l], TILES_OF[l]

                def bc(x, n):
                    return x.unsqueeze(2).to_broadcast([P, x.shape[1], n])

                def over_last(dst, src, op):
                    nc.vector.tensor_reduce(dst, src, AX.X, op)
                    dve.drain()

                def first_max(dst, cand, src, best, desc, n):
                    nc.vector.tensor_tensor(cand, src, bc(best, n), ALU.is_equal)
                    dve.drain()
                    nc.vector.tensor_tensor(cand, cand, desc.unsqueeze(1).to_broadcast([P, nt, n]), ALU.mult)
                    dve.drain()
                    over_last(scal[:, 11, 0:nt], cand, ALU.max)
                    nc.vector.tensor_tensor(dst, cand, bc(scal[:, 11, 0:nt], n), ALU.is_equal)
                    dve.drain()

                sc = lambda x: scal[:, x, 0:nt]
                lgv, gev, gsv, elv, ecv = lg[:, 0:nt, :], ge[:, 0:nt, :], gsel[:, 0:nt, :], elog[:, 0:nt, :], ecand[:, 0:nt, :]
                dve.wait_ge(q["logits"], l + 1)
                rb = vec("route_b")[:, l * TT * ROUTE:l * TT * ROUTE + nt * ROUTE]
                nc.vector.tensor_tensor(lgv.rearrange("p t r -> p (t r)"), bank[4][:, 0:nt * ROUTE], rb, ALU.add)
                dve.drain()
                over_last(sc(0), lgv[:, :, 0:NG], ALU.max)
                nc.vector.tensor_tensor(gev, lgv[:, :, 0:NG], bc(sc(0), NG), ALU.subtract)
                dve.drain().then_inc(q["gexp_in"], 1)
                dve.wait_ge(q["gexp"], l + 1)
                over_last(sc(1), gev, ALU.add)
                over_last(sc(2), gev, ALU.max)
                nc.vector.reciprocal(sc(1), sc(1))
                dve.drain()
                nc.vector.tensor_tensor(sc(1), sc(1), sc(2), ALU.mult)
                first_max(gsv, gev, gev, sc(2), const("gdesc"), NG)
                elg = elv.rearrange("p t (g e) -> p t g e", g=NG)
                for g in range(NG):
                    nc.vector.tensor_tensor(elg[:, :, g, :], lgv[:, :, NG + 8 * g:NG + 8 * g + 8], bc(gsv[:, :, g], 8), ALU.mult)
                nc.vector.tensor_scalar(gev, gsv, -NEG, NEG, ALU.mult, ALU.add)
                dve.drain()
                for g in range(NG):
                    nc.vector.tensor_tensor(elg[:, :, g, :], elg[:, :, g, :], bc(gev[:, :, g], 8), ALU.add)
                dve.drain()
                over_last(sc(2), elv, ALU.max)
                first_max(oh[0][:, 0:nt, :], ecv, elv, sc(2), const("edesc"), NE)
                nc.vector.scalar_tensor_tensor(elv, oh[0][:, 0:nt, :], 2 * NEG, elv, ALU.mult, ALU.add)
                dve.drain()
                over_last(sc(3), elv, ALU.max)
                first_max(oh[1][:, 0:nt, :], ecv, elv, sc(3), const("edesc"), NE)
                nc.vector.tensor_tensor(both[:, 0:nt, :], oh[0][:, 0:nt, :], oh[1][:, 0:nt, :], ALU.add)
                dve.drain().then_inc(q["onehot"], 1)
                nc.vector.tensor_tensor(sc(4), sc(3), sc(2), ALU.subtract)
                dve.drain().then_inc(q["eexp_in"], 1)
                dve.wait_ge(q["eexp"], l + 1)
                nc.vector.tensor_scalar(sc(6), sc(5), 1.0, None, ALU.add)
                dve.drain()
                nc.vector.reciprocal(sc(6), sc(6))
                dve.drain()
                nc.vector.tensor_tensor(sc(7), sc(6), sc(1), ALU.mult)
                dve.drain()
                nc.vector.tensor_tensor(sc(8), sc(7), sc(5), ALU.mult)
                dve.wait_ge(q["counts"], l + 1)
                nc.vector.tensor_scalar(col[0:NE, 0:1], bank[4][0:NE, 0:1], 1.0, None, ALU.mult)
                dve.drain()
                nthr = -(-2 * SC // 2 // MB)
                nc.vector.tensor_scalar(cmpb[0:NE, 0:nthr], const("thr")[0:NE, 0:nthr], col[0:NE, 0:1], None, ALU.is_lt)
                dve.drain()
                nc.vector.tensor_reduce(col[0:NE, 1:2], cmpb[0:NE, 0:nthr], AX.X, ALU.add)
                dve.drain()
                nc.vector.tensor_scalar(nbb[0:NE, :], ones[0:NE, :], col[0:NE, 1:2], None, ALU.mult)
                dve.drain().then_inc(q["nblk"], 1)
                dve.wait_ge(q["starts"], l + 1)
                nc.vector.tensor_copy(col[0:NE, 2:3], bank[6][0:NE, 0:1])
                dve.drain()
                nc.vector.tensor_scalar(cmpb[0:NE, 0:TABW], const("count")[0:NE, 0:TABW], col[0:NE, 2:3], None, ALU.is_ge)
                dve.drain().then_inc(q["cmp"], 1)
                dve.wait_ge(q["exp_row"], l + 1)
                nc.vector.tensor_scalar(exp_i[0:1, 0:TABW], bank[6][0:1, 64:64 + TABW], float(NE - 1), None, ALU.min)
                nc.vector.tensor_scalar(exp_i[0:1, TABW:TABW + 1], bank[7][0:1, TABW:TABW + 1], -1.0, None, ALU.add)
                dve.drain().then_inc(q["expert"], 1)
                dve.wait_ge(q["ranks"], l + 1)
                rkv = rank[:, 0:nt, :]
                nc.vector.tensor_copy(rkv.rearrange("p t e -> p (t e)"), bank[3][:, 0:nt * NE])
                dve.drain()
                ovi = over[:, 0:nt, :].bitcast(I32)
                nc.vector.tensor_copy(ovi, rkv)
                dve.drain()
                nc.vector.tensor_scalar(ovi, ovi, MB.bit_length() - 1, None, ALU.logical_shift_right)
                dve.drain()
                ovv = lg[:, 0:nt, 0:NE]
                nc.vector.tensor_copy(ovv, ovi)
                dve.drain()
                nc.vector.tensor_copy(nbb[:, 0:NE], bank[5][:, 0:NE])
                dve.drain()
                start = nbb[:, 0:NE].unsqueeze(1).to_broadcast([P, nt, NE])
                nc.vector.tensor_tensor(ecv, ovv, start, ALU.add)
                nc.vector.scalar_tensor_tensor(elv, start, float(MB), rkv, ALU.mult, ALU.add)
                dve.drain()
                for which, src in ((0, elv), (1, ecv)):
                    for x in range(2):
                        nc.vector.tensor_tensor(lg[:, 0:nt, 0:NE], oh[x][:, 0:nt, :], src, ALU.mult)
                        dve.drain()
                        over_last(pos_f[:, which, x, 0:nt], lg[:, 0:nt, 0:NE], ALU.add)
                dve.drain()
                blk, row = pos_f[:, 1, :, 0:nt], pos_f[:, 0, :, 0:nt]
                nc.vector.tensor_copy(pos_u[:, :, 0:nt], row)
                nc.vector.scalar_tensor_tensor(place[:, :, 0:nt], blk, -float(MB), row, ALU.mult, ALU.add)
                dve.drain()
                for t in range(nt):
                    for x in range(2):
                        nc.vector.tensor_scalar(at_place[:, 2 * t + x, :], const("count")[:, 0:MB], place[:, x, t:t + 1], None, ALU.is_equal)
                        nc.vector.tensor_scalar(in_block[:, 2 * t + x, :], const("count")[:, 0:TABW], pos_f[:, 1, x, t:t + 1],
                                                const("tok")[:, t:t + 1], ALU.is_equal, ALU.mult)
                dve.drain().then_inc(q["tab_in"], 1)
                dve.wait_ge(q["tab_full"], l + 1)
                nc.vector.tensor_copy(tab_u[:, :], bank[2][0:MB, 0:TABW])
                dve.drain().then_inc(q["table"], 1)

                def copy_x(b):
                    dve.wait_ge(q["xt_full"], b + 1)
                    nc.vector.tensor_copy(xT, bank[2][:, :]).then_inc(q["xt_ready"], 1)

                def mul(b, first=False):
                    dve.wait_ge(q["up_full"], b + 1)
                    dve.wait_ge(q["sg_ready"], b + 1)
                    if not first:
                        dve.wait_ge(q["htp_full"], b)
                    nc.vector.tensor_tensor(hmul[MB:2 * MB, :], hsil[MB:2 * MB, :], bank[0][MB:2 * MB, :], ALU.mult).then_inc(q["h_ready"], 1)

                def copy_h(b):
                    dve.wait_ge(q["htp_full"], b + 1)
                    nc.vector.tensor_copy(hT, bank[6][:, 0:EF // P * MB]).then_inc(q["ht_ready"], 1)

                phase.end()
                last = dve.value_load(exp_i[0:1, TABW:TABW + 1], min_val=2, max_val=NBMAX - 1)
                copy_x(0)
                mul(0, first=True)
                copy_x(1)
                copy_h(0)
                mul(1)
                copy_x(2)
                copy_h(1)
                with dve.Fori(2, last + 1) as b:
                    mul(b)
                    copy_x(b + 1)
                    copy_h(b)
                phase.end()
                for t in range(nt + 1):
                    if t < nt:
                        dve.wait_ge(q[f"got{t % 2}"], 32 * (t // 2 + 1))
                        first, second = yrows[t]
                        nc.vector.tensor_scalar(first, first, scal[:, 7, t:t + 1], None, ALU.mult)
                        dve.drain()
                        nc.vector.scalar_tensor_tensor(first, second, scal[:, 8, t:t + 1], first, ALU.mult, ALU.add).then_inc(q["sum_ready"], 1)
                    if t > 0:
                        n = t - 1
                        dve.wait_ge(q["sum_tr"], n + 1)
                        st, dst = (0, lat[:, :, n * P:(n + 1) * P]) if n < LT else (1, cxt[:, :, (n - LT) * P:(n - LT + 1) * P])
                        for k in range(KT):
                            x = nc.vector.scalar_tensor_tensor(dst[:, k, :], bank[2 * (n % 2) + k // 4][:, (k % 4) * P:(k % 4 + 1) * P],
                                                               mod[:, l, 5, k, st:st + 1], dst[:, k, :], ALU.mult, ALU.add)
                        x.then_inc(q["sum_read"], 1)
                phase.end()

            for s, n in ([(x, 1) for x in free] + [(mod_full, 1), (mod_free, 1), (mod_turned, 1), (act_ready, 2), (s_full, UNITS), (s_evac, 2),
                          (y_norm, 2), (turn_full, 2), (t_evac, 2), (o_evac, 2), (rope_free, 1)]):
                dve.drain().then_inc(s, n)
            dve.wait_ge(loaded, 48)
            nc.vector.tensor_scalar(half_g[:, 0, :], vec("ffn1_post_g"), 0.5, None, ALU.mult)
            nc.vector.tensor_scalar(half_g[:, 1, :], vec("ffn2_post_g"), 0.5, None, ALU.mult)
            ffn(1, "ffn1_pre_g", half_g[:, 0, :])

            pre_norm(vec("mix_pre_g"), u1)
            lm = vec("lru_lambda")
            nc.vector.tensor_scalar(lam8[:, 2, :], lm, -1.0, 0.0, ALU.mult, ALU.max)
            nc.vector.tensor_scalar(lam8[:, 3, :], lm, -1.0, None, ALU.mult)
            dve.drain()
            nc.vector.tensor_tensor(lam8[:, 3, :], lam8[:, 3, :], lm, ALU.min)
            dve.drain().then_inc(cond_ready, 1)
            dve.wait_ge(cond_ready, 3)
            nc.vector.tensor_scalar(lam8[:, 5, :], lam8[:, 4, :], 2.0, None, ALU.add)
            dve.drain()
            nc.vector.reciprocal(lam8[:, 5, :], lam8[:, 5, :])
            dve.drain()
            nc.vector.tensor_tensor(lam8[:, 4, :], lam8[:, 4, :], lam8[:, 5, :], ALU.mult)
            dve.drain()
            nc.vector.tensor_tensor(lam8[:, 5, :], lam8[:, 4, :], lam8[:, 4, :], ALU.mult)
            nc.vector.memset(lam8[:, 6, :], 1.0 / 17)
            dve.drain()
            for odd in range(15, 0, -2):
                nc.vector.tensor_tensor(lam8[:, 6, :], lam8[:, 6, :], lam8[:, 5, :], ALU.mult)
                dve.drain()
                nc.vector.tensor_scalar(lam8[:, 6, :], lam8[:, 6, :], 1.0 / odd, None, ALU.add)
                dve.drain()
            nc.vector.tensor_tensor(lam8[:, 6, :], lam8[:, 6, :], lam8[:, 4, :], ALU.mult)
            dve.drain()
            nc.vector.scalar_tensor_tensor(lam8[:, 6, :], lam8[:, 6, :], 2.0, lam8[:, 2, :], ALU.mult, ALU.add)
            dve.drain()
            nc.vector.tensor_scalar(lam8[:, 0, :], lam8[:, 6, :], LRU_C, None, ALU.mult)
            nc.vector.tensor_scalar(lam8[:, 1, :], lam8[:, 6, :], -LRU_C, None, ALU.mult)
            nc.vector.memset(xbr[:, :, 0:CONV1 - 1], 0.0)
            dve.drain()
            dve.wait_ge(xbr_ready, 1)
            cw, cb = vec("conv_w"), vec("conv_b")
            for t in range(KT):
                nc.vector.tensor_scalar(xc[:, t, :], xbr[:, t, 0:S], cw[:, t:t + 1], cb[:, t:t + 1], ALU.mult, ALU.add)
                for k in range(1, CONV1):
                    dve.drain()
                    x = nc.vector.scalar_tensor_tensor(xc[:, t, :], xbr[:, t, k:k + S], cw[:, KT * k + t:KT * k + t + 1], xc[:, t, :],
                                                       ALU.mult, ALU.add)
                x.then_inc(xc_ready, 1)
            held = KT - 1
            for t in range(KT):
                dve.wait_ge(decay_ready, t + 1)
                nc.vector.tensor_scalar(tmp[:, 0, :], gr[:, t, :], 1.0, None, ALU.add)
                nc.vector.tensor_tensor(gi[:, t, :], gi[:, t, :], xc[:, t, :], ALU.mult)
                dve.drain()
                nc.vector.reciprocal(tmp[:, 0, :], tmp[:, 0, :])
                dve.drain()
                nc.vector.scalar_tensor_tensor(gr[:, t, :], gr[:, t, :], 2.0, tmp[:, 0, :], ALU.mult, ALU.mult).then_inc(msq_ready, 1)
                dve.drain()
                if t < held:
                    rope([qk1[:, t, :]], const("cos1"), const("sin1"), t)
            for t in range(KT):
                dve.wait_ge(mult_ready, t + 1)
                nc.vector.tensor_tensor(gi[:, t, :], gi[:, t, :], gr[:, t, :], ALU.mult)
                dve.drain()
                nc.vector.tensor_tensor_scan(xc[:, t, :], xbr[:, t, 0:S], gi[:, t, :], 0.0, ALU.mult, ALU.add)
            rope([qk1[:, x, :] for x in range(held, KT + 2)], const("cos1"), const("sin1"), held)
            dve.wait_ge(gate_ready, 1)
            for t in range(KT):
                nc.vector.tensor_tensor(xc[:, t, :], xc[:, t, :], f[:, t, :], ALU.mult)
            phase.end()
            attend(False, 0, *att_views(o, 2 * P), vec("sinks1"), const("mask1"))
            phase.end()
            for src, hi, lo in ((xc, lru_high, lru_low), (f, att_high, att_low)):
                for k in range(KT):
                    nc.vector.tensor_copy(hi[:, k, :], src[:, k, :])
                    dve.drain()
                    nc.vector.tensor_tensor(lo[:, k, :], src[:, k, :], hi[:, k, :].bitcast(F32), ALU.subtract).then_inc(mx_ready, 1)
            r0 = plan["merge"][0]
            with dve.Fori(0, 8) as i:
                for n in range(2):
                    dve.wait_ge(full[2 * n + 1], r0 + 1 + i)
                    dve.wait_ge(free[2 * n], r0 + 1 + i)
                    nc.vector.tensor_tensor(tmp[:, 2 + n, :], tmp[:, n, :], bank[2 * n + 1][:, :], ALU.mult).then_inc(free[2 * n + 1], 1)
                dve.drain()
                nc.vector.tensor_tensor(merged[:, bass.ds(i, 1), :].rearrange("p a t -> p (a t)"), tmp[:, 2, :], tmp[:, 3, :],
                                        ALU.add)
                dve.drain().then_inc(mrg_ready, 1)
            rsqrt(S)
            phase.end()
            post_norm(vec("mix_post_g"))
            ffn(2, "ffn2_pre_g", half_g[:, 1, :])
            for l in range(2):
                for w, g in ((0, "norm_mix"), (1, "norm_ffn")):
                    for st in range(2):
                        nc.vector.scalar_tensor_tensor(amod[:, l, w, st, :], mod[:, l, 3 * w + 1, :, st], 1.0,
                                                       vec(g)[:, l * KT:(l + 1) * KT], ALU.add, ALU.mult)
            dve.drain()

            mod_norm(0, 0, True, shift=2)
            phase.end()
            w2 = vec("conv_w2")
            for t in range(4):
                bt, ct, ht, yc = pt[:, 4 + t, :], pt[:, 8 + t, :], pt[:, 12 + t, :], yt[:, 4 + t, :]
                nc.vector.tensor_tensor(ct, ct, ht, ALU.mult)
                dve.drain()
                nc.vector.tensor_scalar(yc, ct, w2[:, 4 + t:5 + t], None, ALU.mult)
                dve.drain()
                for a, n in ((0, S), (S, C)):
                    nc.vector.scalar_tensor_tensor(yc[:, a + 1:a + n], ct[:, a:a + n - 1], w2[:, t:t + 1], yc[:, a + 1:a + n], ALU.mult, ALU.add)
                dve.drain()
                for a, n in ((0, S), (S, C)):
                    nc.vector.scalar_tensor_tensor(yc[:, a:a + n - 1], ct[:, a + 1:a + n], w2[:, 8 + t:9 + t], yc[:, a:a + n - 1], ALU.mult, ALU.add)
                dve.drain()
                nc.vector.tensor_tensor(yc, yc, bt, ALU.mult)
            phase.end()

            def gated_add(name, l, its, context):
                r0 = plan[name][0]
                g1 = mod[:, l, 2, :, :].rearrange("p k c -> p (k c)")
                with dve.Fori(0, its) as i:
                    for j in range(4):
                        dve.wait_ge(full[j], r0 + 1 + i)
                        if context:
                            k, st = 2 * i + j // 2, j % 2
                        else:
                            k, st = 4 * i + j, 0
                        x, n = (lat, S) if st == 0 else (cxt, C)
                        xv = x[:, bass.ds(k, 1), :].rearrange("p a t -> p (a t)")
                        nc.vector.tensor_copy(small[:, 64 + j:65 + j], g1[:, bass.ds(2 * k + st, 1)])
                        dve.drain()
                        nc.vector.scalar_tensor_tensor(xv, bank[j][:, 0:n], small[:, 64 + j:65 + j], xv, ALU.mult,
                                                       ALU.add).then_inc(free[j], 1)

            for k in range(1, KT, 2):
                dve.wait_ge(mh_ready, 3 * KT + k + 1)
                nc.vector.tensor_tensor(y_low[:, k, :], yt[:, k, :], y_high[:, k, :].bitcast(F32), ALU.subtract).then_inc(mx_ready, 1)
            gated_add("even_out", 0, 4, True)
            phase.end()
            mod_norm(0, 1, True)
            moe_layer(0)

            mod_norm(1, 0, True, shift=1)
            for x in range(len(HEAD_TILES) + ROPE_LAG):
                if x < len(HEAD_TILES):
                    a, n = HEAD_TILES[x], HEAD_TILES[x].shape[1]
                    dve.wait_ge(qstd_ready, x + 1)
                    nc.vector.reciprocal(tmp[:, 2 + x % 2, 0:n], tmp[:, 2 + x % 2, 0:n])
                    dve.drain()
                    nc.vector.scalar_tensor_tensor(a, a, vec("q_g") if x < KT else vec("k_g"), tmp[:, 2 + x % 2, 0:n], ALU.mult,
                                                   ALU.mult).then_inc(qn_ready, 1)
                    dve.drain()
                if x - ROPE_LAG in ROTATED:
                    rope([HEAD_TILES[x - ROPE_LAG]], const("cos2"), const("sin2"), 10 + ROTATED.index(x - ROPE_LAG))
            phase.end()
            attend(True, 32, *att_views(att2, 5 * P), vec("sinks2"), const("mask2"))
            phase.end()
            gated_add("wo", 1, 2, False)
            phase.end()
            mod_norm(1, 1, False)
            moe_layer(1)

        @block.gpsimd
        def _(pool):
            phase = Phase(pool)

            def attend(u0, qt, qs):
                with pool.Fori(0, ROUNDS) as i:
                    for m in range(UNITS):
                        n, kv = m % LT, m // LT
                        pool.wait_ge(s_full, u0 + m + 1 + 8 * i)
                        nc.gpsimd.tensor_copy(qs[:, kv, n * P:(n + 1) * P],
                                              qt[:, bass.ds(4 * kv + i, 1), n * P:(n + 1) * P].rearrange("p a t -> p (a t)")
                                              ).then_inc(q_staged, 1)

            def moe_layer(l):
                q, nt = moe[l], TILES_OF[l]
                pool.wait_ge(q["table"], l + 1)
                pool.wait_ge(q["xt_out"], 16 * nt)

                def gather(b, first=False):
                    if not first:
                        pool.wait_ge(q["xt_full"], b)
                    nc.gpsimd.tensor_copy(idx_u[:, :], tab_u[:, bass.ds(b, 1)])
                    pool.drain()
                    pool.indirect_dma_start(out=xg[0:MB, :], out_offset=None, in_=d["rows"][l],
                                            in_offset=bass.IndirectOffsetOnAxis(ap=idx_u[:, :], axis=0)).then_inc(q["gathered"], 16)

                gather(0, first=True)
                phase.end()
                last = pool.value_load(exp_i[0:1, TABW:TABW + 1], min_val=2, max_val=NBMAX - 1)
                gather(1)
                gather(2)
                with pool.Fori(2, last + 1) as b:
                    gather(b + 1)
                phase.end()
                for t in range(nt):
                    if t > 1:
                        pool.wait_ge(q[f"got{t % 2}"], 32 * (t // 2))
                    for x in range(2):
                        pool.indirect_dma_start(out=yrows[t][x], out_offset=None, in_=d["yb"][l],
                                                in_offset=bass.IndirectOffsetOnAxis(ap=pos_u[:, x, t:t + 1], axis=0)
                                                ).then_inc(q[f"got{t % 2}"], 16)
                phase.end()

            def low(s, at, ring, count, rings=ffn_ring):
                pool.wait_ge(wh_ready, count)
                nc.gpsimd.tensor_tensor(w_low[s][:, at], slot[s][:, at], rings[ring][:, 0:at.stop - at.start].bitcast(F32),
                                        ALU.subtract).then_inc(wl_ready, 1)

            def paired_lows(name, its, src, lo, hi, count, step=1):
                w0 = PIECES_BEFORE[name]
                halves = [slice(h * PIECE, (h + 1) * PIECE) for h in range(2)]
                for h in range(2):
                    low(0, halves[h], h, w0 + h + 1, even_ring)
                for k in range(0, KT, step):
                    pool.wait_ge(mh_ready, count + k + 1)
                    nc.gpsimd.tensor_tensor(lo[:, k, :], src[:, k, :], hi[:, k, :].bitcast(F32), ALU.subtract).then_inc(mu_ready, 1)
                with pool.Fori(0, its - 1) as i:
                    for s in range(2):
                        for h in range(2):
                            low(1 - s, halves[h], h, w0 + 2 * s + h + 3 + i * 4, even_ring)
                for h in range(2):
                    low(1, halves[h], h, w0 + 4 * its - 1 + h, even_ring)
                phase.end()

            def ffn(n):
                w0 = PIECES_BEFORE[n]

                halves = [slice(h * PIECE, (h + 1) * PIECE) for h in range(2)]
                for h in range(2):
                    low(0, halves[h], h, w0 + h + 1)
                for k in range(KT):
                    pool.wait_ge(uh_ready, KT * (n - 1) + k + 1)
                    nc.gpsimd.tensor_tensor(u_low[:, k, :], tmp[:, k % 2, :], u_high[:, k, :].bitcast(F32), ALU.subtract).then_inc(u_ready, 1)
                with pool.Fori(0, GU_ROUNDS) as i:
                    for j in range(4):
                        low(1 if j < 2 else 0, halves[j % 2], j % 2, w0 + j + 3 + i * 4)
                        if j > 1:
                            pool.wait_ge(ah_ready, FT * (n - 1) + j - 1 + i * 2)
                            a = bass.ds(2 * i + j - 2, 1)
                            nc.gpsimd.tensor_tensor(act_low[:, a, :].rearrange("p a t -> p (a t)"), tmp[:, j - 2, :],
                                                    act_high[:, a, :].rearrange("p a t -> p (a t)").bitcast(F32), ALU.subtract).then_inc(act_ready, 1)
                w0 += 4 * GU_ROUNDS
                for T in range(KT):
                    for p in range(DOWN_PIECES):
                        if T > 0 or p > 1:
                            at, ring = down_piece(T, p)
                            low(T % 2, at, ring, w0 + DOWN_PIECES * T + p + 1)
                phase.end()

            nc.gpsimd.memset(zeros[:, :], 0.0)
            nc.gpsimd.memset(silu_c[:, :, :], 0.0)
            pool.drain().then_inc(zeros_ready, 1)
            ffn(1)
            w0 = PIECES_BEFORE["mixer"]
            halves = [slice(h * PIECE, (h + 1) * PIECE) for h in range(2)]
            for h in range(2):
                low(0, halves[h], h, w0 + h + 1)
            for k in range(KT):
                pool.wait_ge(mh_ready, k + 1)
                nc.gpsimd.tensor_tensor(p1_low[k], u1[:, k, :], p1_high[:, k, :].bitcast(F32), ALU.subtract).then_inc(mu_ready, 1)
            with pool.Fori(0, 3) as i:
                for j in range(4):
                    low(1 if j < 2 else 0, halves[j % 2], j % 2, w0 + j + 3 + i * 4)
            for h in range(2):
                low(1, halves[h], h, w0 + 2 * KT - 1 + h)
            phase.end()
            attend(0, qt1, att_views(o, 2 * P)[0])
            phase.end()
            w0 = PIECES_BEFORE["merge"]
            halves = [slice(h * PIECE, (h + 1) * PIECE) for h in range(2)]
            for h in range(2):
                low(0, halves[h], h, w0 + h + 1)
            for k in range(KT):
                pool.wait_ge(mh_ready, KT + k + 1)
                nc.gpsimd.tensor_tensor(u1_low[:, k, :], u1[:, k, :], u1_high[:, k, :].bitcast(F32), ALU.subtract).then_inc(mu_ready, 1)
            with pool.Fori(0, KT - 1) as i:
                for j in range(4):
                    low(1 if j < 2 else 0, halves[j % 2], j % 2, w0 + j + 3 + i * 4)
            for h in range(2):
                low(1, halves[h], h, w0 + MERGE_PIECES - 1 + h)
            phase.end()
            ffn(2)
            paired_lows("even_in", 4, u2, u2_low, u2_high, 2 * KT)
            phase.end()
            paired_lows("even_out", 2, yt, y_low, y_high, 3 * KT, step=2)
            moe_layer(0)
            w0 = PIECES_BEFORE["qkv"]
            for h in range(2):
                low(0, halves[h], h, w0 + h + 1, even_ring)
            for k in range(KT):
                pool.wait_ge(mh_ready, 4 * KT + k + 1)
                nc.gpsimd.tensor_tensor(h_low[:, k, :], u2[:, k, :], h_high[:, k, :].bitcast(F32), ALU.subtract).then_inc(mu_ready, 1)
            with pool.Fori(0, 2) as i:
                for j in range(4):
                    low(1 if j < 2 else 0, halves[j % 2], j % 2, w0 + j + 3 + i * 4, even_ring)
            for h in range(2):
                low(1, halves[h], h, w0 + KT + 3 + h, even_ring)
            phase.end()
            attend(32, qt2, att_views(att2, 5 * P)[0])
            phase.end()
            phase.end()
            moe_layer(1)


def tiles(w):
    n = w.shape[1] // P
    t = w.reshape(KT, P, n, P).transpose(2, 1, 0, 3).reshape(n // 2, 2, P, KT * P)
    return t.transpose(0, 2, 1, 3).reshape(n // 2, P, CHUNK)


def mixed(*ws):
    n = ws[0].shape[1] // P
    return tiles(np.stack([w.reshape(D, n, P) for w in ws], 2).reshape(D, -1))


def moving(w):
    return w.reshape(KT, P, C).transpose(1, 0, 2).reshape(1, P, CHUNK)


def groups(w):
    return w.reshape(2, 2, 4, P, 6 * D // MODC, MODC).transpose(0, 4, 1, 3, 2, 5).reshape(-1, P, CHUNK)


def columns(v):
    return np.ascontiguousarray(v).reshape(-1, P).T


def fields(named, spec):
    return np.ascontiguousarray(np.concatenate([named[n].reshape(P, w) for n, w in spec], 1))


def rope_table(pos, freqs):
    ang = pos.astype(np.float32)[:, None] * freqs.astype(np.float32)[None, :]
    return np.cos(ang), np.sin(ang)


def constants():
    p = np.arange(P)
    out = {"ident": np.eye(P), "ones": np.ones((P, P)), "headsum": p[:, None] // HD == p[None, :] // HD,
           "swap1": p[:, None] == (p ^ (HD // 2))[None, :], "swap2": p[:, None] == (p ^ (HD // 4))[None, :],
           "before": p[:, None] < p[None, :]}
    i, s1, s2 = p[:, None], np.arange(2 * P)[None, :], np.arange(3 * P)[None, :]
    out["mask1"] = np.where((P + i - s1 >= 0) & (P + i - s1 < P), 0.0, NEG)
    out["mask2"] = np.where(np.abs(s2 - P - i) <= P, 0.0, NEG)
    half = HD // 2
    c, s = rope_table(np.arange(S), np.float32(10000.0) ** (-np.arange(half, dtype=np.float32) / half))
    out["cos1"], out["sin1"] = c.T[p % half], s.T[p % half] * np.where(p % HD < half, -1.0, 1.0)[:, None]
    n = HD // 4
    freqs = np.float32(10000.0) ** (-np.arange(n, dtype=np.float32) / n)
    t = np.arange(S)
    by_axis = [rope_table(pos, freqs) for pos in (t // 64, t % 64)]
    axis = (p % HD) // half
    out["cos2"] = np.stack([by_axis[a][0][:, x % n] for a, x in zip(axis, p)])
    out["sin2"] = np.stack([by_axis[a][1][:, x % n] * (-1.0 if x % half < n else 1.0) for a, x in zip(axis, p)])
    out["quads"] = p[:, None] % QUAD == np.arange(2)
    out["eps"] = np.full((P, 1), EPS)
    out["gdesc"] = np.tile(np.arange(NG, 0, -1), (P, 1))
    out["edesc"] = np.tile(np.arange(NE, 0, -1), (P, 1))
    e = np.arange(NE)
    out["tri_lt"], out["tri_le"] = np.tile(e[:, None] < e, (P // NE, 1)), np.tile(e[:, None] <= e, (P // NE, 1))
    out["count"] = np.tile(np.arange(max(TABW, MB)), (P, 1))
    out["tok"] = p[:, None] + P * np.arange(TT)
    out["thr"] = np.tile(MB * np.arange(16), (P, 1))
    return fields({k: np.asarray(v, np.float32) for k, v in out.items()}, CONSTS)


def fourier():
    def pair(n):
        ang = 2 * np.pi * ((np.arange(n)[:, None] * np.arange(n)[None, :]) % n) / n
        return np.cos(ang) / np.sqrt(n), np.sin(ang) / np.sqrt(n)

    def rows(m):
        return m.reshape(-1, P, m.shape[1]).transpose(1, 0, 2).reshape(P, -1)

    (cd, sd), (cc, sc), (cl, sl) = pair(P), pair(C), pair(S)
    out = {"cs_d": np.concatenate([cd, sd], 1), "c_ctx": rows(cc), "s_ctx": rows(-sc), "c_lat": rows(cl), "s_lat": rows(-sl)}
    return fields({k: v.astype(np.float32) for k, v in out.items()}, DFT)


def kernel(**inputs):
    import concourse.bacc as bacc
    from concourse.bass_utils import run_bass_kernel_spmd

    x = {k: np.asarray(v) for k, v in inputs.items()}
    order = np.concatenate([np.arange(h * HD, (h + 1) * HD) for h in HEADS])
    w_in, w_in2, qkv = x["w_in"][0], x["w_in_even_2"][0], x["w_qkv_2"][0]
    a = 2 * D + D
    kvw = NH // 4 * HD
    gate, xb, wq = w_in[:, 0:D], w_in[:, D:2 * D], w_in[:, 2 * D:a][:, order]
    wk, wv, g_lru, g_att = w_in[:, a:a + kvw], w_in[:, a + kvw:a + 2 * kvw], w_in[:, a + 2 * kvw:a + 2 * kvw + D], w_in[:, a + 2 * kvw + D:]

    def ffn(n):
        gu = x[f"ffn{n}_w_gu"][0]
        g, u = (t.reshape(D, FF // 256, 256) for t in (gu[:, :FF], gu[:, FF:]))
        return tiles(np.stack([g, u], 2).reshape(D, 2 * FF))

    def down(n):
        return x[f"ffn{n}_w_down"][0].reshape(FT, P, KT, P).transpose(2, 1, 0, 3).reshape(KT, P, SLOT)

    w = np.concatenate([ffn(1), tiles(xb), tiles(wq), tiles(wk), moving(wv), tiles(gate),
                        mixed(g_lru, x["w_proj_lru"][0], g_att, x["w_proj_attn"][0][order]), tiles(x["w_out"][0]), ffn(2),
                        tiles(w_in2), tiles(x["w_out_even_2"][0]), tiles(qkv[:, 0:D][:, order]), tiles(qkv[:, D:D + kvw]),
                        moving(qkv[:, D + kvw:]), tiles(x["w_o_2"][0][order])])
    lru_w = np.zeros((2, KT, 2, HD, 2, HD), np.float32)
    for g, n in enumerate(("lru_w_a", "lru_w_x")):
        for h in range(2):
            lru_w[g, :, h, :, h, :] = x[n][0].reshape(KT, 2, HD, HD)[:, h]
    route_w = np.concatenate([x["w_router_g_2"], x["w_router_e_2"]], 2)
    route_b = np.concatenate([x["b_router_g_2"], x["b_router_e_2"]], 1)
    named = {n: columns(x[n][0]) for n in ("ffn1_pre_g", "ffn1_post_g", "mix_pre_g", "mix_post_g", "ffn2_pre_g", "ffn2_post_g",
                                           "conv_w", "conv_b", "lru_b_a", "lru_b_x", "lru_lambda")}
    named |= {"norm_mix": columns(x["norm_mix_g_2"]), "norm_ffn": columns(x["norm_ffn_g_2"]), "conv_w2": columns(x["conv_w_2"][0]),
              "q_g": np.tile(x["q_norm_g_2"][0], 2)[:, None], "k_g": np.tile(x["k_norm_g_2"][0], 2)[:, None],
              "cond": np.stack([columns(x["c_2"][0]), columns(x["c_ctx_2"])], 2),
              "b_mod": np.repeat(columns(x["b_mod_2"])[:, :, None], 2, 2),
              "sinks1": np.tile(x["attn_sinks"][0][HEADS], (P, 1)), "sinks2": np.tile(x["sink_logit_2"][0][HEADS], (P, 1)),
              "route_b": np.tile(route_b[None, :, None, :], (P, 1, TT, 1))}
    arrays = {"consts": constants(), "dft": fourier(), "vecs": fields(named, VECS),
              "x": x["x"][0].T.reshape(KT, P, S).transpose(1, 0, 2), "ctx": x["ctx_2"][0].T.reshape(KT, P, C).transpose(1, 0, 2),
              "w": w, "wm": groups(x["w_mod_2"]), "wd": np.concatenate([down(1), down(2)]),
              "lru_w": lru_w.reshape(2, KT, P, P).transpose(2, 0, 1, 3),
              "wr": route_w.reshape(2, KT, P, ROUTE).transpose(0, 2, 1, 3), "w1": x["w1_2"], "w3": x["w3_2"], "w2": x["w2_2"]}
    arrays = {f"in_{n}": np.ascontiguousarray(v) for n, v in arrays.items()}
    nc = bacc.Bacc("TRN2", target_bir_lowering=False, num_devices=1)
    d = {n[3:]: nc.dram_tensor(n, v.shape, F32, kind="ExternalInput").ap() for n, v in arrays.items()}
    d["out"] = nc.dram_tensor("out", (P, KT, S), F32, kind="ExternalOutput").ap()
    d["rows"] = [nc.dram_tensor(f"rows{l}", (t, D), F32, kind="Internal").ap() for l, t in enumerate((SC, S))]
    d["yb"] = [nc.dram_tensor(f"yb{l}", (NBMAX * MB, D), F32, kind="Internal").ap() for l in range(2)]
    program(nc, d)
    r = run_bass_kernel_spmd(nc, [arrays], core_ids=[0])
    out = np.asarray(r.results[0]["out"])
    return np.ascontiguousarray(out.transpose(2, 1, 0).reshape(1, S, D))
```
